# Optimizing a Trainium2 kernel written in Bass

```python
import jax, jax.numpy as jnp
from jax import lax
import numpy as np

D_MODEL = 1024
BATCH = 1
SEQ = 512
DEPTH = 2

HEAD_DIM = 64
DSW_GROUPS = ((128, 1), (512, 4), (2048, 16))
DSW_HEADS_PER_GROUP = 4
DSW_HEADS = DSW_HEADS_PER_GROUP * len(DSW_GROUPS)
SB_HEADS = D_MODEL // (4 * HEAD_DIM)
W_A = DSW_HEADS * HEAD_DIM
W_B = SB_HEADS * HEAD_DIM
OUT_A = DSW_HEADS_PER_GROUP * HEAD_DIM
OUT_B = W_B
N_IN = 3 * W_A + 3 * W_B + 2 * D_MODEL
BLOCK = 128
D_FF = 2816
CONV_WIDTH = 3
RMS_EPS = 1e-6


def rmsnorm(x, g):
    xf = x.astype(jnp.float32)
    y = xf * lax.rsqrt(jnp.mean(xf * xf, axis=-1, keepdims=True) + RMS_EPS)
    return (y * g.astype(jnp.float32)).astype(x.dtype)

def alibi_slopes(n):
    return jnp.asarray(2.0 ** (-8.0 * np.arange(1, n + 1) / n), dtype=jnp.float32)

def dilated_window_attention(q, k, v, slopes, window, dilation):
    B, S, H, hd = q.shape
    W = window // dilation
    L = S // dilation
    nb = -(-L // W)
    Lp = nb * W

    def to_sub(a):
        a = a.reshape(B, L, dilation, H, hd).transpose(0, 2, 3, 1, 4)
        return jnp.pad(a, ((0, 0), (0, 0), (0, 0), (0, Lp - L), (0, 0)))

    def windows(a):
        ap = jnp.pad(to_sub(a), ((0, 0), (0, 0), (0, 0), (W, 0), (0, 0))).reshape(B, dilation, H, nb + 1, W, hd)
        return jnp.concatenate([ap[:, :, :, :-1], ap[:, :, :, 1:]], axis=-2)

    qs = to_sub(q).reshape(B, dilation, H, nb, W, hd)
    kw = windows(k)
    vw = windows(v).astype(jnp.float32)
    scores = jnp.einsum('brhnqc,brhnkc->brhnqk', qs, kw).astype(jnp.float32) * (hd ** -0.5)
    qi = jnp.arange(W)[:, None]
    kj = jnp.arange(2 * W)[None, :]
    delta = qi + W - kj
    key_sub = (jnp.arange(nb) * W - W)[:, None, None] + kj[None]
    valid = (delta >= 0) & (delta <= W) & (key_sub >= 0)
    bias = -slopes[:, None, None, None] * (delta * dilation).astype(jnp.float32)
    scores = jnp.where(valid, scores + bias, -jnp.inf)
    mx = jnp.max(scores, axis=-1, keepdims=True)
    p = jnp.exp(scores - mx)
    den = jnp.sum(p, axis=-1, keepdims=True)
    o = jnp.einsum('brhnqk,brhnkc->brhnqc', p, vw) / den
    lse = (mx + jnp.log(den))[..., 0]
    o = o.reshape(B, dilation, H, Lp, hd)[:, :, :, :L].transpose(0, 3, 1, 2, 4).reshape(B, S, H, hd)
    lse = lse.reshape(B, dilation, H, Lp)[:, :, :, :L].transpose(0, 3, 1, 2).reshape(B, S, H)
    return o, lse

def dilated_mixture(q, k, v):
    B, S = q.shape[:2]
    slopes = alibi_slopes(DSW_HEADS)
    outs, lses = [], []
    for g, (window, dilation) in enumerate(DSW_GROUPS):
        hs = slice(g * DSW_HEADS_PER_GROUP, (g + 1) * DSW_HEADS_PER_GROUP)
        o, lse = dilated_window_attention(q[:, :, hs], k[:, :, hs], v[:, :, hs], slopes[hs], window, dilation)
        outs.append(o)
        lses.append(lse)
    alpha = jax.nn.softmax(jnp.stack(lses, axis=0), axis=0)
    o = jnp.sum(alpha[..., None] * jnp.stack(outs, axis=0), axis=0)
    return o.reshape(B, S, OUT_A).astype(q.dtype)

def stick_breaking_attention(q, k, v):
    B, S, H, hd = q.shape
    nq = S // BLOCK
    scale = hd ** -0.5
    qb = q.reshape(B, nq, BLOCK, H, hd).transpose(1, 0, 3, 2, 4)
    kt = k.transpose(0, 2, 1, 3)
    vt = v.transpose(0, 2, 1, 3).astype(jnp.float32)
    key_pos = jnp.arange(S)

    def block(args):
        q_blk, i = args
        z = jnp.einsum('bhqc,bhkc->bhqk', q_blk, kt).astype(jnp.float32) * scale
        qpos = i * BLOCK + jnp.arange(BLOCK)
        causal = key_pos[None, :] < qpos[:, None]
        log_stay = jnp.where(causal, jax.nn.log_sigmoid(-z), 0.0)
        later = lax.cumsum(log_stay, axis=3, reverse=True) - log_stay
        attn = jnp.where(causal, jnp.exp(jax.nn.log_sigmoid(z) + later), 0.0)
        return jnp.einsum('bhqk,bhkc->bhqc', attn, vt)

    o = lax.map(block, (qb, jnp.arange(nq)))
    return o.transpose(1, 0, 3, 2, 4).reshape(B, S, H * hd).astype(q.dtype)

def causal_depthwise_conv(a, w, b):
    S = a.shape[1]
    ap = jnp.pad(a, ((0, 0), (CONV_WIDTH - 1, 0), (0, 0)))
    y = b
    for i in range(CONV_WIDTH):
        y = y + ap[:, i:i + S] * w[i]
    return y

def first_inputs(seed: int = 0) -> dict:
    key = jax.random.key(seed)
    ks = jax.random.split(key, 12)
    f32 = jnp.float32
    x = jax.random.normal(ks[0], (BATCH, SEQ, D_MODEL), f32)
    norm1 = 1.0 + 0.05 * jax.random.normal(ks[1], (DEPTH, D_MODEL), f32)
    w_in = jax.random.normal(ks[2], (DEPTH, D_MODEL, N_IN), f32) * D_MODEL ** -0.5
    b_gate = 0.01 * jax.random.normal(ks[3], (DEPTH, 2 * D_MODEL), f32)
    w_br = jax.random.normal(ks[4], (DEPTH, OUT_A + OUT_B, D_MODEL), f32) * OUT_A ** -0.5
    w_o = jax.random.normal(ks[5], (DEPTH, D_MODEL, D_MODEL), f32) * D_MODEL ** -0.5
    norm2 = 1.0 + 0.05 * jax.random.normal(ks[6], (DEPTH, D_MODEL), f32)
    w_up = jax.random.normal(ks[7], (DEPTH, D_MODEL, 2 * D_FF), f32) * D_MODEL ** -0.5
    conv_w = jax.random.normal(ks[8], (DEPTH, CONV_WIDTH, D_FF), f32) * CONV_WIDTH ** -0.5
    conv_b = 0.01 * jax.random.normal(ks[9], (DEPTH, D_FF), f32)
    w_down = jax.random.normal(ks[10], (DEPTH, D_FF, D_MODEL), f32) * D_FF ** -0.5
    norm_f = 1.0 + 0.05 * jax.random.normal(ks[11], (D_MODEL,), f32)
    return {"x": x, "norm1": norm1, "w_in": w_in, "b_gate": b_gate, "w_br": w_br, "w_o": w_o,
            "norm2": norm2, "w_up": w_up, "conv_w": conv_w, "conv_b": conv_b, "w_down": w_down,
            "norm_f": norm_f}

def first_block(x, norm1, w_in, b_gate, w_br, w_o, norm2, w_up, conv_w, conv_b, w_down, norm_f):
    B, S, _ = x.shape
    splits = [W_A, 2 * W_A, 3 * W_A, 3 * W_A + W_B, 3 * W_A + 2 * W_B, 3 * W_A + 3 * W_B]
    for l in range(DEPTH):
        h = rmsnorm(x, norm1[l])
        proj = h @ w_in[l]
        qa, ka, va, qb, kb, vb, gate_pre = jnp.split(proj, splits, axis=-1)
        hd4 = lambda t, n: t.reshape(B, S, n, HEAD_DIM)
        o_a = dilated_mixture(hd4(qa, DSW_HEADS), hd4(ka, DSW_HEADS), hd4(va, DSW_HEADS))
        o_b = stick_breaking_attention(hd4(qb, SB_HEADS), hd4(kb, SB_HEADS), hd4(vb, SB_HEADS))
        gates = jax.nn.sigmoid(gate_pre + b_gate[l])
        g_a, g_b = gates[..., :D_MODEL], gates[..., D_MODEL:]
        merged = g_a * (o_a @ w_br[l, :OUT_A]) + g_b * (o_b @ w_br[l, OUT_A:])
        x = x + merged @ w_o[l]
        h2 = rmsnorm(x, norm2[l])
        up = h2 @ w_up[l]
        a, v = up[..., :D_FF], up[..., D_FF:]
        a = causal_depthwise_conv(a, conv_w[l], conv_b[l])
        x = x + (jax.nn.gelu(a, approximate=False) * v) @ w_down[l]
    return rmsnorm(x, norm_f)


N_MEM = 256
EPS = 1e-6
SC_WIDTH = D_MODEL // 2
SC_GROUPS = 8
CONV_K = 3
POOL_WIDTH = D_MODEL // 2
POOL_WINDOWS = (2, 4, 8, 16)
POOL_GROUP = POOL_WIDTH // len(POOL_WINDOWS)
EVEN_IN = 3 * SC_WIDTH + POOL_WIDTH
EVEN_MIX = SC_WIDTH + POOL_WIDTH
ML_HEADS = 4
ML_HEAD_DIM = 128
ML_WIDTH = ML_HEADS * ML_HEAD_DIM
ML_CHUNK = 64
MLA_HEADS = 8
QK_NOPE = 64
QK_ROPE = 32
V_DIM = 64
Q_LORA = 384
KV_LORA = 256
MLA_WIDTH = MLA_HEADS * V_DIM
Q_BLOCK = 128
ROPE_THETA = 10000.0
ODD_SIZES = (ML_WIDTH, ML_WIDTH, ML_WIDTH, ML_WIDTH, 2 * ML_HEADS, Q_LORA, KV_LORA, QK_ROPE)
ODD_SPLIT = tuple(int(v) for v in np.cumsum(ODD_SIZES)[:-1])
ODD_IN = sum(ODD_SIZES)
ODD_MIX = ML_WIDTH + MLA_WIDTH
XA_HEADS = 4
XA_HEAD_DIM = 128
XA_WIDTH = XA_HEADS * XA_HEAD_DIM
FFN_HIDDEN = ((8 * D_MODEL + 3 * 256 - 1) // (3 * 256)) * 256
N_EVEN = (DEPTH + 1) // 2
N_ODD = DEPTH // 2


def rmsnorm_2(x, g):
    xf = x.astype(jnp.float32)
    y = xf * lax.rsqrt(jnp.mean(xf * xf, axis=-1, keepdims=True) + EPS)
    return (y * g.astype(jnp.float32)).astype(x.dtype)

def causal_dwconv(u, w):
    c = u.shape[-1]
    return lax.conv_general_dilated(u, w[:, None, :].astype(u.dtype), window_strides=(1,),
                                    padding=[(CONV_K - 1, 0)],
                                    dimension_numbers=('NWC', 'WIO', 'NWC'),
                                    feature_group_count=c)

def causal_pool_mixer(u, pool_w, pool_scale):
    B, S, _ = u.shape
    ug = u.reshape(B, S, len(POOL_WINDOWS), POOL_GROUP)
    csum = jnp.cumsum(ug.astype(jnp.float32), axis=1)
    t1 = jnp.arange(1, S + 1)
    means = []
    for gi, w in enumerate(POOL_WINDOWS):
        cg = csum[:, :, gi]
        shifted = jnp.pad(cg, ((0, 0), (w, 0), (0, 0)))[:, :S]
        cnt = jnp.minimum(t1, w).astype(jnp.float32)
        means.append((cg - shifted) / cnt[None, :, None])
    pooled = jnp.stack(means, axis=2).astype(u.dtype)
    y = jnp.einsum('bsgc,gcd->bsgd', pooled - ug, pool_w)
    return y.reshape(B, S, POOL_WIDTH) * pool_scale

def even_mixer(h, w_in, conv_w, pool_w, pool_scale, w_out):
    z = h @ w_in
    g_b, g_c, xa, xb = jnp.split(z, [SC_WIDTH, 2 * SC_WIDTH, 3 * SC_WIDTH], axis=-1)
    ya = g_b * causal_dwconv(g_c * xa, conv_w)
    yb = causal_pool_mixer(xb, pool_w, pool_scale)
    return jnp.concatenate([ya, yb], axis=-1) @ w_out

def mlstm_chunkwise(q, k, v, i_pre, f_pre):
    B, S, H, D = q.shape
    L = ML_CHUNK
    NC = S // L

    def chunk(t):
        return t.reshape(B, NC, L, H, D).transpose(0, 3, 1, 2, 4)

    def chunk_g(t):
        return t.reshape(B, NC, L, H).transpose(0, 3, 1, 2)

    qc, kc, vc = chunk(q), chunk(k) * (D ** -0.5), chunk(v)
    ig = chunk_g(i_pre)
    bcum = jnp.cumsum(chunk_g(jax.nn.log_sigmoid(f_pre)), axis=-1)
    gtot = bcum[..., -1]

    a = gtot[..., None] - bcum + ig
    m_loc = jnp.max(a, axis=-1)
    w_loc = jnp.exp(a - m_loc[..., None])
    C_loc = jnp.einsum('bhcl,bhclv,bhclk->bhcvk', w_loc, vc, kc)
    n_loc = jnp.einsum('bhcl,bhclk->bhck', w_loc, kc)

    def step(carry, xs):
        C, n, m = carry
        g_c, m_l, C_l, n_l = xs
        m_new = jnp.maximum(g_c + m, m_l)
        s_old = jnp.exp(g_c + m - m_new)
        s_new = jnp.exp(m_l - m_new)
        C_new = s_old[..., None, None] * C + s_new[..., None, None] * C_l
        n_new = s_old[..., None] * n + s_new[..., None] * n_l
        return (C_new, n_new, m_new), (C, n, m)

    init = (jnp.zeros((B, H, D, D), jnp.float32), jnp.zeros((B, H, D), jnp.float32),
            jnp.zeros((B, H), jnp.float32))
    xs = (jnp.moveaxis(gtot, 2, 0), jnp.moveaxis(m_loc, 2, 0),
          jnp.moveaxis(C_loc, 2, 0), jnp.moveaxis(n_loc, 2, 0))
    _, (C_prev, n_prev, m_prev) = lax.scan(step, init, xs)
    C_prev = jnp.moveaxis(C_prev, 0, 2)
    n_prev = jnp.moveaxis(n_prev, 0, 2)
    m_prev = jnp.moveaxis(m_prev, 0, 2)

    causal = jnp.tril(jnp.ones((L, L), dtype=bool))
    dmat = jnp.where(causal, bcum[..., :, None] - bcum[..., None, :] + ig[..., None, :], -jnp.inf)
    inter = bcum + m_prev[..., None]
    m_t = jnp.maximum(inter, jnp.max(dmat, axis=-1))
    w_intra = jnp.exp(dmat - m_t[..., None])
    w_inter = jnp.exp(inter - m_t)
    sw = w_intra * jnp.einsum('bhcld,bhcsd->bhcls', qc, kc)
    num = (w_inter[..., None] * jnp.einsum('bhcvk,bhclk->bhclv', C_prev, qc)
           + jnp.einsum('bhcls,bhcsv->bhclv', sw, vc))
    den_raw = w_inter * jnp.einsum('bhck,bhclk->bhcl', n_prev, qc) + jnp.sum(sw, axis=-1)
    den = jnp.maximum(jnp.abs(den_raw), jnp.exp(-m_t))
    hc = num / den[..., None]
    return hc.transpose(0, 2, 3, 1, 4).reshape(B, S, H, D)

def rope_tables(positions):
    half = QK_ROPE // 2
    inv_freq = ROPE_THETA ** (-jnp.arange(half, dtype=jnp.float32) / half)
    ang = positions.astype(jnp.float32)[..., None] * inv_freq
    return jnp.cos(ang)[:, :, None, :], jnp.sin(ang)[:, :, None, :]

def apply_rope(t, cos, sin):
    half = t.shape[-1] // 2
    tf = t.astype(jnp.float32)
    t1, t2 = tf[..., :half], tf[..., half:]
    return jnp.concatenate([t1 * cos - t2 * sin, t1 * sin + t2 * cos], axis=-1).astype(t.dtype)

def mla_attention(q_nope, q_rope, k_nope, k_rope, v):
    B, S, H, _ = q_nope.shape
    nb = S // Q_BLOCK
    scale = (QK_NOPE + QK_ROPE) ** -0.5
    k_idx = jnp.arange(S)

    def to_blocks(t):
        return jnp.moveaxis(t.reshape(B, nb, Q_BLOCK, H, t.shape[-1]), 1, 0)

    def attend_block(args):
        blk, qn, qr = args
        s = (jnp.einsum('bqhd,bkhd->bhqk', qn, k_nope)
             + jnp.einsum('bqhr,bkr->bhqk', qr, k_rope)).astype(jnp.float32) * scale
        q_idx = blk * Q_BLOCK + jnp.arange(Q_BLOCK)
        s = jnp.where(k_idx[None, :] <= q_idx[:, None], s, -jnp.inf)
        p = jax.nn.softmax(s, axis=-1).astype(v.dtype)
        return jnp.einsum('bhqk,bkhd->bqhd', p, v)

    out = lax.map(attend_block, (jnp.arange(nb), to_blocks(q_nope), to_blocks(q_rope)))
    return jnp.moveaxis(out, 0, 1).reshape(B, S, H * V_DIM)

def odd_mixer(h, positions, w_in, gate_bias, ml_norm_g, q_norm_g, kv_norm_g, w_uq, w_ukv, w_out):
    B, S, _ = h.shape
    z = h @ w_in
    q_m, k_m, v_m, o_m, gates, c_q, c_kv, k_r = jnp.split(z, ODD_SPLIT, axis=-1)
    gates = (gates + gate_bias).astype(jnp.float32)
    i_pre, f_pre = gates[..., :ML_HEADS], gates[..., ML_HEADS:]
    hs = (B, S, ML_HEADS, ML_HEAD_DIM)
    hm = mlstm_chunkwise(q_m.reshape(hs).astype(jnp.float32), k_m.reshape(hs).astype(jnp.float32),
                         v_m.reshape(hs).astype(jnp.float32), i_pre, f_pre).astype(h.dtype)
    hm = jax.nn.sigmoid(o_m).reshape(hs) * hm
    hm = rmsnorm_2(hm, ml_norm_g.reshape(ML_HEADS, ML_HEAD_DIM)).reshape(B, S, ML_WIDTH)

    q = (rmsnorm_2(c_q, q_norm_g) @ w_uq).reshape(B, S, MLA_HEADS, QK_NOPE + QK_ROPE)
    kv = (rmsnorm_2(c_kv, kv_norm_g) @ w_ukv).reshape(B, S, MLA_HEADS, QK_NOPE + V_DIM)
    cos, sin = rope_tables(positions)
    q_nope, q_rope = q[..., :QK_NOPE], apply_rope(q[..., QK_NOPE:], cos, sin)
    k_nope, v = kv[..., :QK_NOPE], kv[..., QK_NOPE:]
    k_rope = apply_rope(k_r[:, :, None, :], cos, sin)[:, :, 0]
    ha = mla_attention(q_nope, q_rope, k_nope, k_rope, v)
    return jnp.concatenate([hm, ha], axis=-1) @ w_out

def memory_cross_attention(h, mem_n, wq, wkv, wo):
    B, S, _ = h.shape
    q = (h @ wq).reshape(B, S, XA_HEADS, XA_HEAD_DIM)
    k, v = jnp.split(mem_n @ wkv, 2, axis=-1)
    k = k.reshape(B, N_MEM, XA_HEADS, XA_HEAD_DIM)
    v = v.reshape(B, N_MEM, XA_HEADS, XA_HEAD_DIM)
    s = jnp.einsum('bshd,bmhd->bhsm', q, k).astype(jnp.float32) * (XA_HEAD_DIM ** -0.5)
    p = jax.nn.softmax(s, axis=-1).astype(v.dtype)
    return jnp.einsum('bhsm,bmhd->bshd', p, v).reshape(B, S, XA_WIDTH) @ wo

def swiglu(h, w_gate_up, w_down):
    g, u = jnp.split(h @ w_gate_up, 2, axis=-1)
    return (jax.nn.silu(g) * u) @ w_down

def second_inputs(seed: int = 0) -> dict:
    key = jax.random.key(seed)
    ks = iter(jax.random.split(key, 40))
    f32 = jnp.float32

    def dense(shape, fan_in):
        return jax.random.normal(next(ks), shape, f32) * (fan_in ** -0.5)

    def gain(shape):
        return 1.0 + 0.05 * jax.random.normal(next(ks), shape, f32)

    x = jax.random.normal(next(ks), (BATCH, SEQ, D_MODEL), f32)
    mem = jax.random.normal(next(ks), (BATCH, N_MEM, D_MODEL), f32)
    offsets = jax.random.randint(next(ks), (BATCH, 1), 0, 1024, dtype=jnp.int32)
    positions = offsets + jnp.arange(SEQ, dtype=jnp.int32)[None, :]

    f_bias = jnp.linspace(3.0, 6.0, ML_HEADS, dtype=f32)[None, :] + 0.1 * jax.random.normal(next(ks), (N_ODD, ML_HEADS), f32)
    i_bias = 0.1 * jax.random.normal(next(ks), (N_ODD, ML_HEADS), f32)

    return {
        'x': x,
        'mem': mem,
        'positions': positions,
        'norm_mix_g': gain((DEPTH, D_MODEL)),
        'norm_xattn_g': gain((DEPTH, D_MODEL)),
        'mem_norm_g': gain((DEPTH, D_MODEL)),
        'xattn_wq': dense((DEPTH, D_MODEL, XA_WIDTH), D_MODEL),
        'xattn_wkv': dense((DEPTH, D_MODEL, 2 * XA_WIDTH), D_MODEL),
        'xattn_wo': dense((DEPTH, XA_WIDTH, D_MODEL), XA_WIDTH),
        'norm_ffn_g': gain((DEPTH, D_MODEL)),
        'ffn_w_gate_up': dense((DEPTH, D_MODEL, 2 * FFN_HIDDEN), D_MODEL),
        'ffn_w_down': dense((DEPTH, FFN_HIDDEN, D_MODEL), FFN_HIDDEN),
        'ev_w_in': dense((N_EVEN, D_MODEL, EVEN_IN), D_MODEL),
        'ev_conv_w': dense((N_EVEN, CONV_K, SC_WIDTH), CONV_K),
        'ev_pool_w': dense((N_EVEN, len(POOL_WINDOWS), POOL_GROUP, POOL_GROUP), POOL_GROUP),
        'ev_pool_scale': 1.0 + 0.1 * jax.random.normal(next(ks), (N_EVEN, POOL_WIDTH), f32),
        'ev_w_out': dense((N_EVEN, EVEN_MIX, D_MODEL), EVEN_MIX),
        'od_w_in': dense((N_ODD, D_MODEL, ODD_IN), D_MODEL),
        'od_gate_bias': jnp.concatenate([i_bias, f_bias], axis=-1),
        'od_ml_norm_g': gain((N_ODD, ML_WIDTH)),
        'od_q_norm_g': gain((N_ODD, Q_LORA)),
        'od_kv_norm_g': gain((N_ODD, KV_LORA)),
        'od_w_uq': dense((N_ODD, Q_LORA, MLA_HEADS * (QK_NOPE + QK_ROPE)), Q_LORA),
        'od_w_ukv': dense((N_ODD, KV_LORA, MLA_HEADS * (QK_NOPE + V_DIM)), KV_LORA),
        'od_w_out': dense((N_ODD, ODD_MIX, D_MODEL), ODD_MIX),
        'final_norm_g': gain((D_MODEL,)),
    }

def second_block(x, mem, positions, norm_mix_g, norm_xattn_g, mem_norm_g, xattn_wq, xattn_wkv, xattn_wo,
              norm_ffn_g, ffn_w_gate_up, ffn_w_down, ev_w_in, ev_conv_w, ev_pool_w, ev_pool_scale,
              ev_w_out, od_w_in, od_gate_bias, od_ml_norm_g, od_q_norm_g, od_kv_norm_g, od_w_uq,
              od_w_ukv, od_w_out, final_norm_g):
    for layer in range(DEPTH):
        h = rmsnorm_2(x, norm_mix_g[layer])
        if layer % 2 == 0:
            e = layer // 2
            mix = even_mixer(h, ev_w_in[e], ev_conv_w[e], ev_pool_w[e], ev_pool_scale[e], ev_w_out[e])
        else:
            o = layer // 2
            mix = odd_mixer(h, positions, od_w_in[o], od_gate_bias[o], od_ml_norm_g[o], od_q_norm_g[o],
                            od_kv_norm_g[o], od_w_uq[o], od_w_ukv[o], od_w_out[o])
        x = x + mix
        mem_n = rmsnorm_2(mem, mem_norm_g[layer])
        x = x + memory_cross_attention(rmsnorm_2(x, norm_xattn_g[layer]), mem_n,
                                       xattn_wq[layer], xattn_wkv[layer], xattn_wo[layer])
        x = x + swiglu(rmsnorm_2(x, norm_ffn_g[layer]), ffn_w_gate_up[layer], ffn_w_down[layer])
    return rmsnorm_2(x, final_norm_g)


def setup_inputs(seed=0):
    out = dict(first_inputs(seed))
    for name, value in second_inputs(seed + 1).items():
        if name != "x":
            out[name + "_2"] = value
    return out


def reference(
    x, norm1, w_in, b_gate, w_br, w_o, norm2, w_up, conv_w, conv_b, w_down, norm_f, mem_2,
    positions_2, norm_mix_g_2, norm_xattn_g_2, mem_norm_g_2, xattn_wq_2, xattn_wkv_2,
    xattn_wo_2, norm_ffn_g_2, ffn_w_gate_up_2, ffn_w_down_2, ev_w_in_2, ev_conv_w_2,
    ev_pool_w_2, ev_pool_scale_2, ev_w_out_2, od_w_in_2, od_gate_bias_2, od_ml_norm_g_2,
    od_q_norm_g_2, od_kv_norm_g_2, od_w_uq_2, od_w_ukv_2, od_w_out_2, final_norm_g_2,
):
    x = first_block(
        x, norm1, w_in, b_gate, w_br, w_o, norm2, w_up, conv_w, conv_b, w_down, norm_f,
    )
    return second_block(
        x, mem_2, positions_2, norm_mix_g_2, norm_xattn_g_2, mem_norm_g_2, xattn_wq_2,
        xattn_wkv_2, xattn_wo_2, norm_ffn_g_2, ffn_w_gate_up_2, ffn_w_down_2, ev_w_in_2,
        ev_conv_w_2, ev_pool_w_2, ev_pool_scale_2, ev_w_out_2, od_w_in_2, od_gate_bias_2,
        od_ml_norm_g_2, od_q_norm_g_2, od_kv_norm_g_2, od_w_uq_2, od_w_ukv_2, od_w_out_2,
        final_norm_g_2,
    )


_drawn_inputs = setup_inputs


def setup_inputs(seed=0):
    import zlib

    import numpy as np

    out = dict(_drawn_inputs(seed))
    spreads = {}
    factors = {'b_gate': 8.0,
     'conv_b': 4.266,
     'norm_xattn_g_2': 8.0,
     'mem_norm_g_2': 5.883,
     'od_q_norm_g_2': 8.0,
     'od_kv_norm_g_2': 8.0,
     'od_ml_norm_g_2': 3.228}
    for name, (base, spread) in spreads.items():
        noise = np.random.default_rng([zlib.crc32(name.encode()), seed]).standard_normal(out[name].shape)
        drawn = base * np.exp(spread * noise) if base else spread * noise
        out[name] = __import__('jax').numpy.asarray(drawn.astype(out[name].dtype))
    for name, factor in factors.items():
        out[name] = (out[name] * factor).astype(out[name].dtype)
    return out
```

```python
from contextlib import ExitStack

import numpy as np
import concourse.bass as bass
from concourse import mybir

F32 = mybir.dt.float32
F32R = mybir.dt.float32r
I32 = mybir.dt.int32
ALU = mybir.AluOpType
ACT = mybir.ActivationFunctionType
AX_X = mybir.AxisListType.X

P = 128
S = 512
D = 1024
KT = D // P
TT = S // P
DEPTH = 2
HD = 64
SLOTS = 4
GROUPS = 3
DIL = (1, 4, 16)
W_A = SLOTS * GROUPS * HD
W_B = SLOTS * HD
D_FF = 2816
FT = D_FF // P
HALVES = ((0, 12), (12, 10))
EPS = 1e-6
MASKED = -1e30
HALF = D

VEC_GROUPS = (
    (("norm1", DEPTH * 8), ("norm2", DEPTH * 8), ("norm_f", 8), ("norm_mix_g_2", DEPTH * 8),
     ("norm_xattn_g_2", DEPTH * 8), ("mem_norm_g_2", DEPTH * 8), ("norm_ffn_g_2", DEPTH * 8),
     ("final_norm_g_2", 8)),
    (("b_gate", DEPTH * 16), ("conv_b", DEPTH * FT), ("ev_conv_w_2", 12), ("ev_pool_scale_2", 4),
     ("od_ml_norm_g_2", 4), ("od_q_norm_g_2", 3), ("od_kv_norm_g_2", 2)),
    (("conv_w0", 3 * FT),),
    (("conv_w1", 3 * FT),),
)
N_MEM = 256
ML_HEADS = 4
MLA_HEADS = 8
NOPE, ROPE = 64, 32
QK_DIM = NOPE + ROPE
WINDOWS = (2, 4, 8, 16)
TWO_PI = 2 * np.pi
TURN_1 = 6.28125
TURN_2 = float(np.float32(TWO_PI - TURN_1))
TURN_3 = float(np.float32(TWO_PI - TURN_1 - TURN_2))
ROUND = 1.5 * 2 ** 23
INPUTS = 2 + sum(len(g) for g in VEC_GROUPS) + TT
BLOCK2 = True
NORMS = [(KT, True)] * (2 * DEPTH) + [(KT, False)]
for _l in range(DEPTH if BLOCK2 else 0):
    NORMS += [(KT, True)] + ([(3, True), (2, True)] if _l else []) + [(KT, True)] * 3
if BLOCK2:
    NORMS += [(KT, False)]
LAST_NORM = len(NORMS) - 1
MIX, MEMORY, XATTN, FFN = ([5, 9], [6, 12], [7, 13], [8, 14])
LATENT_Q, LATENT_KV = 10, 11
VEC = {}
VEC_ROWS = []
_at = 0
for _g in VEC_GROUPS:
    _row = 0
    for _name, _n in _g:
        VEC[_name] = _at + _row
        _row += _n
    VEC_ROWS.append((_at, _row))
    _at += _row
VEC_COLS = _at

C_IDENT, C_ONES, C_TRI, C_LATER, C_CAUSAL, C_CAUSAL_T, C_ROT, C_FREQ, C_INV, C_BIAS = (
    0, 128, 256, 384, 512, 640, 768, 800, 804, 820)
PLANES = 4
C_COLS = C_BIAS + SLOTS * PLANES * P


def shape_constants():
    c = np.zeros((P, C_COLS), np.float32)
    i, j = np.arange(P)[:, None], np.arange(P)[None, :]
    c[:, C_IDENT:C_IDENT + P] = i == j
    c[:, C_ONES:C_ONES + P] = 1.0
    c[:, C_TRI:C_TRI + P] = i > j
    c[:, C_LATER:C_LATER + P] = j > i
    c[:, C_CAUSAL:C_CAUSAL + P] = np.where(j <= i, 0.0, MASKED)
    c[:, C_CAUSAL_T:C_CAUSAL_T + P] = np.where(i <= j, 0.0, MASKED)
    for a in range(16):
        c[80 + a, C_ROT + a] = -1.0
        c[64 + a, C_ROT + 16 + a] = 1.0
        f = np.float32(10000.0) ** (-np.float32(a) / np.float32(16))
        c[64 + a, C_FREQ] = c[80 + a, C_FREQ] = f
    c[:, C_INV:C_INV + 16] = 1.0 / np.arange(1, 17)
    heads = SLOTS * GROUPS
    slopes = (2.0 ** (-8.0 * np.arange(1, heads + 1) / heads)).astype(np.float32)
    for h in range(SLOTS):
        own = (i - j).astype(np.float32)
        planes = (
            (slopes[h], own, j <= i),
            (slopes[h], own + P, j >= i),
            (slopes[SLOTS + h], own * DIL[1], j <= i),
            (slopes[2 * SLOTS + h], own * DIL[1], (i % 4 == j % 4) & (j <= i)),
        )
        for n, (slope, distance, valid) in enumerate(planes):
            at = C_BIAS + (h * PLANES + n) * P
            c[:, at:at + P] = np.where(valid, -slope * distance, np.float32(MASKED))
    return c


def chunk_starts():
    sizes = []
    for l in range(DEPTH):
        sizes += [(f"qk{l}", 8), (f"v{l}", 4), (f"gate{l}", 8), (f"br{l}", 2), (f"wo{l}", 4)]
        for half, (_, n) in enumerate(HALVES):
            sizes += [(f"up{l}{half}", n), (f"down{l}{half}", 8)]
    for l in range(DEPTH if BLOCK2 else 0):
        if l == 0:
            sizes += [("ev_in", 8), ("ev_out", 4)]
        else:
            sizes += [("od_in", 8), ("od_lat", 2), ("od_gk", 2), ("od_uq", 4), ("od_ukv", 4), ("od_uv", 2), ("od_out", 4)]
        sizes += [(f"xkv{l}", 4), (f"xq{l}", 2), (f"xo{l}", 4)]
        for half, (_, n) in enumerate(HALVES):
            sizes += [(f"up{2 + l}{half}", n), (f"down{2 + l}{half}", 8)]
    starts, at = {}, 0
    for name, n in sizes:
        starts[name] = (at, n)
        at += n
    return starts, at


def block_program(nc, dram, out):
    start, chunks = chunk_starts()
    size = [HALF] * chunks
    for name, n_each in () if not BLOCK2 else (("od_uq", 3 * P), ("od_ukv", 2 * P), ("od_uv", 2 * P), ("xo0", 4 * P), ("xo1", 4 * P)):
        for c in range(start[name][0], sum(start[name])):
            size[c] = n_each
    for l in range(2 * DEPTH if BLOCK2 else DEPTH):
        for half, (_, n) in enumerate(HALVES):
            c0, count = start[f"down{l}{half}"]
            size[c0:c0 + count] = [n // 2 * P] * count

    with ExitStack() as ctx:
        def sb(name, shape, dt=F32, scope=ctx):
            return scope.enter_context(nc.sbuf_tensor(name, shape, dt))

        def sem(name):
            return ctx.enter_context(nc.semaphore(name))

        M = [ctx.enter_context(nc.psum_tensor(f"M{i}", [P, S], F32)) for i in range(4)]
        A = [ctx.enter_context(nc.psum_tensor(f"A{i}", [P, S], F32)) for i in range(4)]

        const = sb("const", [P, C_COLS])
        eps = sb("eps", [P, 1])
        half_pi = sb("half_pi", [P, 1])
        gate_bias = sb("gate_bias", [P, 2])
        soft_max, neg_max, soft_den = sb("soft_max", [P, 8]), sb("neg_max", [P, 8]), sb("soft_den", [P, 8])
        neg_gate = sb("neg_gate", [P, DEPTH * 16])
        vec = sb("vec", [P, VEC_COLS])
        x = sb("x", [P, KT, S])
        h_hi = sb("h_hi", [P, KT, S], F32R)
        h_lo = sb("h_lo", [P, KT, S], F32R)
        stage = sb("stage", [P, 2, HALF])
        w_hi = sb("w_hi", [P, 2, 2 * HALF], F32R)
        w_lo = sb("w_lo", [P, 2, 2 * HALF], F32R)
        ident = const[:, C_IDENT:C_IDENT + P]
        ones = const[:, C_ONES:C_ONES + P]
        tri = const[:, C_TRI:C_TRI + P]
        later_mask = const[:, C_LATER:C_LATER + P]
        bias = const[:, C_BIAS:].rearrange("p (h n c) -> p h n c", h=SLOTS, n=PLANES)

        with ExitStack() as scope:
            x_tok = sb("x_tok", [P, TT, D], scope=scope)
            rows = sb("rows", [P, len(VEC_ROWS), P], scope=scope)
        with ExitStack() as scope:
            qk_a = sb("qk_a", [P, 12, S], scope=scope)
            qk_b = sb("qk_b", [P, 4, S], scope=scope)
            v_a = sb("v_a", [P, TT, GROUPS * SLOTS // 2, 3, HD], scope=scope)
            v_b = sb("v_b", [P, TT, W_B], scope=scope)
            gate = sb("gate", [P, 2 * KT, S], scope=scope)
            o_a = sb("o_a", [P, 2, S], scope=scope)
            prob = sb("prob", [P, PLANES, S], scope=scope)
            top = sb("top", [P, GROUPS, S], scope=scope)
            top_all = sb("top_all", [P, S], scope=scope)
            row_max = sb("row_max", [P, 16], scope=scope)
        with ExitStack() as scope:
            o_hi = sb("o_hi", [P, 4, S], F32R, scope=scope)
            o_lo = sb("o_lo", [P, 4, S], F32R, scope=scope)
        with ExitStack() as scope:
            hid_hi = sb("hid_hi", [P, 12, S], F32R, scope=scope)
            hid_lo = sb("hid_lo", [P, 12, S], F32R, scope=scope)
            conv = sb("conv", [P, 2, S], scope=scope)
            acted = sb("acted", [P, 2, S], scope=scope)
            hid = sb("hid", [P, 2, S], scope=scope)
            square = sb("square", [P, 2, S], scope=scope)
            normed = sb("normed", [P, 2, S], scope=scope)
            root = sb("root", [P, S], scope=scope)
            rstd = sb("rstd", [P, S], scope=scope)
        pads = []

        def lay(*items):
            made, at = [], 0
            with ExitStack() as scope:
                for kib, name, shape, dt in items:
                    if kib * 256 > at:
                        pads.append(sb(f"gap{len(pads)}", [P, kib * 256 - at], scope=scope))
                        at = kib * 256
                    made.append(sb(name, [P, *shape], dt, scope=scope))
                    at += int(np.prod(shape))
            return made

        g_b, g_c, gated, pooled, y_hi, y_lo, y, window, pool_w = lay(
            (0, "g_b", [4, S], F32), (8, "g_c", [4, S], F32), (16, "gated", [4, S], F32),
            (24, "pooled", [4, S], F32), (32, "y_hi", [KT, S], F32R), (48, "y_lo", [KT, S], F32R),
            (72, "y", [2, S], F32), (76, "window", [2, S], F32), (80, "pool_w", [4, P], F32))
        mem_tok, mem_t, mem_hi, mem_lo, k_x, v_x, q_x, x_prob, x_turned = lay(
            (0, "mem_tok", [N_MEM // P, D], F32), (8, "mem_t", [KT, N_MEM], F32),
            (16, "mem_hi", [KT, N_MEM], F32R), (24, "mem_lo", [KT, N_MEM], F32R),
            (32, "k_x", [4, N_MEM], F32), (36, "v_x", [N_MEM // P, S], F32), (40, "q_x", [4, S], F32),
            (72, "x_prob", [2, 4 * N_MEM], F32), (80, "x_turned", [2, 2 * S], F32))
        xo_hi, xo_lo = lay((0, "xo_hi", [4, S], F32R), (8, "xo_lo", [4, S], F32R))
        (cq_hi, cq_lo, ckv_hi, ckv_lo, k_rope, cos, sin, latent, g_i, g_f, g_sum, g_top, g_one, a_col,
         ml_w, ml_sw, ml_diag, ml_0, ml_1, ml_2, ml_3, q_m, k_m, v_ml, sig_o) = lay(
            (0, "cq_hi", [3, S], F32R), (6, "cq_lo", [3, S], F32R), (12, "ckv_hi", [2, S], F32R),
            (16, "ckv_lo", [2, S], F32R), (20, "k_rope", [S], F32), (22, "cos", [S], F32), (24, "sin", [S], F32),
            (26, "latent", [5, S], F32), (36, "g_i", [S], F32), (38, "g_f", [S], F32), (40, "g_sum", [S], F32),
            (42, "g_top", [S], F32), (44, "g_one", [S], F32), (46, "a_col", [16], F32),
            (47, "ml_w", [1280], F32), (52, "ml_sw", [1280], F32), (57, "ml_diag", [S], F32),
            (60, "ml_0", [S], F32), (62, "ml_1", [S], F32), (64, "ml_2", [S], F32), (66, "ml_3", [S], F32),
            (72, "q_m", [4, S], F32), (80, "k_m", [4, S], F32), (88, "v_ml", [TT, S], F32),
            (96, "sig_o", [4, S], F32))
        q_h, v_h, m_prob, m_turned, k_h, rotated = lay(
            (26, "q_h", [MLA_HEADS, S], F32), (42, "v_h", [TT, S], F32), (50, "m_prob", [2, 1280], F32),
            (60, "m_turned", [2, 1280], F32), (72, "k_h", [MLA_HEADS, S], F32), (88, "rotated", [MLA_HEADS, S], F32))
        pos, angle, turns, rest, rest_abs = lay(
            (47, "pos", [S], I32), (49, "angle", [S], F32), (51, "turns", [S], F32), (53, "rest", [S], F32),
            (55, "rest_abs", [S], F32))
        RR = slice(NOPE, QK_DIM)
        with ExitStack() as scope:
            x_out = sb("x_out", [P, TT, D], scope=scope)
        o_b = v_a[:, :, :, :, :].rearrange("p t a b c -> p (t a b c)")[:, 0:2 * S].rearrange("p (n c) -> p n c", n=2)
        merged = prob

        ST = [0, S, 2 * S - P, 3 * S - 3 * P]
        ST_N = [S - P * kb for kb in range(TT)]
        prob_flat = prob[:, :, :].rearrange("p n c -> p (n c)")
        log_one = prob_flat[:, 0:1280]
        log_sig = top[:, :, :].rearrange("p n c -> p (n c)")[:, 0:1280]
        log_stay = qk_a[:, 8:11, :].rearrange("p n c -> p (n c)")[:, 0:1280]

        landed = [sem("part0_landed"), sem("part1_landed")]
        w_hi_done, w_lo_done = sem("w_hi_done"), sem("w_lo_done")
        w_used = sem("w_used")
        m_free = sem("m_free")
        inputs_landed = sem("inputs_landed")
        turned, turned_out = sem("turned"), sem("turned_out")
        ones_set, consts_set = sem("ones_set"), sem("consts_set")
        square_done, square_used, root_done, rstd_done = (
            sem("square_done"), sem("square_used"), sem("root_done"), sem("rstd_done"))
        normed_done, h_hi_done, h_lo_done = sem("normed_done"), sem("h_hi_done"), sem("h_lo_done")
        scores_done, plane_biased, max_a, max_b, max_done, shifted = (
            sem("scores_done"), sem("plane_biased"), sem("max_a"), sem("max_b"), sem("max_done"), sem("shifted"))
        max_spread, max_copied, exp_done, turned_plane, plane_back, pv_done = (
            sem("max_spread"), sem("max_copied"), sem("exp_done"), sem("turned_plane"), sem("plane_back"), sem("pv_done"))
        top1, top2, top_shift, weight_done, mix_step, a_free, o_done = (
            sem("top1"), sem("top2"), sem("top_shift"), sem("weight_done"), sem("mix_step"), sem("a_free"), sem("o_done"))
        z_done, st_act, log_done, st_dve, stay_done, later_done, st_arg, st_exp, st_prob, st_pv = (
            sem("z_done"), sem("st_act"), sem("log_done"), sem("st_dve"), sem("stay_done"), sem("later_done"),
            sem("st_arg"), sem("st_exp"), sem("st_prob"), sem("st_pv"))
        gate_exp, gate_ln, gate_done = sem("gate_exp"), sem("gate_ln"), sem("gate_done")
        den_step, den_done = sem("den_step"), sem("den_done")
        o_hi_done, o_lo_done = sem("o_hi_done"), sem("o_lo_done")
        br_full, br_free, br_sum, merged_done, mg_hi_done, mg_lo_done = (
            sem("br_full"), sem("br_free"), sem("br_sum"), sem("merged_done"), sem("mg_hi_done"), sem("mg_lo_done"))
        tap_done, conv_step, conv_done, acted_done, hid_done, hid_hi_done, hid_lo_done = (
            sem("tap_done"), sem("conv_step"), sem("conv_done"), sem("acted_done"), sem("hid_done"),
            sem("hid_hi_done"), sem("hid_lo_done"))
        out_turned, out_ready, out_stored = sem("out_turned"), sem("out_ready"), sem("out_stored")
        pool_landed, mem_landed, pos_landed = sem("pool_landed"), sem("mem_landed"), sem("pos_landed")
        pool_in, pool_out, ev_y, ev_y_hi, ev_y_lo = (
            sem("pool_in"), sem("pool_out"), sem("ev_y"), sem("ev_y_hi"), sem("ev_y_lo"))
        mem_turned, mem_out = sem("mem_turned"), sem("mem_out")
        at_scores, at_reduced, at_max, at_exp, at_recip, at_norm, at_turned, at_back, at_pv, at_hi, at_out = (
            sem("at_scores"), sem("at_reduced"), sem("at_max"), sem("at_exp"), sem("at_recip"), sem("at_norm"),
            sem("at_turned"), sem("at_back"), sem("at_pv"), sem("at_hi"), sem("at_out"))
        og_exp, og_ln, og_done = sem("og_exp"), sem("og_ln"), sem("og_done")
        trig_arg, trig_done, rope_turned, rope_free, rope_k, rope_spread, rope_done = (
            sem("trig_arg"), sem("trig_done"), sem("rope_turned"), sem("rope_free"), sem("rope_k"),
            sem("rope_spread"), sem("rope_done"))
        f_in, f_step, f_log, rows_done, a_turned, a_out = (
            sem("f_in"), sem("f_step"), sem("f_log"), sem("rows_done"), sem("a_turned"), sem("a_out"))
        ml_scores, ml_diag_done, ml_w_done, ml_sw_done, ml_nd, ml_abs, ml_hm, ml_sq, ml_ss, ml_ln, ml_rs, ml_y, ml_hi, ml_out = (
            sem("ml_scores"), sem("ml_diag_done"), sem("ml_w_done"), sem("ml_sw_done"), sem("ml_nd"),
            sem("ml_abs"), sem("ml_hm"), sem("ml_sq"), sem("ml_ss"), sem("ml_ln"), sem("ml_rs"), sem("ml_y"),
            sem("ml_hi"), sem("ml_out"))
        chain = sem("chain")

        AT0 = {"x0": 0, "mla": 4, "x1": 12}

        def attention(kind):
            if kind == "mla":
                widths = [(i + 1) * P for i in range(TT)]
                return (MLA_HEADS, TT, widths, [0, P, 3 * P, 6 * P], ST, [kt * P for kt in range(TT)],
                        m_prob, m_turned, QK_DIM ** -0.5)
            return (4, N_MEM // P, [N_MEM] * TT, [i * N_MEM for i in range(TT)], [0, S], [0, 0],
                    x_prob, x_turned, P ** -0.5)

        def head_banks(h):
            return A if h % 2 == 0 else M

        def result(kind, h):
            if kind == "mla":
                lo = (h % 2) * HD
                return h_hi[lo:lo + HD, 4 + h // 2, :], h_lo[lo:lo + HD, 4 + h // 2, :], slice(lo, lo + HD)
            return xo_hi[:, h, :], xo_lo[:, h, :], slice(0, P)

        def col(name, n=0):
            return vec[:, VEC[name] + n:VEC[name] + n + 1]

        def col_at(name, n):
            return vec[:, bass.ds(n + VEC[name], 1)]

        def over(t, g):
            return t if g == 0 else t.rearrange("p (r l) -> p l r", r=DIL[1])

        def nat(t, g):
            return t if g == 0 else t.rearrange("p (l r) -> p l r", r=DIL[1])

        def by_residue(t, g):
            return t if g == 0 else t.rearrange("p (l r) -> p r l", r=DIL[1])

        def as_residue(t, g):
            return t if g == 0 else t.rearrange("p (r l) -> p r l", r=DIL[1])

        def split_norm(n):
            return sum(kt for kt, split in NORMS[:n] if split)

        def norm_tiles(n):
            return sum(kt for kt, _ in NORMS[:n])

        def up_counts(l, half):
            return l * FT + HALVES[half][0]

        block = ctx.enter_context(nc.Block())

        @block.sync
        def _(sp):
            def load(c, part0, part1, dst0, dst1):
                for n, (src, dst) in enumerate(((part0, dst0), (part1, dst1))):
                    if not (isinstance(c, int) and c == 0):
                        sp.wait_ge(w_lo_done, c * 2 - 1 + n)
                    sp.dma_start(dst, src).then_inc(landed[n], 16)

            def halves(k, n):
                return [stage[:, part, 0:k * n].rearrange("p (k n) -> p k n", n=n) for part in range(2)]

            def by_tile(w):
                return w.rearrange("(k p) (m c) -> m p k c", p=P, c=P)

            def load_tiles(c, w, m, k=KT):
                load(c, w[m], w[m + 1], *halves(k, P))

            def load_wide(c, w, m):
                v = w.rearrange("(k p) (m c) -> m p k c", p=P, c=2 * P)[m]
                load(c, v[:, 0:4, :], v[:, 4:8, :], *halves(4, 2 * P))

            def load_up(layer, w):
                t = by_tile(w)
                return t

            def feed_forward(l, w_up, w_down):
                up, down = by_tile(w_up), by_tile(w_down)
                for half, (f0, n) in enumerate(HALVES):
                    c0 = start[f"up{l}{half}"][0]
                    with sp.Fori(0, n // 2) as i:
                        for s in range(2):
                            load(i * 2 + (c0 + s), up[i * 2 + (f0 + s)], up[i * 2 + (f0 + s + FT)],
                                 *halves(KT, P))
                    c0 = start[f"down{l}{half}"][0]
                    k = n // 2
                    with sp.Fori(0, KT // 2) as i:
                        for s in range(2):
                            tile = down[i * 2 + s]
                            load(i * 2 + (c0 + s), tile[:, f0:f0 + k, :], tile[:, f0 + k:f0 + n, :],
                                 *halves(k, P))

            sources = dict(dram)
            for l in range(DEPTH):
                sources[f"conv_w{l}"] = dram["conv_w"][l]
            sp.dma_start(const[:, :], dram["shape_constants"]).then_inc(inputs_landed, 16)
            count = 1
            for g, group in enumerate(VEC_GROUPS):
                row = 0
                for name, n in group:
                    a = sources[name]
                    flat = {1: "(r c) -> r c", 2: "a (r c) -> (a r) c"}
                    src = a.rearrange("a b (r c) -> (a b r) c", c=P) if len(a.shape) == 3 else \
                        a.rearrange(flat[len(a.shape)], c=P)
                    sp.dma_start(rows[row:row + n, g, :], src).then_inc(inputs_landed, 16)
                    row += n
                    count += 1
            sp.dma_start(gate_bias[0:ML_HEADS, :], dram["od_gate_bias_2"][0].rearrange("(a p) -> p a", a=2),
                         allow_slow_non_contiguous=True).then_inc(inputs_landed, 16)
            for j in range(TT):
                sp.dma_start(x_tok[:, j, :], dram["x"][0, j * P:(j + 1) * P, :]).then_inc(inputs_landed, 16)

            for l in range(DEPTH):
                w = dram["w_in"][l]
                tiles = by_tile(w)
                c0 = start[f"qk{l}"][0]
                for n, m in enumerate((0, 2, 4, 6, 8, 10, 18, 20)):
                    load_tiles(c0 + n, tiles, m)
                c0 = start[f"v{l}"][0]
                for n, m in enumerate((6, 7, 8, 11)):
                    load_wide(c0 + n, w, m)
                c0 = start[f"gate{l}"][0]
                with sp.Fori(0, 4) as i:
                    for s in range(2):
                        load(i * 2 + (c0 + s), tiles[i * 4 + (24 + 2 * s)], tiles[i * 4 + (25 + 2 * s)],
                             *halves(KT, P))
                c0 = start[f"br{l}"][0]
                w = dram["w_br"][l].rearrange("(k p) (m c) -> m p k c", p=P, c=S)
                for n in range(2):
                    load(c0 + n, w[n][:, 0:2, :], w[n][:, 2:4, :], *halves(2, S))
                c0 = start[f"wo{l}"][0]
                tiles = by_tile(dram["w_o"][l])
                with sp.Fori(0, 2) as i:
                    for s in range(2):
                        load(i * 2 + (c0 + s), tiles[i * 4 + 2 * s], tiles[i * 4 + (2 * s + 1)],
                             *halves(KT, P))
                feed_forward(l, dram["w_up"][l], dram["w_down"][l])
            def cross_attention(l):
                w = dram["xattn_wkv_2"][l]
                c0 = start[f"xkv{l}"][0]
                for n in range(2):
                    load_tiles(c0 + n, by_tile(w), 2 * n)
                sp.wait_ge(w_used, c0 + 2)
                for t in range(N_MEM // P):
                    sp.dma_start(mem_tok[:, t, :], dram["mem_2"][0, t * P:(t + 1) * P, :]).then_inc(mem_landed, 16)
                for n in range(2):
                    load_wide(c0 + 2 + n, w, 2 + n)
                for n in range(2):
                    load_tiles(start[f"xq{l}"][0] + n, by_tile(dram["xattn_wq_2"][l]), 2 * n)
                for n in range(4):
                    load_tiles(start[f"xo{l}"][0] + n, by_tile(dram["xattn_wo_2"][l]), 2 * n, k=4)
                feed_forward(2 + l, dram["ffn_w_gate_up_2"][l], dram["ffn_w_down_2"][l])

            tiles = by_tile(dram["ev_w_in_2"][0])
            for n in range(8):
                load_tiles(start["ev_in"][0] + n, tiles, 2 * n)
                if n == 1:
                    sp.wait_ge(normed_done, norm_tiles(MIX[0]) + KT)
                    sp.dma_start(pool_w[:, :, :], dram["ev_pool_w_2"][0].rearrange("g c d -> c g d"))\
                      .then_inc(pool_landed, 16)
            for n in range(4):
                load_tiles(start["ev_out"][0] + n, by_tile(dram["ev_w_out_2"][0]), 2 * n)
            cross_attention(0)
            w = dram["od_w_in_2"][0]
            tiles = by_tile(w[:, 0:4 * S])
            c0 = start["od_in"][0]
            for n in range(4):
                load_tiles(c0 + n, tiles, 2 * n)
                if n == 1:
                    sp.wait_ge(normed_done, norm_tiles(MIX[1]) + KT)
                    sp.dma_start(pos[RR, :], dram["positions_2"].broadcast_to([ROPE, S])).then_inc(pos_landed, 16)
            for n in range(2):
                load_wide(c0 + 4 + n, w[:, 0:4 * S], 4 + n)
            for n in range(2):
                load_tiles(c0 + 6 + n, tiles, 12 + 2 * n)

            def columns(first, n=P):
                return w[:, first:first + n].rearrange("(k p) c -> p k c", p=P)
            lat = 4 * S + 2 * ML_HEADS
            blocks = [columns(lat + n * P) for n in range(5)] + [
                columns(lat + 5 * P + ROPE - QK_DIM, QK_DIM), columns(4 * S), columns(4 * S + ML_HEADS)]
            for n in range(4):
                c = start["od_lat"][0] + n
                dst = halves(KT, P)
                if n == 2:
                    dst[1] = dst[1][:, :, 0:QK_DIM]
                load(c, blocks[2 * n], blocks[2 * n + 1], *dst)
            uq = dram["od_w_uq_2"][0].rearrange("(k p) (h c) -> h p k c", p=P, c=QK_DIM)
            for n in range(4):
                load(start["od_uq"][0] + n, uq[2 * n], uq[2 * n + 1], *[d[:, :, 0:QK_DIM] for d in halves(3, P)])
            for n in range(4):
                load_tiles(start["od_ukv"][0] + n, by_tile(dram["od_w_ukv_2"][0]), 2 * n, k=2)
            uv = dram["od_w_ukv_2"][0].rearrange("(k p) (h c) -> k p h c", p=P, c=P)[:, :, :, NOPE:P]
            for n in range(2):
                load(start["od_uv"][0] + n, uv[0][:, 4 * n:4 * n + 4, :], uv[1][:, 4 * n:4 * n + 4, :],
                     *halves(4, HD))
            for n in range(4):
                load_tiles(start["od_out"][0] + n, by_tile(dram["od_w_out_2"][0]), 2 * n)
            cross_attention(1)
            sp.wait_ge(out_ready, KT)
            for t in range(TT):
                sp.dma_start(out[0, t * P:(t + 1) * P, :], x_out[:, t, :]).then_inc(out_stored, 16)
            sp.wait_ge(out_stored, 16 * TT)

        @block.tensor
        def _(pe):
            def product(bank, lhs, rhs, k):
                last = None
                for n in range(k):
                    (a_hi, a_lo), (b_hi, b_lo) = lhs(n), rhs(n)
                    pe.matmul(bank, a_hi, b_hi, start=(n == 0), stop=False)
                    pe.matmul(bank, a_hi, b_lo, start=False, stop=False)
                    last = pe.matmul(bank, a_lo, b_hi, start=False, stop=(n == k - 1))
                return last

            def weight(s, m, width=P):
                def at(k):
                    o = m * HALF + k * P
                    return w_hi[:, s, o:o + width], w_lo[:, s, o:o + width]
                return at

            def operand(hi, lo, n=S):
                def at(k):
                    return hi[:, k, 0:n], lo[:, k, 0:n]
                return at

            hidden = operand(hid_hi, hid_lo)
            normal = operand(h_hi, h_lo)

            def chunk_in(c):
                pe.wait_ge(w_lo_done, c * 2 + 2)
                pe.wait_ge(m_free, c + 1)

            def two_tiles(c, s, rhs, k, widths=(P, P), n=S):
                chunk_in(c)
                for m in range(2):
                    last = product(M[2 * s + m][0:widths[m], 0:n], weight(s, m, widths[m]), rhs, k)
                last.then_inc(w_used, 1)

            def token_major(c, s, hi, lo, k, tiles, pick=None):
                chunk_in(c)
                for t in range(tiles):
                    def tokens(n):
                        if pick is None:
                            return hi[:, n, t * P:(t + 1) * P], lo[:, n, t * P:(t + 1) * P]
                        return pick(hi[:, n, :], t), pick(lo[:, n, :], t)

                    def columns(n):
                        o = (n // (k // 2)) * HALF + (n % (k // 2)) * 2 * P
                        return w_hi[:, s, o:o + 2 * P], w_lo[:, s, o:o + 2 * P]
                    half = (t % 2) * 2 * P
                    last = product(M[2 * s + t // 2][:, half:half + 2 * P], tokens, columns, k)
                last.then_inc(w_used, 1)

            def norm(n, tokens=S):
                kt = NORMS[n][0]
                for k in range(kt):
                    pe.wait_ge(square_done, norm_tiles(n) + k + 1)
                    pe.matmul(A[0][:, 0:tokens], ones, square[:, k % 2, 0:tokens], start=(k == 0), stop=(k == kt - 1))\
                      .then_inc(square_used, 1)

            def feed_forward(l, n_norm):
                for half, (f0, n) in enumerate(HALVES):
                    c0 = start[f"up{l}{half}"][0]
                    if half == 0:
                        pe.wait_ge(h_lo_done, split_norm(n_norm) + KT)
                    with pe.Fori(0, n // 2) as i:
                        for s in range(2):
                            two_tiles(i * 2 + (c0 + s), s, normal, KT)
                    c0 = start[f"down{l}{half}"][0]
                    pe.wait_ge(hid_lo_done, up_counts(l, half) + n)

                    def down_weight(s):
                        def at(k):
                            o = (k // (n // 2)) * HALF + (k % (n // 2)) * P
                            return w_hi[:, s, o:o + P], w_lo[:, s, o:o + P]
                        return at
                    with pe.Fori(0, KT // 2) as i:
                        for s in range(2):
                            chunk_in(i * 2 + (c0 + s))
                            product(M[2 * s][:, :], down_weight(s), hidden, n).then_inc(w_used, 1)

            def mixture_head(l, h):
                n = l * SLOTS + h
                lo = (h % 2) * HD
                q = [qk_a[lo:lo + HD, 2 * g + h // 2, :] for g in range(GROUPS)]
                k = [qk_a[lo:lo + HD, 6 + 2 * g + h // 2, :] for g in range(GROUPS)]
                blocks = [(0, 0, b, b) for b in range(TT)] + [(1, 0, b, b - 1) for b in range(1, TT)]
                blocks += [(g + 1, g, b, b) for g in (1, 2) for b in range(TT)]
                pe.wait_ge(a_free, l * 2 * SLOTS + h + 1)
                for plane, g, qb, kb in blocks:
                    last = pe.matmul(A[plane][:, qb * P:(qb + 1) * P], q[g][:, qb * P:(qb + 1) * P],
                                     k[g][:, kb * P:(kb + 1) * P], start=True, stop=True)
                last.then_inc(scores_done, 1)
                gate_tile(l, h, 0)
                pe.wait_ge(max_done, n + 1)
                for g, at in enumerate((0, 8, 12)):
                    for b in range(TT):
                        last = pe.matmul(A[g][:, b * P:(b + 1) * P],
                                         row_max[:, at + b:at + b + 1].broadcast_to([P, P]), ident,
                                         start=True, stop=True)
                last.then_inc(max_spread, 1)
                gate_tile(l, h, 1)
                pe.wait_ge(exp_done, n + 1)
                pe.wait_ge(max_copied, GROUPS * (n + 1))
                for plane in range(PLANES):
                    for b in range(1 if plane == 1 else 0, TT):
                        last = pe.transpose(A[plane][:, b * P:(b + 1) * P],
                                            prob[:, plane, b * P:(b + 1) * P], ident)
                    last.then_inc(turned_plane, 1)
                for g in range(GROUPS):
                    pair = g * SLOTS // 2 + h // 2
                    pe.wait_ge(plane_back, PLANES * n + (2 if g == 0 else g + 2))
                    for b in range(TT):
                        keys = [(0, b), (1, b - 1)] if g == 0 else [(g + 1, b)]
                        keys = [(plane, kb) for plane, kb in keys if kb >= 0]
                        for j, (plane, kb) in enumerate(keys):
                            last = pe.matmul(A[g][:, b * P:(b + 1) * P],
                                             v_a[:, kb, pair, h % 2:h % 2 + 2, :].rearrange("p a c -> p (a c)"),
                                             prob[:, plane, b * P:(b + 1) * P],
                                             start=(j == 0), stop=(j == len(keys) - 1))
                last.then_inc(pv_done, 1)

            def stick_head(l, h):
                n = l * SLOTS + h
                lo = (h % 2) * HD
                q, k = qk_b[lo:lo + HD, h // 2, :], qk_b[lo:lo + HD, 2 + h // 2, :]
                pe.wait_ge(a_free, l * 2 * SLOTS + SLOTS + h + 1)
                where = [(A[0], 0), (A[1], 0), (A[2], 0), (A[2], 2 * P)]
                for kb, (bank, at) in enumerate(where):
                    last = pe.matmul(bank[:, at:at + ST_N[kb]], k[:, kb * P:(kb + 1) * P], q[:, kb * P:],
                                     start=True, stop=True)
                last.then_inc(z_done, 1)
                gate_tile(l, SLOTS + h, 0)
                pe.wait_ge(stay_done, n + 1)
                for kb, (bank, at) in enumerate(where):
                    for jb in range(kb, TT):
                        skip = (jb - kb) * P
                        last = pe.matmul(bank[:, at + skip:at + ST_N[kb]], tri if jb == kb else ones,
                                         log_stay[:, ST[jb]:ST[jb] + ST_N[jb]],
                                         start=(jb == kb), stop=(jb == TT - 1))
                last.then_inc(later_done, 1)
                gate_tile(l, SLOTS + h, 1)
                pe.wait_ge(st_prob, n + 1)
                for kb in range(TT):
                    last = pe.matmul(A[3][lo:lo + HD, kb * P:], v_b[:, kb, h * HD:(h + 1) * HD],
                                     log_one[:, ST[kb]:ST[kb] + ST_N[kb]], start=(kb == 0), stop=(kb == TT - 1))
                last.then_inc(st_pv, 1)

            def gate_tile(l, j, m):
                c = start[f"gate{l}"][0] + j
                if m == 0:
                    chunk_in(c)
                last = product(M[2 * (c % 2) + m][:, :], weight(c % 2, m), normal, KT)
                if m == 1:
                    last.then_inc(w_used, 1)

            pe.sem_inc(w_used, 2)
            pe.wait_ge(inputs_landed, 16 * INPUTS)
            for g, (at, n) in enumerate(VEC_ROWS):
                last = pe.transpose(A[0][:, at:at + n], rows[0:n, g, :], ident[0:n, 0:n])
            last.then_inc(turned, 1)
            for k in range(KT):
                bank = A[1 + k % 3]
                if k >= 3:
                    pe.wait_ge(turned_out, 1 + k - 2)
                for j in range(TT):
                    last = pe.transpose(bank[:, j * P:(j + 1) * P], x_tok[:, j, k * P:(k + 1) * P], ident)
                last.then_inc(turned, 1)

            for l in range(DEPTH):
                norm(2 * l)
                pe.wait_ge(h_lo_done, split_norm(2 * l) + KT)
                c0 = start[f"qk{l}"][0]
                with pe.Fori(0, 4) as i:
                    for s in range(2):
                        two_tiles(i * 2 + (c0 + s), s, normal, KT)
                c0 = start[f"v{l}"][0]
                for g in range(GROUPS):
                    def residue_tile(t, n, g=g):
                        if g == 0:
                            return t[:, n * P:(n + 1) * P]
                        r = by_residue(t, g)
                        return r[:, n, :]
                    token_major(c0 + g, g % 2, h_hi, h_lo, KT, TT, residue_tile)
                token_major(c0 + 3, 1, h_hi, h_lo, KT, TT)
                pe.wait_ge(m_free, c0 + 4 + 2)
                pe.wait_ge(ones_set, l + 1)
                for h in range(SLOTS):
                    mixture_head(l, h)
                for h in range(SLOTS):
                    stick_head(l, h)
                c0 = start[f"br{l}"][0]
                pe.wait_ge(o_lo_done, 2 * l + 2)
                for n in range(2):
                    chunk_in(c0 + n) if n == 0 else pe.wait_ge(w_lo_done, 2 * (c0 + n) + 2)
                    for m in range(4):
                        j = n * 4 + m
                        pe.wait_ge(br_free, l * KT + j + 1)
                        for ab in range(2):
                            def branch(k):
                                o = ab * HALF + k * S + m * P
                                return w_hi[:, n, o:o + P], w_lo[:, n, o:o + P]

                            def mixed(k):
                                return o_hi[:, 2 * ab + k, :], o_lo[:, 2 * ab + k, :]
                            last = product(M[2 * (j % 2) + ab][:, :], branch, mixed, 2)
                        last.then_inc(w_used if m == 3 else br_full, 1)
                pe.wait_ge(mg_lo_done, KT * (l + 1))
                c0 = start[f"wo{l}"][0]
                with pe.Fori(0, 2) as i:
                    for s in range(2):
                        two_tiles(i * 2 + (c0 + s), s, normal, KT)
                norm(2 * l + 1)
                feed_forward(l, 2 * l + 1)
            norm(2 * DEPTH)
            def looped_tiles(name, rhs, k):
                c0, n = start[name]
                with pe.Fori(0, n // 2) as i:
                    for s in range(2):
                        two_tiles(i * 2 + (c0 + s), s, rhs, k)

            def attend(kind, scores, values):
                heads, key_tiles, widths, at, turned_at, first_q, prob_, turned_, _ = attention(kind)
                n0 = AT0[kind]

                def score(h):
                    if h >= 2:
                        pe.wait_ge(at_out, n0 + h - 1)
                    scores(h, head_banks(h)).then_inc(at_scores, 1)
                score(0)
                for h in range(heads):
                    if h + 1 < heads:
                        score(h + 1)
                    bank = head_banks(h)
                    pe.wait_ge(at_norm, n0 + h + 1)
                    for kt in range(key_tiles):
                        for i in range(first_q[kt] // P, TT):
                            last = pe.transpose(bank[kt][:, i * P:(i + 1) * P],
                                                prob_[:, h % 2, at[i] + kt * P:at[i] + (kt + 1) * P], ident)
                    last.then_inc(at_turned, 1)
                    pe.wait_ge(at_back, n0 + h + 1)
                    rows_ = result(kind, h)[2]
                    for kt in range(key_tiles):
                        last = pe.matmul(bank[0][rows_, first_q[kt]:], values(h, kt),
                                         turned_[:, h % 2, turned_at[kt]:turned_at[kt] + S - first_q[kt]],
                                         start=(kt == 0), stop=(kt == key_tiles - 1))
                    last.then_inc(at_pv, 1)

            def cross_attention(l):
                pe.wait_ge(mem_landed, 16 * (N_MEM // P) * (l + 1))
                for k in range(KT):
                    if k >= 4:
                        pe.wait_ge(mem_out, l * KT + k - 3)
                    for t in range(N_MEM // P):
                        last = pe.transpose(A[k % 4][:, t * P:(t + 1) * P], mem_tok[:, t, k * P:(k + 1) * P], ident)
                    last.then_inc(mem_turned, 1)
                norm(MEMORY[l], N_MEM)
                pe.wait_ge(h_lo_done, split_norm(MEMORY[l]) + KT)
                c0 = start[f"xkv{l}"][0]
                for n in range(2):
                    two_tiles(c0 + n, n, operand(mem_hi, mem_lo, N_MEM), KT, n=N_MEM)
                for n in range(2):
                    token_major(c0 + 2 + n, n, mem_hi, mem_lo, KT, N_MEM // P)
                norm(XATTN[l])
                pe.wait_ge(h_lo_done, split_norm(XATTN[l]) + KT)
                for n in range(2):
                    two_tiles(start[f"xq{l}"][0] + n, n, normal, KT)
                pe.wait_ge(m_free, sum(start[f"xq{l}"]) + 2)

                def scores(h, bank):
                    for i in range(TT):
                        last = pe.matmul(bank[i][:, 0:N_MEM], q_x[:, h, i * P:(i + 1) * P], k_x[:, h, :],
                                         start=True, stop=True)
                    return last
                attend(f"x{l}", scores, lambda h, kt: v_x[:, kt, h * P:(h + 1) * P])
                pe.wait_ge(at_out, AT0[f"x{l}"] + 4)
                looped_tiles(f"xo{l}", operand(xo_hi, xo_lo), 4)
                norm(FFN[l])
                feed_forward(2 + l, FFN[l])

            norm(MIX[0])
            pe.wait_ge(h_lo_done, split_norm(MIX[0]) + KT)
            looped_tiles("ev_in", normal, KT)
            pe.wait_ge(pool_landed, 16)
            for g in range(4):
                pe.wait_ge(pool_in, g + 1)
                pe.matmul(A[g][:, :], pool_w[:, g, :], pooled[:, g, :], start=True, stop=True).then_inc(pool_out, 1)
            pe.wait_ge(ev_y_lo, KT)
            looped_tiles("ev_out", operand(y_hi, y_lo), KT)
            cross_attention(0)

            norm(MIX[1])
            pe.wait_ge(h_lo_done, split_norm(MIX[1]) + KT)
            c0 = start["od_in"][0]
            with pe.Fori(0, 2) as i:
                for s in range(2):
                    two_tiles(i * 2 + (c0 + s), s, normal, KT)
            for n in range(2):
                token_major(c0 + 4 + n, n, h_hi, h_lo, KT, TT)
            for n in range(2):
                two_tiles(c0 + 6 + n, n, normal, KT)
            c0 = start["od_lat"][0]
            for n in range(4):
                two_tiles(c0 + n, n % 2, normal, KT, widths=(P, QK_DIM) if n == 2 else (P, P))
            pe.wait_ge(rows_done, 1)
            for t in range(TT):
                last = pe.transpose(A[1][:, t * ML_HEADS:(t + 1) * ML_HEADS],
                                    g_i[0:ML_HEADS, t * P:(t + 1) * P], ident[0:ML_HEADS, 0:ML_HEADS])
            last.then_inc(a_turned, 1)
            norm(LATENT_Q)
            norm(LATENT_KV)
            pe.wait_ge(a_out, 1)
            pe.wait_ge(rstd_done, LATENT_KV + 1)
            pe.wait_ge(m_free, sum(start["od_gk"]) + 2)
            pe.wait_ge(og_done, 2)

            key_banks = [(A[0], 0), (A[1], 0), (A[2], 0), (A[2], 2 * P)]

            def ml_score(h):
                for st, (bank, at) in enumerate(key_banks):
                    pe.matmul(bank[:, at:at + ST_N[st]], k_m[:, h, st * P:(st + 1) * P], q_m[:, h, st * P:],
                              start=True, stop=True)
                row = ident[0:ML_HEADS, h:h + 1].broadcast_to([ML_HEADS, P])
                pe.matmul(A[3][:, :], row, g_top[0:ML_HEADS, :], start=True, stop=True)
                pe.matmul(M[0][:, :], row, g_sum[0:ML_HEADS, :], start=True, stop=True).then_inc(ml_scores, 1)

            ml_score(0)
            for h in range(ML_HEADS):
                pe.wait_ge(ml_sw_done, h + 1)
                if h:
                    pe.wait_ge(ml_hm, h)
                for st in range(TT):
                    pe.matmul(M[1][:, st * P:], v_ml[:, st, h * P:(h + 1) * P], ml_sw[:, ST[st]:ST[st] + ST_N[st]],
                              start=(st == 0), stop=(st == TT - 1))
                for st in range(TT):
                    last = pe.matmul(M[2][:, st * P:], ones, ml_sw[:, ST[st]:ST[st] + ST_N[st]],
                                     start=(st == 0), stop=(st == TT - 1))
                last.then_inc(ml_nd, 1)
                if h + 1 < ML_HEADS:
                    ml_score(h + 1)
                pe.wait_ge(ml_sq, h + 1)
                pe.matmul(M[3][:, :], ones, ml_3[:, :], start=True, stop=True).then_inc(ml_ss, 1)
            pe.wait_ge(ml_out, ML_HEADS)
            pe.wait_ge(h_lo_done, split_norm(LATENT_KV) + 2)
            for n in range(4):
                two_tiles(start["od_uq"][0] + n, n % 2, operand(cq_hi, cq_lo), 3, widths=(QK_DIM, QK_DIM))
            for n in range(4):
                two_tiles(start["od_ukv"][0] + n, n % 2, operand(ckv_hi, ckv_lo), 2)
            for n in range(2):
                token_major(start["od_uv"][0] + n, n % 2, ckv_hi, ckv_lo, 2, TT)
            rot = const[RR, C_ROT:C_ROT + ROPE]
            pe.wait_ge(m_free, sum(start["od_uv"]) + 2)
            for n in range(MLA_HEADS + 1):
                if n >= 4:
                    pe.wait_ge(rope_free, n - 3)
                src = k_rope[RR, :] if n == 0 else q_h[RR, n - 1, :]
                pe.matmul(A[n % 4][RR, :], rot, src, start=True, stop=True).then_inc(rope_turned, 1)
            pe.wait_ge(rope_done, 1)
            pe.wait_ge(rope_spread, 1)

            def scores(h, bank):
                for i in range(TT):
                    n = (i + 1) * P
                    pe.matmul(bank[i][:, 0:n], q_h[0:QK_DIM, h, i * P:(i + 1) * P], k_h[0:QK_DIM, h, 0:n],
                              start=True, stop=False)
                    last = pe.matmul(bank[i][:, n - P:n], ident, const[:, C_CAUSAL:C_CAUSAL + P],
                                     start=False, stop=True)
                return last
            attend("mla", scores, lambda h, kt: v_h[:, kt, h * HD:(h + 1) * HD])
            pe.wait_ge(at_out, AT0["mla"] + MLA_HEADS)
            looped_tiles("od_out", normal, KT)
            cross_attention(1)
            norm(LAST_NORM)
            for k in range(KT):
                pe.wait_ge(normed_done, norm_tiles(LAST_NORM) + k + 1)
                if k >= 4:
                    pe.wait_ge(out_ready, k - 3)
                for t in range(TT):
                    last = pe.transpose(A[k % 4][:, t * P:(t + 1) * P], x[:, k, t * P:(t + 1) * P], ident)
                last.then_inc(out_turned, 1)

        @block.scalar
        def _(act):
            def split_hi(c, s, n=HALF):
                act.wait_ge(w_used, c + 1)
                for part in range(2):
                    act.wait_ge(landed[part], c * 16 + 16)
                    act.activation(w_hi[:, s, part * HALF:part * HALF + n], stage[:, part, 0:n], ACT.Copy)\
                       .then_inc(w_hi_done, 1)

            def split_after(c, s):
                if c + 2 < chunks:
                    split_hi(c + 2, s, size[c + 2])

            def splits(name):
                c0, n = start[name]
                with act.Fori(0, n // 2) as i:
                    for s in range(2):
                        split_hi(i * 2 + (c0 + s + 2), s)

            def norm(n, src, x_ready, hi=h_hi, tokens=S):
                kt, before = NORMS[n][0], norm_tiles(n)
                act.wait_ge(*x_ready)
                for k in range(kt):
                    if k >= 2:
                        act.wait_ge(square_used, before + k - 1)
                    act.activation(square[:, k % 2, 0:tokens], src[:, k, 0:tokens], ACT.Square).then_inc(square_done, 1)
                act.wait_ge(square_used, before + kt)
                act.activation(rstd[:, 0:tokens], A[0][:, 0:tokens], ACT.Ln, bias=eps[:, 0:1], scale=1.0 / (kt * P))\
                   .then_inc(root_done, 1)
                act.wait_ge(root_done, n + 1)
                act.activation(rstd[:, 0:tokens], rstd[:, 0:tokens], ACT.Exp, scale=-0.5).then_inc(rstd_done, 1)
                if hi is not None:
                    for k in range(kt):
                        act.wait_ge(normed_done, before + k + 1)
                        act.activation(hi[:, k, 0:tokens], normed[:, k % 2, 0:tokens], ACT.Copy).then_inc(h_hi_done, 1)

            def feed_forward(l, kind):
                for half, (f0, n) in enumerate(HALVES):
                    c0 = start[f"up{l}{half}"][0]
                    u0 = up_counts(l, half)
                    with act.Fori(0, n // 2) as i:
                        for s in range(2):
                            u = i * 2 + (u0 + s)
                            act.wait_ge(w_used, i * 2 + (c0 + s + 3))
                            if kind == "conv":
                                act.activation(conv[:, s, :], M[2 * s][:, :], ACT.Identity,
                                               bias=col_at("conv_b", i * 2 + (l * FT + f0 + s)),
                                               scale=col_at(f"conv_w{l}", i * 2 + (2 * FT + f0 + s)))\
                                   .then_inc(tap_done, 1)
                                split_hi(i * 2 + (c0 + s + 2), s)
                                act.wait_ge(conv_done, u + 1)
                                act.activation(acted[:, s, :], conv[:, s, :], ACT.Gelu).then_inc(acted_done, 1)
                            else:
                                act.activation(acted[:, s, :], M[2 * s][:, :], ACT.Silu).then_inc(acted_done, 1)
                                split_hi(i * 2 + (c0 + s + 2), s)
                            act.wait_ge(m_free, i * 2 + (c0 + s + 3))
                            act.activation(hid_hi[:, i * 2 + s, :], hid[:, s, :], ACT.Copy).then_inc(hid_hi_done, 1)
                    if sum(start[f"down{l}{half}"]) < chunks:
                        splits(f"down{l}{half}")
                    else:
                        for c in range(start[f"down{l}{half}"][0], chunks):
                            split_after(c, c % 2)

            def gate_chunk(l, j):
                c = start[f"gate{l}"][0] + j
                act.wait_ge(w_used, c + 3)
                for m in range(2):
                    act.activation(gate[:, 2 * j + m, :], M[2 * (c % 2) + m][:, :], ACT.Exp,
                                   bias=neg_gate[:, l * 16 + 2 * j + m:l * 16 + 2 * j + m + 1], scale=-1.0)\
                       .then_inc(gate_exp, 1)
                two = gate[:, 2 * j:2 * j + 2, :]
                act.wait_ge(gate_exp, (l * 8 + j) * 2 + 2)
                act.activation(two, two, ACT.Ln, bias=1.0).then_inc(gate_ln, 1)
                split_after(c, c % 2)
                act.wait_ge(gate_ln, l * 8 + j + 1)
                act.activation(two, two, ACT.Exp, scale=-1.0).then_inc(gate_done, 1)

            def mixture_head(l, h):
                n = l * SLOTS + h
                act.wait_ge(max_spread, n + 1)
                for g in range(GROUPS):
                    act.activation(nat(top[:, g, :], g), over(A[g][:, :], g), ACT.Copy).then_inc(max_copied, 1)
                act.wait_ge(shifted, n + 1)
                act.activation(prob[:, :, :], prob[:, :, :], ACT.Exp).then_inc(exp_done, 1)
                for plane in range(PLANES):
                    act.wait_ge(turned_plane, PLANES * n + plane + 1)
                    skip = P if plane == 1 else 0
                    act.activation(prob[:, plane, skip:], A[plane][:, skip:], ACT.Copy).then_inc(plane_back, 1)
                act.wait_ge(top_shift, n + 1)
                act.activation(top[:, :, :], top[:, :, :], ACT.Exp).then_inc(weight_done, 1)
                lo = (h % 2) * HD
                act.wait_ge(mix_step, 3 * n + 3)
                act.activation(prob[lo:lo + HD, 3, :], prob[lo:lo + HD, 3, :], ACT.Ln).then_inc(den_step, 1)
                act.wait_ge(den_step, n + 1)
                act.activation(prob[lo:lo + HD, 3, :], prob[lo:lo + HD, 3, :], ACT.Exp, scale=-1.0)\
                   .then_inc(den_done, 1)
                gate_chunk(l, h)

            def stick_head(l, h):
                n = l * SLOTS + h
                act.wait_ge(z_done, n + 1)
                if h == 0:
                    act.wait_ge(o_done, (l + 1) * SLOTS)
                for bank, at, width in ((A[0], 0, S), (A[1], S, S - P), (A[2], 2 * S - P, S - P)):
                    last = act.activation(log_one[:, at:at + width], bank[:, 0:width], ACT.Abs, scale=HD ** -0.5)
                last.then_inc(st_act, 1)
                act.wait_ge(st_act, 2 * n + 1)
                act.activation(log_one, log_one, ACT.Exp, scale=-1.0).then_inc(st_act, 1)
                act.wait_ge(st_act, 2 * n + 2)
                act.activation(log_one, log_one, ACT.Ln, bias=1.0).then_inc(log_done, 1)
                act.wait_ge(st_arg, n + 1)
                act.activation(log_one, log_sig, ACT.Exp).then_inc(st_exp, 1)
                gate_chunk(l, SLOTS + h)

            split_hi(0, 0)
            split_hi(1, 1)
            act.wait_ge(consts_set, 2)

            for l in range(DEPTH):
                norm(2 * l, x, (turned_out, KT + 1) if l == 0 else (m_free, start[f"qk{l}"][0] + 2))
                for stage_name in (f"qk{l}", f"v{l}"):
                    splits(stage_name)
                for h in range(SLOTS):
                    mixture_head(l, h)
                for h in range(SLOTS):
                    stick_head(l, h)
                    if h == 0:
                        act.wait_ge(o_done, (l + 1) * SLOTS)
                        act.activation(o_hi[:, 0:2, :], o_a[:, :, :], ACT.Copy).then_inc(o_hi_done, 1)
                act.wait_ge(a_free, (l + 1) * 2 * SLOTS + 1)
                act.activation(o_hi[:, 2:4, :], o_b[:, :, :], ACT.Copy).then_inc(o_hi_done, 1)
                c0 = start[f"br{l}"][0]
                for j in range(KT):
                    act.wait_ge(merged_done, l * KT + j + 1)
                    act.activation(h_hi[:, j, :], merged[:, j % 2, :], ACT.Copy).then_inc(mg_hi_done, 1)
                    if j % 4 == 3:
                        split_after(c0 + j // 4, (c0 + j // 4) % 2)
                splits(f"wo{l}")
                norm(2 * l + 1, x, (m_free, start[f"up{l}0"][0] + 2))
                feed_forward(l, "conv")
            norm(2 * DEPTH, x, (m_free, (start["ev_in"][0] if BLOCK2 else chunks) + 2), hi=None)
            def attend(kind):
                heads, key_tiles, widths, at, turned_at, first_q, prob_, turned_, scale = attention(kind)
                n0 = AT0[kind]

                def exps(h):
                    act.wait_ge(at_max, n0 + h + 1)
                    for i in range(TT):
                        last = act.activation(prob_[:, h % 2, at[i]:at[i] + widths[i]],
                                              head_banks(h)[i][:, 0:widths[i]], ACT.Exp,
                                              bias=neg_max[:, 4 * (h % 2) + i:4 * (h % 2) + i + 1], scale=scale,
                                              accum_out=soft_den[:, 4 * (h % 2) + i:4 * (h % 2) + i + 1])
                    last.then_inc(at_exp, 1)
                exps(0)
                for h in range(heads):
                    if h + 1 < heads:
                        exps(h + 1)
                    act.wait_ge(at_turned, n0 + h + 1)
                    for kt in range(key_tiles):
                        last = act.activation(turned_[:, h % 2, turned_at[kt]:turned_at[kt] + S - first_q[kt]],
                                              head_banks(h)[kt][:, first_q[kt]:], ACT.Copy)
                    last.then_inc(at_back, 1)
                    act.wait_ge(at_pv, n0 + h + 1)
                    hi, _, rows_ = result(kind, h)
                    act.activation(hi, head_banks(h)[0][rows_, :], ACT.Copy).then_inc(at_hi, 1)

            def straight_splits(name):
                c0, n = start[name]
                for c in range(c0, c0 + n):
                    split_after(c, c % 2)

            def cross_attention(l):
                norm(MEMORY[l], mem_t, (mem_out, KT * (l + 1)), hi=mem_hi, tokens=N_MEM)
                straight_splits(f"xkv{l}")
                norm(XATTN[l], x, (m_free, sum(start[f"xkv{l}"]) + 2))
                straight_splits(f"xq{l}")
                attend(f"x{l}")
                splits(f"xo{l}")
                norm(FFN[l], x, (m_free, sum(start[f"xo{l}"]) + 2))
                feed_forward(2 + l, "silu")

            norm(MIX[0], x, (normed_done, norm_tiles(MIX[0])))
            def round_y(t):
                act.wait_ge(ev_y, t + 1)
                act.activation(y_hi[:, t, :], y[:, t % 2, :], ACT.Copy).then_inc(ev_y_hi, 1)

            c0 = start["ev_in"][0]
            for n in range(8):
                split_after(c0 + n, n % 2)
                if n in (4, 5):
                    round_y(2 * (n - 4))
                    round_y(2 * (n - 4) + 1)
            for t in range(4, KT):
                round_y(t)
            splits("ev_out")
            cross_attention(0)

            norm(MIX[1], x, (m_free, start["od_in"][0] + 2))
            act.wait_ge(trig_arg, 1)
            act.activation(sin[RR, :], rest[RR, :], ACT.Sin).then_inc(trig_done, 1)
            act.activation(rest_abs[RR, :], rest[RR, :], ACT.Abs).then_inc(trig_done, 1)
            act.wait_ge(trig_done, 2)
            act.activation(cos[RR, :], rest_abs[RR, :], ACT.Sin, bias=half_pi[RR, 0:1], scale=-1.0)\
               .then_inc(trig_done, 1)
            c0 = start["od_in"][0]
            for c in range(c0, c0 + 6):
                split_after(c, c % 2)
            for n in range(2):
                c = c0 + 6 + n
                act.wait_ge(w_used, c + 3)
                for m in range(2):
                    act.activation(sig_o[:, 2 * n + m, :], M[2 * (c % 2) + m][:, :], ACT.Exp, scale=-1.0)\
                       .then_inc(og_exp, 1)
                two = sig_o[:, 2 * n:2 * n + 2, :]
                act.wait_ge(og_exp, 2 * n + 2)
                act.activation(two, two, ACT.Ln, bias=1.0).then_inc(og_ln, 1)
                act.wait_ge(og_ln, n + 1)
                act.activation(two, two, ACT.Exp, scale=-1.0).then_inc(og_done, 1)
                split_after(c, c % 2)
            straight_splits("od_lat")
            straight_splits("od_gk")
            act.wait_ge(f_in, 2)
            fr = g_one[0:ML_HEADS, :]
            act.activation(fr, g_f[0:ML_HEADS, :], ACT.Abs).then_inc(f_step, 1)
            act.wait_ge(f_step, 1)
            act.activation(fr, fr, ACT.Exp, scale=-1.0).then_inc(f_step, 1)
            act.wait_ge(f_step, 2)
            act.activation(fr, fr, ACT.Ln, bias=1.0).then_inc(f_log, 1)
            norm(LATENT_Q, latent[:, 0:3, :], (m_free, sum(start["od_gk"]) + 2), hi=cq_hi)
            norm(LATENT_KV, latent[:, 3:5, :], (m_free, sum(start["od_gk"]) + 2), hi=ckv_hi)
            for h in range(ML_HEADS):
                act.wait_ge(ml_diag_done, h + 1)
                act.activation(ml_0[:, :], M[0][:, :], ACT.Exp, scale=-1.0)
                for st in range(TT):
                    a_st = a_col[:, st * ML_HEADS + h:st * ML_HEADS + h + 1]
                    last = act.activation(ml_w[:, ST[st]:ST[st] + P], ml_diag[:, st * P:(st + 1) * P], ACT.Exp, bias=a_st)
                    if st + 1 < TT:
                        act.activation(ml_w[:, ST[st] + P:ST[st] + ST_N[st]], A[3][:, (st + 1) * P:], ACT.Exp,
                                       bias=a_st, scale=-1.0)
                last.then_inc(ml_w_done, 1)
                act.wait_ge(ml_nd, h + 1)
                act.activation(ml_1[:, :], M[2][:, :], ACT.Abs).then_inc(ml_abs, 1)
                act.wait_ge(ml_hm, h + 1)
                act.activation(ml_3[:, :], ml_2[:, :], ACT.Square).then_inc(ml_sq, 1)
                act.wait_ge(ml_ss, h + 1)
                act.activation(ml_0[:, :], M[3][:, :], ACT.Ln, bias=eps[:, 0:1], scale=1.0 / P).then_inc(ml_ln, 1)
                act.wait_ge(ml_ln, h + 1)
                act.activation(ml_0[:, :], ml_0[:, :], ACT.Exp, scale=-0.5).then_inc(ml_rs, 1)
                act.wait_ge(ml_y, h + 1)
                act.activation(h_hi[:, h, :], ml_2[:, :], ACT.Copy).then_inc(ml_hi, 1)
            for name in ("od_uq", "od_ukv", "od_uv"):
                straight_splits(name)
            act.wait_ge(rope_k, 1)
            act.activation(k_h[RR, :, :], k_rope[RR, :].unsqueeze(1).broadcast_to([ROPE, MLA_HEADS, S]), ACT.Copy)\
               .then_inc(rope_spread, 1)
            attend("mla")
            splits("od_out")
            cross_attention(1)
            norm(LAST_NORM, x, (m_free, chunks + 2), hi=None)

        @block.vector
        def _(dve):
            def split_lo(c, s, n=HALF):
                for part in range(2):
                    dve.wait_ge(w_hi_done, c * 2 + (part + 1))
                    dve.tensor_tensor(w_lo[:, s, part * HALF:part * HALF + n], stage[:, part, 0:n],
                                      w_hi[:, s, part * HALF:part * HALF + n].bitcast(F32), ALU.subtract)\
                       .then_inc(w_lo_done, 1)

            def split_after(c, s):
                if c + 2 < chunks:
                    split_lo(c + 2, s, size[c + 2])

            def pass_banks(c):
                dve.wait_ge(m_free, c + 2)
                dve.sem_inc(m_free, 1)

            def norm(n, src, hi=h_hi, lo=h_lo, gain=None, tokens=S):
                kt, split = NORMS[n][0], split_norm(n)
                dve.wait_ge(rstd_done, n + 1)

                def scaled(k):
                    dst = normed[:, k % 2, 0:tokens] if hi is not None else src[:, k, 0:tokens]
                    if k >= 2 and hi is not None:
                        dve.wait_ge(h_lo_done, split + k - 1)
                    dve.scalar_tensor_tensor(dst, src[:, k, 0:tokens], col(gain[0], gain[1] + k),
                                             rstd[:, 0:tokens], ALU.mult, ALU.mult).then_inc(normed_done, 1)
                if split:
                    dve.wait_ge(h_lo_done, split)
                scaled(0)
                for k in range(kt):
                    if k + 1 < kt:
                        scaled(k + 1)
                    if hi is not None:
                        dve.wait_ge(h_hi_done, split + k + 1)
                        dve.tensor_tensor(lo[:, k, 0:tokens], normed[:, k % 2, 0:tokens],
                                          hi[:, k, 0:tokens].bitcast(F32), ALU.subtract).then_inc(h_lo_done, 1)

            def add_residual(name):
                c0, n = start[name]
                with dve.Fori(0, n // 2) as i:
                    for s in range(2):
                        dve.wait_ge(w_used, i * 2 + (c0 + s + 3))
                        for m in range(2):
                            last = dve.tensor_tensor(x[:, i * 4 + (2 * s + m), :], x[:, i * 4 + (2 * s + m), :],
                                                     M[2 * s + m][:, :], ALU.add)
                        last.then_inc(m_free, 1)
                        split_lo(i * 2 + (c0 + s + 2), s)

            def feed_forward(l, kind):
                for half, (f0, n) in enumerate(HALVES):
                    c0 = start[f"up{l}{half}"][0]
                    u0 = up_counts(l, half)
                    with dve.Fori(0, n // 2) as i:
                        for s in range(2):
                            u = i * 2 + (u0 + s)
                            if kind == "conv":
                                for tap in (1, 0):
                                    back = 2 - tap
                                    if tap == 1:
                                        dve.wait_ge(tap_done, u + 1)
                                    else:
                                        dve.wait_ge(conv_step, u + 1)
                                    dve.scalar_tensor_tensor(
                                        conv[:, s, back:], M[2 * s][:, 0:S - back],
                                        col_at(f"conv_w{l}", i * 2 + (tap * FT + f0 + s)), conv[:, s, back:],
                                        ALU.mult, ALU.add).then_inc(conv_step if tap == 1 else conv_done, 1)
                            split_lo(i * 2 + (c0 + s + 2), s)
                            dve.wait_ge(acted_done, u + 1)
                            dve.tensor_tensor(hid[:, s, :], acted[:, s, :], M[2 * s + 1][:, :], ALU.mult)\
                               .then_inc(m_free, 1)
                            dve.wait_ge(hid_hi_done, u + 1)
                            dve.tensor_tensor(hid_lo[:, i * 2 + s, :], hid[:, s, :],
                                              hid_hi[:, i * 2 + s, :].bitcast(F32), ALU.subtract)\
                               .then_inc(hid_lo_done, 1)
                    c0, count = start[f"down{l}{half}"]

                    def down_chunk(c, s, tile, n_split):
                        dve.wait_ge(w_used, c + 3)
                        dve.tensor_tensor(x[:, tile, :], x[:, tile, :], M[2 * s][:, :], ALU.add)\
                           .then_inc(m_free, 1)
                        if n_split:
                            split_lo(c + 2, s, n_split)
                    if c0 + count < chunks:
                        with dve.Fori(0, KT // 2) as i:
                            for s in range(2):
                                down_chunk(i * 2 + (c0 + s), s, i * 2 + s, HALF)
                    else:
                        for j in range(KT):
                            down_chunk(c0 + j, j % 2, j, size[c0 + j + 2] if c0 + j + 2 < chunks else 0)

            def gate_chunk(l, j):
                c = start[f"gate{l}"][0] + j
                dve.wait_ge(gate_exp, (l * 8 + j) * 2 + 2)
                pass_banks(c)
                split_after(c, c % 2)

            def mixture_head(l, h):
                n = l * SLOTS + h
                dve.wait_ge(scores_done, n + 1)
                if n > 0:
                    dve.wait_ge(o_done, n)
                for plane in range(PLANES):
                    b = 1 if plane == 1 else 0
                    blocks = TT - b
                    dve.scalar_tensor_tensor(
                        prob[:, plane, b * P:].rearrange("p (b c) -> p b c", c=P),
                        A[plane][:, b * P:].rearrange("p (b c) -> p b c", c=P), HD ** -0.5,
                        bias[:, h, plane, :].unsqueeze(1).broadcast_to([P, blocks, P]), ALU.mult, ALU.add)\
                       .then_inc(plane_biased, 1)
                dve.memset(prob[:, 1, 0:P], MASKED).then_inc(plane_biased, 1)
                dve.wait_ge(plane_biased, (PLANES + 1) * (n + 1))
                blocks = prob[:, :, :].rearrange("p n (b c) -> p (n b) c", c=P)
                dve.tensor_reduce(row_max[:, :], blocks, AX_X, ALU.max).then_inc(max_a, 1)
                dve.wait_ge(max_a, n + 1)
                dve.tensor_tensor(row_max[:, 0:4], row_max[:, 0:4], row_max[:, 4:8], ALU.max).then_inc(max_b, 1)
                dve.wait_ge(max_b, n + 1)
                dve.tensor_copy(row_max[:, 4:8], row_max[:, 0:4]).then_inc(max_done, 1)
                dve.wait_ge(max_done, n + 1)
                dve.tensor_tensor(blocks, blocks, row_max[:, :].unsqueeze(2).broadcast_to([P, 16, P]), ALU.subtract)\
                   .then_inc(shifted, 1)
                dve.wait_ge(max_copied, GROUPS * (n + 1))
                dve.tensor_tensor(top_all[:, :], top[:, 0, :], top[:, 1, :], ALU.max).then_inc(top1, 1)
                dve.wait_ge(top1, n + 1)
                dve.tensor_tensor(top_all[:, :], top_all[:, :], top[:, 2, :], ALU.max).then_inc(top2, 1)
                dve.wait_ge(top2, n + 1)
                dve.tensor_tensor(top[:, :, :], top[:, :, :], top_all[:, :].unsqueeze(1).broadcast_to([P, GROUPS, S]),
                                  ALU.subtract).then_inc(top_shift, 1)
                dve.wait_ge(weight_done, n + 1)
                dve.wait_ge(pv_done, n + 1)
                for g in range(GROUPS):
                    last = dve.tensor_tensor(nat(prob[:, g, :], g), nat(top[:, g, :], g), over(A[g][:, :], g), ALU.mult)
                last.then_inc(a_free, 1)
                step = 3 * n
                dve.wait_ge(a_free, l * 2 * SLOTS + h + 2)
                dve.tensor_tensor(prob[:, 0, :], prob[:, 0, :], prob[:, 1, :], ALU.add).then_inc(mix_step, 1)
                dve.wait_ge(mix_step, step + 1)
                dve.tensor_tensor(prob[:, 0, :], prob[:, 0, :], prob[:, 2, :], ALU.add).then_inc(mix_step, 1)
                dve.wait_ge(mix_step, step + 2)
                lo = (h % 2) * HD
                den = HD - lo
                dve.tensor_copy(prob[lo:lo + HD, 3, :], prob[den:den + HD, 0, :]).then_inc(mix_step, 1)
                dve.wait_ge(den_done, n + 1)
                dve.tensor_tensor(o_a[lo:lo + HD, h // 2, :], prob[lo:lo + HD, 0, :], prob[lo:lo + HD, 3, :], ALU.mult)\
                   .then_inc(o_done, 1)
                gate_chunk(l, h)

            def stick_head(l, h):
                n = l * SLOTS + h
                parts = ((A[0], 0, S), (A[1], S, S - P), (A[2], 2 * S - P, S - P))
                scale = HD ** -0.5
                dve.wait_ge(st_act, 2 * n + 1)
                if h == 0:
                    dve.wait_ge(o_done, (l + 1) * SLOTS)
                for bank, at, width in parts:
                    last = dve.tensor_scalar(log_sig[:, at:at + width], bank[:, 0:width], scale, 0.0, ALU.mult, ALU.min)
                last.then_inc(st_dve, 1)
                dve.wait_ge(st_dve, 3 * n + 1)
                dve.wait_ge(log_done, n + 1)
                dve.tensor_tensor(log_sig, log_sig, log_one, ALU.subtract).then_inc(st_dve, 1)
                dve.wait_ge(st_dve, 3 * n + 2)
                for bank, at, width in parts:
                    last = dve.scalar_tensor_tensor(log_stay[:, at:at + width], bank[:, 0:width], -scale,
                                                    log_sig[:, at:at + width], ALU.mult, ALU.add)
                last.then_inc(st_dve, 1)
                dve.wait_ge(st_dve, 3 * n + 3)
                for kb in range(TT):
                    diagonal = log_stay[:, ST[kb]:ST[kb] + P]
                    last = dve.tensor_tensor(diagonal, diagonal, later_mask, ALU.mult)
                last.then_inc(stay_done, 1)
                dve.wait_ge(later_done, n + 1)
                for bank, at, width in parts:
                    last = dve.tensor_tensor(log_sig[:, at:at + width], log_sig[:, at:at + width], bank[:, 0:width], ALU.add)
                last.then_inc(st_arg, 1)
                dve.wait_ge(st_exp, n + 1)
                for kb in range(TT):
                    diagonal = log_one[:, ST[kb]:ST[kb] + P]
                    last = dve.tensor_tensor(diagonal, diagonal, later_mask, ALU.mult)
                last.then_inc(st_prob, 1)
                if h == 0:
                    dve.wait_ge(o_hi_done, 2 * l + 1)
                    dve.tensor_tensor(o_lo[:, 0:2, :], o_a[:, :, :], o_hi[:, 0:2, :].bitcast(F32), ALU.subtract)\
                       .then_inc(o_lo_done, 1)
                dve.wait_ge(st_pv, n + 1)
                lo = (h % 2) * HD
                dve.tensor_copy(o_b[lo:lo + HD, h // 2, :], A[3][lo:lo + HD, :]).then_inc(a_free, 1)
                gate_chunk(l, SLOTS + h)

            dve.memset(half_pi[:, 0:1], np.pi / 2)
            dve.memset(eps[:, 0:1], EPS).then_inc(consts_set, 1)
            dve.sem_inc(m_free, 2)
            dve.sem_inc(br_free, 2)
            dve.sem_inc(a_free, 1)
            split_lo(0, 0)
            split_lo(1, 1)
            dve.wait_ge(turned, 1)
            dve.tensor_copy(vec[:, :], A[0][:, 0:VEC_COLS]).then_inc(turned_out, 1)
            for k in range(KT):
                dve.wait_ge(turned, k + 2)
                dve.tensor_copy(x[:, k, :], A[1 + k % 3][:, :]).then_inc(turned_out, 1)
            dve.wait_ge(turned_out, 1)
            dve.tensor_scalar(neg_gate[:, :], vec[:, VEC["b_gate"]:VEC["b_gate"] + DEPTH * 16], -1.0, None, ALU.mult)\
               .then_inc(consts_set, 1)

            for l in range(DEPTH):
                norm(2 * l, x, gain=("norm1", l * KT))
                dve.memset(v_a[:, :, :, 1, :], 1.0).then_inc(ones_set, 1)
                c0 = start[f"qk{l}"][0]
                for j in range(8):
                    c = c0 + j
                    dve.wait_ge(w_used, c + 3)
                    for m in range(2):
                        if j < 6:
                            g = j % 3
                            dst = as_residue(qk_a[:, 2 * j + m, :], g)
                        else:
                            g = 0
                            dst = qk_b[:, 2 * (j - 6) + m, :]
                        last = dve.tensor_copy(dst, by_residue(M[2 * (c % 2) + m][:, :], g))
                    last.then_inc(m_free, 1)
                    split_after(c, c % 2)
                c0 = start[f"v{l}"][0]
                for j in range(4):
                    c = c0 + j
                    dve.wait_ge(w_used, c + 3)
                    for b in range(2):
                        src = M[2 * (c % 2) + b][:, :]
                        if j == GROUPS:
                            last = dve.tensor_copy(v_b[:, 2 * b:2 * b + 2, :], src.rearrange("p (t c) -> p t c", t=2))
                            continue
                        for t in range(2):
                            last = dve.tensor_copy(
                                v_a[:, 2 * b + t, 2 * j:2 * j + 2, 0:3:2, :],
                                src[:, t * 2 * P:(t + 1) * 2 * P].rearrange("p (a e c) -> p a e c", a=2, e=2))
                    last.then_inc(m_free, 1)
                    split_after(c, c % 2)
                for h in range(SLOTS):
                    mixture_head(l, h)
                for h in range(SLOTS):
                    stick_head(l, h)
                dve.wait_ge(o_hi_done, 2 * l + 2)
                dve.tensor_tensor(o_lo[:, 2:4, :], o_b[:, :, :], o_hi[:, 2:4, :].bitcast(F32), ALU.subtract)\
                   .then_inc(o_lo_done, 1)
                c0 = start[f"br{l}"][0]
                for j in range(KT):
                    n, m = divmod(j, 4)
                    if j == 0:
                        dve.wait_ge(gate_done, (l + 1) * 8)
                    jj = l * KT + j
                    if m < 3:
                        dve.wait_ge(br_full, l * 6 + n * 3 + m + 1)
                    else:
                        dve.wait_ge(w_used, c0 + n + 3)
                    if j >= 2:
                        dve.wait_ge(mg_hi_done, jj - 1)
                    dve.tensor_tensor(merged[:, j % 2, :], gate[:, j, :], M[2 * (j % 2)][:, :], ALU.mult)
                    dve.tensor_tensor(merged[:, 2 + j % 2, :], gate[:, KT + j, :], M[2 * (j % 2) + 1][:, :], ALU.mult)\
                       .then_inc(br_free, 1)
                    dve.wait_ge(br_free, jj + 3)
                    dve.tensor_tensor(merged[:, j % 2, :], merged[:, j % 2, :], merged[:, 2 + j % 2, :], ALU.add)\
                       .then_inc(merged_done, 1)
                    dve.wait_ge(mg_hi_done, jj + 1)
                    dve.tensor_tensor(h_lo[:, j, :], merged[:, j % 2, :], h_hi[:, j, :].bitcast(F32), ALU.subtract)\
                       .then_inc(mg_lo_done, 1)
                    if m == 3:
                        pass_banks(c0 + n)
                        split_after(c0 + n, (c0 + n) % 2)
                add_residual(f"wo{l}")
                norm(2 * l + 1, x, gain=("norm2", l * KT))
                feed_forward(l, "conv")
            norm(2 * DEPTH, x, hi=None, gain=("norm_f", 0))
            done = [0]

            def link(instruction):
                done[0] += 1
                instruction.then_inc(chain, 1)
                dve.wait_ge(chain, done[0])

            def read_out(name, c, tiles):
                dve.wait_ge(w_used, c + 3)
                for dst, src, factor in tiles:
                    if factor is None:
                        last = dve.tensor_copy(dst, src)
                    else:
                        last = dve.tensor_scalar(dst, src, factor, None, ALU.mult)
                last.then_inc(m_free, 1)
                split_after(c, c % 2)

            def attend(kind):
                heads, key_tiles, widths, at, turned_at, first_q, prob_, turned_, scale = attention(kind)
                n0 = AT0[kind]

                def maxima(h):
                    col0 = 4 * (h % 2)
                    dve.wait_ge(at_scores, n0 + h + 1)
                    for i in range(TT):
                        last = dve.tensor_reduce(soft_max[:, col0 + i:col0 + i + 1], head_banks(h)[i][:, 0:widths[i]],
                                                 AX_X, ALU.max)
                    last.then_inc(at_reduced, 1)
                    dve.wait_ge(at_reduced, n0 + h + 1)
                    dve.tensor_scalar(neg_max[:, col0:col0 + 4], soft_max[:, col0:col0 + 4], -scale, None, ALU.mult)\
                       .then_inc(at_max, 1)
                maxima(0)
                for h in range(heads):
                    if h + 1 < heads:
                        maxima(h + 1)
                    col0 = 4 * (h % 2)
                    dve.wait_ge(at_exp, n0 + h + 1)
                    dve.reciprocal(soft_den[:, col0:col0 + 4], soft_den[:, col0:col0 + 4]).then_inc(at_recip, 1)
                    dve.wait_ge(at_recip, n0 + h + 1)
                    for i in range(TT):
                        part = prob_[:, h % 2, at[i]:at[i] + widths[i]]
                        last = dve.tensor_scalar(part, part, soft_den[:, col0 + i:col0 + i + 1], None, ALU.mult)
                    last.then_inc(at_norm, 1)
                    hi, lo, rows_ = result(kind, h)
                    dve.wait_ge(at_hi, n0 + h + 1)
                    dve.tensor_tensor(lo, head_banks(h)[0][rows_, :], hi.bitcast(F32), ALU.subtract).then_inc(at_out, 1)

            def cross_attention(l):
                for k in range(KT):
                    dve.wait_ge(mem_turned, l * KT + k + 1)
                    dve.tensor_copy(mem_t[:, k, :], A[k % 4][:, 0:N_MEM]).then_inc(mem_out, 1)
                norm(MEMORY[l], mem_t, hi=mem_hi, lo=mem_lo, gain=("mem_norm_g_2", l * KT), tokens=N_MEM)
                c0 = start[f"xkv{l}"][0]
                for n in range(2):
                    read_out("k", c0 + n, [(k_x[:, 2 * n + m, :], M[2 * n + m][:, 0:N_MEM], None) for m in range(2)])
                for n in range(2):
                    read_out("v", c0 + 2 + n, [(v_x[:, :, n * 2 * P:(n + 1) * 2 * P],
                                                M[2 * n][:, :].rearrange("p (t c) -> p t c", t=2), None)])
                norm(XATTN[l], x, gain=("norm_xattn_g_2", l * KT))
                for n in range(2):
                    read_out("q", start[f"xq{l}"][0] + n,
                             [(q_x[:, 2 * n + m, :], M[2 * n + m][:, :], None) for m in range(2)])
                attend(f"x{l}")
                add_residual(f"xo{l}")
                norm(FFN[l], x, gain=("norm_ffn_g_2", l * KT))
                feed_forward(2 + l, "silu")

            norm(MIX[0], x, gain=("norm_mix_g_2", 0))
            y_count = [0]

            def y_slot():
                t = y_count[0]
                if t >= 2:
                    dve.wait_ge(ev_y_hi, t - 1)
                return y[:, t % 2, :]

            def y_split():
                t = y_count[0]
                dve.wait_ge(ev_y_hi, t + 1)
                dve.tensor_tensor(y_lo[:, t, :], y[:, t % 2, :], y_hi[:, t, :].bitcast(F32), ALU.subtract)\
                   .then_inc(ev_y_lo, 1)
                y_count[0] += 1

            def convolve(t):
                u, v = gated[:, t, :], window[:, 0, :]
                link(dve.tensor_scalar(v, u, col("ev_conv_w_2", 8 + t), None, ALU.mult))
                for back in (1, 2):
                    link(dve.scalar_tensor_tensor(v[:, back:], u[:, 0:S - back], col("ev_conv_w_2", (2 - back) * 4 + t),
                                                  v[:, back:], ALU.mult, ALU.add))
                dve.tensor_tensor(y_slot(), g_b[:, t, :], v, ALU.mult).then_inc(ev_y, 1)
                y_split()

            def pool(g):
                width = WINDOWS[g]
                src, span, n = pooled[:, g, :], 1, 0
                while span < width:
                    dst = window[:, n % 2, :]
                    dve.tensor_copy(dst[:, 0:span], src[:, 0:span])
                    link(dve.tensor_tensor(dst[:, span:], src[:, span:], src[:, 0:S - span], ALU.add))
                    src, span, n = dst, span * 2, n + 1
                head = window[:, n % 2, 0:width]
                link(dve.tensor_tensor(head, src[:, 0:width], const[:, C_INV:C_INV + width], ALU.mult))
                dve.scalar_tensor_tensor(pooled[:, g, width:], src[:, width:], 1.0 / width, pooled[:, g, width:],
                                         ALU.mult, ALU.subtract)
                link(dve.tensor_tensor(pooled[:, g, 0:width], head, pooled[:, g, 0:width], ALU.subtract))
                dve.sem_inc(pool_in, 1)

            c0 = start["ev_in"][0]
            for n in range(8):
                bank = [M[2 * (n % 2) + m][:, :] for m in range(2)]
                if n < 4:
                    dst = g_b if n < 2 else g_c
                    read_out("g", c0 + n, [(dst[:, 2 * (n % 2) + m, :], bank[m], None) for m in range(2)])
                elif n < 6:
                    dve.wait_ge(w_used, c0 + n + 3)
                    for m in range(2):
                        t = 2 * (n - 4) + m
                        last = dve.tensor_tensor(gated[:, t, :], g_c[:, t, :], bank[m], ALU.mult)
                    last.then_inc(m_free, 1)
                    split_after(c0 + n, n % 2)
                    dve.wait_ge(m_free, c0 + n + 3)
                    convolve(2 * (n - 4))
                    convolve(2 * (n - 4) + 1)
                else:
                    read_out("xb", c0 + n, [(pooled[:, 2 * (n - 6) + m, :], bank[m], None) for m in range(2)])
                    dve.wait_ge(m_free, c0 + n + 3)
                    pool(2 * (n - 6))
                    pool(2 * (n - 6) + 1)
            for g in range(4):
                dve.wait_ge(pool_out, g + 1)
                dve.tensor_scalar(y_slot(), A[g][:, :], col("ev_pool_scale_2", g), None, ALU.mult).then_inc(ev_y, 1)
                y_split()
            add_residual("ev_out")
            cross_attention(0)

            norm(MIX[1], x, gain=("norm_mix_g_2", KT))
            dve.wait_ge(pos_landed, 16)
            ang, turn, left = angle[RR, :], turns[RR, :], rest[RR, :]
            link(dve.tensor_copy(ang, pos[RR, :]))
            link(dve.tensor_scalar(ang, ang, const[RR, C_FREQ:C_FREQ + 1], None, ALU.mult))
            link(dve.tensor_scalar(turn, ang, 1.0 / TWO_PI, ROUND, ALU.mult, ALU.add))
            link(dve.tensor_scalar(turn, turn, -ROUND, None, ALU.add))
            for n, part in enumerate((TURN_1, TURN_2, TURN_3)):
                link(dve.scalar_tensor_tensor(left, turn, -part, ang if n == 0 else left, ALU.mult, ALU.add))
            dve.tensor_scalar(left, left, -3.1415925, 3.1415925, ALU.max, ALU.min).then_inc(trig_arg, 1)

            c0 = start["od_in"][0]
            for n in range(4):
                dst, factor = (q_m, None) if n < 2 else (k_m, P ** -0.5)
                read_out("qk", c0 + n, [(dst[:, 2 * (n % 2) + m, :], M[2 * (n % 2) + m][:, :], factor) for m in range(2)])
            for n in range(2):
                read_out("v", c0 + 4 + n, [(v_ml[:, 2 * b:2 * b + 2, n * 2 * P:(n + 1) * 2 * P],
                                            M[2 * n + b][:, :].rearrange("p (t c) -> p t c", t=2), None)
                                           for b in range(2)])
            for n in range(2):
                dve.wait_ge(og_exp, 2 * n + 2)
                pass_banks(c0 + 6 + n)
                split_after(c0 + 6 + n, n % 2)
            c0 = start["od_lat"][0]
            for n in range(2):
                read_out("latent", c0 + n, [(latent[:, 2 * n + m, :], M[2 * n + m][:, :], None) for m in range(2)])
            read_out("latent", c0 + 2, [(latent[:, 4, :], M[0][:, :], None), (k_rope[RR, :], M[1][RR, :], None)])
            H4 = slice(0, ML_HEADS)
            dve.wait_ge(w_used, c0 + 3 + 3)
            dve.tensor_scalar(g_i[H4, :], M[2][H4, :], gate_bias[H4, 0:1], None, ALU.add).then_inc(f_in, 1)
            dve.tensor_scalar(g_f[H4, :], M[3][H4, :], gate_bias[H4, 1:2], None, ALU.add).then_inc(f_in, 1)
            dve.wait_ge(f_in, 2)
            pass_banks(c0 + 3)
            split_after(c0 + 3, 1)
            dve.wait_ge(f_log, 1)
            link(dve.tensor_scalar(g_f[H4, :], g_f[H4, :], 0.0, None, ALU.min))
            link(dve.tensor_tensor(g_f[H4, :], g_f[H4, :], g_one[H4, :], ALU.subtract))
            link(dve.memset(g_one[H4, :], 1.0))
            link(dve.tensor_tensor_scan(g_sum[H4, :], g_one[H4, :], g_f[H4, :], 0.0, ALU.mult, ALU.add))
            link(dve.tensor_tensor(g_i[H4, :], g_i[H4, :], g_sum[H4, :], ALU.subtract))
            link(dve.tensor_tensor_scan(g_top[H4, :], g_i[H4, :], g_i[H4, :], 0.0, ALU.max, ALU.max))
            dve.tensor_tensor(g_sum[H4, :], g_sum[H4, :], g_top[H4, :], ALU.add).then_inc(rows_done, 1)
            dve.wait_ge(a_turned, 1)
            dve.tensor_copy(a_col[:, :], A[1][:, 0:16]).then_inc(a_out, 1)
            norm(LATENT_Q, latent[:, 0:3, :], hi=cq_hi, lo=cq_lo, gain=("od_q_norm_g_2", 0))
            norm(LATENT_KV, latent[:, 3:5, :], hi=ckv_hi, lo=ckv_lo, gain=("od_kv_norm_g_2", 0))
            for h in range(ML_HEADS):
                dve.wait_ge(ml_scores, h + 1)
                dve.scalar_tensor_tensor(ml_diag[:, :].rearrange("p (t c) -> p t c", t=TT),
                                         A[3][:, :].rearrange("p (t c) -> p t c", t=TT), -1.0,
                                         const[:, C_CAUSAL_T:C_CAUSAL_T + P].unsqueeze(1).broadcast_to([P, TT, P]),
                                         ALU.mult, ALU.add).then_inc(ml_diag_done, 1)
                dve.wait_ge(ml_w_done, h + 1)
                for bank, at, width in ((A[0], 0, S), (A[1], S, S - P), (A[2], 2 * S - P, S - P)):
                    last = dve.tensor_tensor(ml_sw[:, at:at + width], ml_w[:, at:at + width], bank[:, 0:width], ALU.mult)
                last.then_inc(ml_sw_done, 1)
                dve.wait_ge(ml_abs, h + 1)
                link(dve.tensor_tensor(ml_1[:, :], ml_1[:, :], ml_0[:, :], ALU.max))
                link(dve.reciprocal(ml_1[:, :], ml_1[:, :]))
                link(dve.tensor_tensor(ml_2[:, :], M[1][:, :], ml_1[:, :], ALU.mult))
                dve.tensor_tensor(ml_2[:, :], ml_2[:, :], sig_o[:, h, :], ALU.mult).then_inc(ml_hm, 1)
                dve.wait_ge(ml_rs, h + 1)
                dve.scalar_tensor_tensor(ml_2[:, :], ml_2[:, :], col("od_ml_norm_g_2", h), ml_0[:, :], ALU.mult, ALU.mult)\
                   .then_inc(ml_y, 1)
                dve.wait_ge(ml_hi, h + 1)
                dve.tensor_tensor(h_lo[:, h, :], ml_2[:, :], h_hi[:, h, :].bitcast(F32), ALU.subtract).then_inc(ml_out, 1)
            for n in range(4):
                read_out("q", start["od_uq"][0] + n,
                         [(q_h[0:QK_DIM, 2 * n + m, :], M[2 * (n % 2) + m][0:QK_DIM, :], None) for m in range(2)])
            for n in range(4):
                read_out("k", start["od_ukv"][0] + n,
                         [(k_h[0:NOPE, 2 * n + m, :], M[2 * (n % 2) + m][0:NOPE, :], None) for m in range(2)])
            for n in range(2):
                read_out("v", start["od_uv"][0] + n,
                         [(v_h[:, 2 * b:2 * b + 2, n * 2 * P:(n + 1) * 2 * P],
                           M[2 * n + b][:, :].rearrange("p (t c) -> p t c", t=2), None) for b in range(2)])
            dve.wait_ge(trig_done, 3)
            dve.wait_ge(rope_turned, 1)
            dve.tensor_tensor(rotated[RR, 0, :], A[0][RR, :], sin[RR, :], ALU.mult).then_inc(rope_free, 1)
            dve.wait_ge(rope_free, 1)
            link(dve.tensor_tensor(k_rope[RR, :], k_rope[RR, :], cos[RR, :], ALU.mult))
            dve.tensor_tensor(k_rope[RR, :], k_rope[RR, :], rotated[RR, 0, :], ALU.add).then_inc(rope_k, 1)
            dve.wait_ge(rope_k, 1)
            for h in range(MLA_HEADS):
                dve.wait_ge(rope_turned, h + 2)
                dve.tensor_tensor(rotated[RR, h, :], A[(h + 1) % 4][RR, :], sin[RR, :], ALU.mult).then_inc(rope_free, 1)
            q_rope = q_h[RR, :, :]
            dve.wait_ge(rope_free, MLA_HEADS + 1)
            link(dve.tensor_tensor(q_rope, q_rope, cos[RR, :].unsqueeze(1).broadcast_to([ROPE, MLA_HEADS, S]), ALU.mult))
            dve.tensor_tensor(q_rope, q_rope, rotated[RR, :, :], ALU.add).then_inc(rope_done, 1)
            attend("mla")
            add_residual("od_out")
            cross_attention(1)
            norm(LAST_NORM, x, hi=None, gain=("final_norm_g_2", 0))
            for k in range(KT):
                dve.wait_ge(out_turned, k + 1)
                dve.tensor_copy(x_out[:, :, k * P:(k + 1) * P], A[k % 4][:, :].rearrange("p (t c) -> p t c", t=TT))\
                   .then_inc(out_ready, 1)


_INS = ['x', 'norm1', 'w_in', 'b_gate', 'w_br', 'w_o', 'norm2', 'w_up', 'conv_w', 'conv_b', 'w_down', 'norm_f',
        'mem_2', 'positions_2', 'norm_mix_g_2', 'norm_xattn_g_2', 'mem_norm_g_2', 'xattn_wq_2', 'xattn_wkv_2',
        'xattn_wo_2', 'norm_ffn_g_2', 'ffn_w_gate_up_2', 'ffn_w_down_2', 'ev_w_in_2', 'ev_conv_w_2', 'ev_pool_w_2',
        'ev_pool_scale_2', 'ev_w_out_2', 'od_w_in_2', 'od_gate_bias_2', 'od_ml_norm_g_2', 'od_q_norm_g_2',
        'od_kv_norm_g_2', 'od_w_uq_2', 'od_w_ukv_2', 'od_w_out_2', 'final_norm_g_2']


def kernel(**inputs):
    import concourse.bacc as _bacc
    from concourse.bass_utils import run_bass_kernel_spmd as _run

    nc = _bacc.Bacc("TRN2", target_bir_lowering=False, num_devices=1)
    arrays, dram = {}, {}
    for name in _INS:
        a = np.ascontiguousarray(inputs[name])
        arrays[f"in_{name}"] = a
        dram[name] = nc.dram_tensor(f"in_{name}", a.shape, mybir.dt.from_np(a.dtype), kind="ExternalInput").ap()
    a = shape_constants()
    arrays["in_shape_constants"] = a
    dram["shape_constants"] = nc.dram_tensor("in_shape_constants", a.shape, F32, kind="ExternalInput").ap()
    out = nc.dram_tensor("out_0", (1, S, D), F32, kind="ExternalOutput").ap()
    block_program(nc, dram, out)
    r = _run(nc, [arrays], core_ids=[0])
    return np.array(r.results[0]["out_0"])
```

```python
from contextlib import ExitStack

import numpy as np
import concourse.bass as bass
from concourse import mybir

F32 = mybir.dt.float32
F32R = mybir.dt.float32r
I32 = mybir.dt.int32
ALU = mybir.AluOpType
ACT = mybir.ActivationFunctionType
LOG_EXP = "natural_log_exp_and_others"
AX_X = mybir.AxisListType.X

P = 128
S = 512
D = 1024
KT = D // P
TT = S // P
DEPTH = 2
HD = 64
SLOTS = 4
GROUPS = 3
DIL = (1, 4, 16)
W_B = SLOTS * HD
D_FF = 2816
FT = D_FF // P
HALVES = ((0, 12), (12, 10))
EPS = 1e-6
MASKED = -1e30
HALF = D

VEC_GROUPS = (
    (("norm1", DEPTH * 8), ("norm2", DEPTH * 8), ("norm_f", 8), ("norm_mix_g_2", DEPTH * 8),
     ("norm_xattn_g_2", DEPTH * 8), ("mem_norm_g_2", DEPTH * 8), ("norm_ffn_g_2", DEPTH * 8),
     ("final_norm_g_2", 8)),
    (("b_gate", DEPTH * 16), ("conv_b", DEPTH * FT), ("ev_conv_w_2", 12), ("ev_pool_scale_2", 4),
     ("od_ml_norm_g_2", 4), ("od_q_norm_g_2", 3), ("od_kv_norm_g_2", 2)),
    (("conv_w0", 3 * FT),),
    (("conv_w1", 3 * FT),),
)
N_MEM = 256
ML_HEADS = 4
MLA_HEADS = 8
NOPE, ROPE = 64, 32
QK_DIM = NOPE + ROPE
WINDOWS = (2, 4, 8, 16)
Y_ORDER = (4, 5, 6, 7, 0, 1, 2, 3)
TWO_PI = 2 * np.pi
TURN_1 = 6.28125
TURN_2 = float(np.float32(TWO_PI - TURN_1))
TURN_3 = float(np.float32(TWO_PI - TURN_1 - TURN_2))
ROUND = 1.5 * 2 ** 23
INPUTS = 1 + sum(len(g) for g in VEC_GROUPS)
NORMS = [(KT, True)] * (2 * DEPTH) + [(KT, False)]
for _l in range(DEPTH):
    NORMS += [(KT, True)] + ([(3, True), (2, True)] if _l else []) + [(KT, True)] * 3
NORMS += [(KT, False)]
LAST_NORM = len(NORMS) - 1
MIX, XATTN, MEMORY, FFN = ([5, 9], [6, 12], [7, 13], [8, 14])
LATENT_Q, LATENT_KV = 10, 11
VEC = {}
VEC_ROWS = []
_at = 0
for _g in VEC_GROUPS:
    _row = 0
    for _name, _n in _g:
        VEC[_name] = _at + _row
        _row += _n
    VEC_ROWS.append((_at, _row))
    _at += _row
VEC_COLS = _at

C_IDENT, C_ONES, C_TRI, C_LATER, C_CAUSAL, C_CAUSAL_T, C_ROT, C_FREQ, C_INV, C_BIAS = (
    0, 128, 256, 384, 512, 640, 768, 800, 804, 820)
PLANES = 4
C_COLS = C_BIAS + SLOTS * PLANES * P


def shape_constants():
    c = np.zeros((P, C_COLS), np.float32)
    i, j = np.arange(P)[:, None], np.arange(P)[None, :]
    c[:, C_IDENT:C_IDENT + P] = i == j
    c[:, C_ONES:C_ONES + P] = 1.0
    c[:, C_TRI:C_TRI + P] = i > j
    c[:, C_LATER:C_LATER + P] = j > i
    c[:, C_CAUSAL:C_CAUSAL + P] = np.where(j <= i, 0.0, MASKED)
    c[:, C_CAUSAL_T:C_CAUSAL_T + P] = np.where(i <= j, 0.0, MASKED)
    for a in range(16):
        c[80 + a, C_ROT + a] = -1.0
        c[64 + a, C_ROT + 16 + a] = 1.0
        f = np.float32(10000.0) ** (-np.float32(a) / np.float32(16))
        c[64 + a, C_FREQ] = c[80 + a, C_FREQ] = f
    c[:, C_INV:C_INV + 16] = 1.0 / np.arange(1, 17)
    heads = SLOTS * GROUPS
    slopes = (2.0 ** (-8.0 * np.arange(1, heads + 1) / heads)).astype(np.float32)
    for h in range(SLOTS):
        own = (i - j).astype(np.float32)
        planes = (
            (slopes[h], own, j <= i),
            (slopes[h], own + P, j >= i),
            (slopes[SLOTS + h], own * DIL[1], j <= i),
            (slopes[2 * SLOTS + h], own * DIL[1], (i % 4 == j % 4) & (j <= i)),
        )
        for n, (slope, distance, valid) in enumerate(planes):
            at = C_BIAS + (h * PLANES + n) * P
            c[:, at:at + P] = np.where(valid, -slope * distance, np.float32(MASKED))
    return c


def chunk_starts():
    sizes = []
    for l in range(DEPTH):
        sizes += [(f"qk{l}", 8), (f"v{l}", 4), (f"gate{l}", 8), (f"br{l}", 2), (f"wo{l}", 4)]
        for half, (_, n) in enumerate(HALVES):
            sizes += [(f"up{l}{half}", n), (f"down{l}{half}", 8)]
    for l in range(DEPTH):
        if l == 0:
            sizes += [("ev_in", 8), ("ev_out", 4)]
        else:
            sizes += [("od_in", 8), ("od_lat", 2), ("od_gk", 2), ("od_uq", 4), ("od_ukv", 4), ("od_uv", 2),
                      ("od_out", 4)]
        sizes += [(f"xq{l}", 2), (f"xkv{l}", 4), (f"xo{l}", 4)]
        for half, (_, n) in enumerate(HALVES):
            sizes += [(f"up{2 + l}{half}", n), (f"down{2 + l}{half}", 8)]
    starts, at = {}, 0
    for name, n in sizes:
        starts[name] = (at, n)
        at += n
    return starts, at


def block_program(nc, dram, out):
    start, chunks = chunk_starts()
    size = [HALF] * chunks
    for name, n_each in (("od_uq", 3 * P), ("od_ukv", 2 * P), ("od_uv", 2 * P), ("xo0", 4 * P), ("xo1", 4 * P)):
        for c in range(start[name][0], sum(start[name])):
            size[c] = n_each
    for l in range(2 * DEPTH):
        for half, (_, n) in enumerate(HALVES):
            c0, count = start[f"down{l}{half}"]
            size[c0:c0 + count] = [n // 2 * P] * count

    with ExitStack() as ctx:
        def sb(name, shape, dt=F32, scope=ctx):
            return scope.enter_context(nc.sbuf_tensor(name, shape, dt))

        def sem(name):
            return ctx.enter_context(nc.semaphore(name))

        M = [ctx.enter_context(nc.psum_tensor(f"M{i}", [P, S], F32)) for i in range(4)]
        A = [ctx.enter_context(nc.psum_tensor(f"A{i}", [P, S], F32)) for i in range(4)]

        const = sb("const", [P, C_COLS])
        eps = sb("eps", [P, 1])
        half_pi = sb("half_pi", [P, 1])
        gate_bias = sb("gate_bias", [P, 2])
        soft_max, neg_max, soft_den = sb("soft_max", [P, 8]), sb("neg_max", [P, 8]), sb("soft_den", [P, 8])
        neg_gate = sb("neg_gate", [P, DEPTH * 16])
        vec = sb("vec", [P, VEC_COLS])
        x = sb("x", [P, KT, S])
        h_hi = sb("h_hi", [P, KT, S], F32R)
        h_lo = sb("h_lo", [P, KT, S], F32R)
        stage = sb("stage", [P, 2, HALF])
        w_hi = sb("w_hi", [P, 2, 2 * HALF], F32R)
        w_lo = sb("w_lo", [P, 2, 2 * HALF], F32R)
        ident = const[:, C_IDENT:C_IDENT + P]
        ones = const[:, C_ONES:C_ONES + P]
        tri = const[:, C_TRI:C_TRI + P]
        later_mask = const[:, C_LATER:C_LATER + P]
        bias = const[:, C_BIAS:].rearrange("p (h n c) -> p h n c", h=SLOTS, n=PLANES)

        with ExitStack() as scope:
            x_tok = sb("x_tok", [P, TT, D], scope=scope)
            rows = sb("rows", [P, len(VEC_ROWS), P], scope=scope)
        with ExitStack() as scope:
            qk_a = sb("qk_a", [P, 12, S], scope=scope)
            qk_b = sb("qk_b", [P, 4, S], scope=scope)
            v_a = sb("v_a", [P, TT, GROUPS * SLOTS // 2, 3, HD], scope=scope)
            v_b = sb("v_b", [P, TT, W_B], scope=scope)
            gate = sb("gate", [P, 2 * KT, S], scope=scope)
            o_a = sb("o_a", [P, 2, S], scope=scope)
            prob = sb("prob", [P, PLANES, S], scope=scope)
            top = sb("top", [P, GROUPS, S], scope=scope)
            top_all = sb("top_all", [P, S], scope=scope)
            row_max = sb("row_max", [P, 16], scope=scope)
        with ExitStack() as scope:
            o_hi = sb("o_hi", [P, 4, S], F32R, scope=scope)
            o_lo = sb("o_lo", [P, 4, S], F32R, scope=scope)
        with ExitStack() as scope:
            hid_hi = sb("hid_hi", [P, 12, S], F32R, scope=scope)
            hid_lo = sb("hid_lo", [P, 12, S], F32R, scope=scope)
            conv = sb("conv", [P, 2, S], scope=scope)
            acted = sb("acted", [P, 2, S], scope=scope)
            hid = sb("hid", [P, 2, S], scope=scope)
            square = sb("square", [P, 2, S], scope=scope)
            normed = sb("normed", [P, 2, S], scope=scope)
            square_sum = sb("square_sum", [P, S], scope=scope)
            rstd = sb("rstd", [P, S], scope=scope)
        pads = []

        def lay(*items):
            made, at = [], 0
            with ExitStack() as scope:
                for kib, name, shape, dt in items:
                    if kib * 256 > at:
                        pads.append(sb(f"gap{len(pads)}", [P, kib * 256 - at], scope=scope))
                        at = kib * 256
                    made.append(sb(name, [P, *shape], dt, scope=scope))
                    at += int(np.prod(shape))
            return made

        g_c, gated, pooled, y_hi, y, window, pool_w, y_lo = lay(
            (8, "g_c", [4, S], F32), (16, "gated", [4, S], F32),
            (24, "pooled", [4, S], F32), (32, "y_hi", [KT, S], F32R),
            (48, "y", [2, S], F32), (52, "window", [2, S], F32), (56, "pool_w", [4, P], F32),
            (72, "y_lo", [KT, S], F32R))
        mem_t, mem_hi, mem_lo, k_x, v_x, q_x, x_prob, x_turned, mem_tok = lay(
            (8, "mem_t", [KT, N_MEM], F32),
            (16, "mem_hi", [KT, N_MEM], F32R), (24, "mem_lo", [KT, N_MEM], F32R),
            (32, "k_x", [4, N_MEM], F32), (36, "v_x", [N_MEM // P, S], F32), (40, "q_x", [4, S], F32),
            (72, "x_prob", [2, 4 * N_MEM], F32), (80, "x_turned", [2, 2 * S], F32),
            (96, "mem_tok", [N_MEM // P, D], F32))
        xo_hi, xo_lo = lay((0, "xo_hi", [4, S], F32R), (8, "xo_lo", [4, S], F32R))
        (cq_hi, cq_lo, ckv_hi, ckv_lo, k_rope, cos, sin, latent, g_i, g_f, g_sum, g_top, g_one, a_col,
         ml_w, ml_sw, ml_diag, ml_0, ml_1, ml_2, ml_3, ml_floor, q_m, k_m, v_ml, sig_o) = lay(
            (0, "cq_hi", [3, S], F32R), (6, "cq_lo", [3, S], F32R), (12, "ckv_hi", [2, S], F32R),
            (16, "ckv_lo", [2, S], F32R), (20, "k_rope", [S], F32), (22, "cos", [S], F32), (24, "sin", [S], F32),
            (26, "latent", [5, S], F32), (36, "g_i", [S], F32), (38, "g_f", [S], F32), (40, "g_sum", [S], F32),
            (42, "g_top", [S], F32), (44, "g_one", [S], F32), (46, "a_col", [16], F32),
            (47, "ml_w", [1280], F32), (52, "ml_sw", [1280], F32), (57, "ml_diag", [S], F32),
            (60, "ml_0", [S], F32), (62, "ml_1", [S], F32), (64, "ml_2", [S], F32), (66, "ml_3", [S], F32),
            (68, "ml_floor", [2, S], F32),
            (72, "q_m", [4, S], F32), (80, "k_m", [4, S], F32), (88, "v_ml", [TT, S], F32),
            (96, "sig_o", [4, S], F32))
        q_h, v_h, m_prob, m_turned, k_h, rotated = lay(
            (26, "q_h", [MLA_HEADS, S], F32), (42, "v_h", [TT, S], F32), (50, "m_prob", [2, 1280], F32),
            (60, "m_turned", [2, 1280], F32), (72, "k_h", [MLA_HEADS, S], F32), (88, "rotated", [MLA_HEADS, S], F32))
        pos, angle, turns, rest, rest_abs = lay(
            (47, "pos", [S], I32), (49, "angle", [S], F32), (51, "turns", [S], F32), (53, "rest", [S], F32),
            (55, "rest_abs", [S], F32))
        RR = slice(NOPE, QK_DIM)
        with ExitStack() as scope:
            x_out = sb("x_out", [P, TT, D], scope=scope)
        o_b = v_a[:, :, :, :, :].rearrange("p t a b c -> p (t a b c)")[:, 0:2 * S].rearrange("p (n c) -> p n c", n=2)
        merged = prob

        ST = [0, S, 2 * S - P, 3 * S - 3 * P]
        ST_N = [S - P * kb for kb in range(TT)]
        prob_flat = prob[:, :, :].rearrange("p n c -> p (n c)")
        log_one = prob_flat[:, 0:1280]
        log_sig = top[:, :, :].rearrange("p n c -> p (n c)")[:, 0:1280]
        log_stay = qk_a[:, 8:11, :].rearrange("p n c -> p (n c)")[:, 0:1280]

        landed = [sem("part0_landed"), sem("part1_landed")]
        w_hi_done, w_lo_done = sem("w_hi_done"), sem("w_lo_done")
        w_used = sem("w_used")
        m_free = sem("m_free")
        tokens_landed, inputs_landed, bias_landed = sem("tokens_landed"), sem("inputs_landed"), sem("bias_landed")
        turned, turned_out = sem("turned"), sem("turned_out")
        ones_set, consts_set = sem("ones_set"), sem("consts_set")
        square_done, square_added, spread_done, root_done, rstd_done = (
            sem("square_done"), sem("square_added"), sem("spread_done"), sem("root_done"), sem("rstd_done"))
        normed_done, h_hi_done, h_lo_done = sem("normed_done"), sem("h_hi_done"), sem("h_lo_done")
        scores_done, plane_biased, max_a, max_b, max_done, shifted = (
            sem("scores_done"), sem("plane_biased"), sem("max_a"), sem("max_b"), sem("max_done"), sem("shifted"))
        max_spread, max_copied, exp_done, turned_plane, plane_back, pv_done = (
            sem("max_spread"), sem("max_copied"), sem("exp_done"), sem("turned_plane"), sem("plane_back"), sem("pv_done"))
        top1, top2, top_shift, weight_done, mix_step, a_free, o_done = (
            sem("top1"), sem("top2"), sem("top_shift"), sem("weight_done"), sem("mix_step"), sem("a_free"), sem("o_done"))
        z_done, st_act, log_done, st_dve, stay_done, later_done, st_arg, st_exp, st_prob, st_pv = (
            sem("z_done"), sem("st_act"), sem("log_done"), sem("st_dve"), sem("stay_done"), sem("later_done"),
            sem("st_arg"), sem("st_exp"), sem("st_prob"), sem("st_pv"))
        gate_exp, gate_ln, gate_done = sem("gate_exp"), sem("gate_ln"), sem("gate_done")
        den_step, den_done = sem("den_step"), sem("den_done")
        o_hi_done, o_lo_done = sem("o_hi_done"), sem("o_lo_done")
        br_full, br_free, merged_done, mg_hi_done, mg_lo_done = (
            sem("br_full"), sem("br_free"), sem("merged_done"), sem("mg_hi_done"), sem("mg_lo_done"))
        tap_done, conv_step, conv_done, acted_done, hid_hi_done, hid_lo_done = (
            sem("tap_done"), sem("conv_step"), sem("conv_done"), sem("acted_done"), sem("hid_hi_done"), sem("hid_lo_done"))
        out_turned, out_ready, out_stored = sem("out_turned"), sem("out_ready"), sem("out_stored")
        pool_landed, mem_landed, pos_landed = sem("pool_landed"), sem("mem_landed"), sem("pos_landed")
        pool_in, pool_out, ev_y, ev_y_hi, ev_y_lo = (
            sem("pool_in"), sem("pool_out"), sem("ev_y"), sem("ev_y_hi"), sem("ev_y_lo"))
        mem_turned, mem_out = sem("mem_turned"), sem("mem_out")
        at_scores, at_reduced, at_max, at_exp, at_recip, at_norm, at_turned, at_back, at_pv, at_hi, at_out = (
            sem("at_scores"), sem("at_reduced"), sem("at_max"), sem("at_exp"), sem("at_recip"), sem("at_norm"),
            sem("at_turned"), sem("at_back"), sem("at_pv"), sem("at_hi"), sem("at_out"))
        og_exp, og_ln, og_done = sem("og_exp"), sem("og_ln"), sem("og_done")
        trig_arg, trig_done, rope_turned, rope_free, rope_k, rope_spread, rope_done = (
            sem("trig_arg"), sem("trig_done"), sem("rope_turned"), sem("rope_free"), sem("rope_k"),
            sem("rope_spread"), sem("rope_done"))
        f_in, f_step, f_log, rows_done, a_turned, a_out = (
            sem("f_in"), sem("f_step"), sem("f_log"), sem("rows_done"), sem("a_turned"), sem("a_out"))
        (ml_scores, ml_diag_done, ml_w_done, ml_sw_done, ml_nd, ml_abs, ml_hm, ml_sq, ml_ss, ml_ln, ml_rs, ml_y,
         ml_hi, ml_out, ml_den, ml_inv) = (
            sem("ml_scores"), sem("ml_diag_done"), sem("ml_w_done"), sem("ml_sw_done"), sem("ml_nd"),
            sem("ml_abs"), sem("ml_hm"), sem("ml_sq"), sem("ml_ss"), sem("ml_ln"), sem("ml_rs"), sem("ml_y"),
            sem("ml_hi"), sem("ml_out"), sem("ml_den"), sem("ml_inv"))
        chain = sem("chain")

        AT0 = {"x0": 0, "mla": 4, "x1": 12}

        def attention(kind):
            if kind == "mla":
                widths = [(i + 1) * P for i in range(TT)]
                return (MLA_HEADS, TT, widths, [0, P, 3 * P, 6 * P], ST, [kt * P for kt in range(TT)],
                        m_prob, m_turned, QK_DIM ** -0.5)
            return (4, N_MEM // P, [N_MEM] * TT, [i * N_MEM for i in range(TT)], [0, S], [0, 0],
                    x_prob, x_turned, P ** -0.5)

        def head_banks(h):
            return A if h % 2 == 0 else M

        def result(kind, h):
            if kind == "mla":
                lo = (h % 2) * HD
                return h_hi[lo:lo + HD, 4 + h // 2, :], h_lo[lo:lo + HD, 4 + h // 2, :], slice(lo, lo + HD)
            return xo_hi[:, h, :], xo_lo[:, h, :], slice(0, P)

        def col(name, n=0):
            return vec[:, VEC[name] + n:VEC[name] + n + 1]

        def col_at(name, n):
            return vec[:, bass.ds(n + VEC[name], 1)]

        def over(t, g):
            return t if g == 0 else t.rearrange("p (r l) -> p l r", r=DIL[1])

        def nat(t, g):
            return t if g == 0 else t.rearrange("p (l r) -> p l r", r=DIL[1])

        def by_residue(t, g):
            return t if g == 0 else t.rearrange("p (l r) -> p r l", r=DIL[1])

        def as_residue(t, g):
            return t if g == 0 else t.rearrange("p (r l) -> p r l", r=DIL[1])

        def split_norm(n):
            return sum(kt for kt, split in NORMS[:n] if split)

        def norm_tiles(n):
            return sum(kt for kt, _ in NORMS[:n])

        def additions(n):
            return sum(kt + 1 for kt, _ in NORMS[:n])

        def up_counts(l, half):
            return l * FT + HALVES[half][0]

        block = ctx.enter_context(nc.Block())

        @block.sync
        def _(sp):
            def load(c, part0, part1, dst0, dst1):
                for n, (src, dst) in enumerate(((part0, dst0), (part1, dst1))):
                    if not (isinstance(c, int) and c == 0):
                        sp.wait_ge(w_lo_done, c * 2 - 1 + n)
                    sp.dma_start(dst, src).then_inc(landed[n], 16)

            def halves(k, n):
                return [stage[:, part, 0:k * n].rearrange("p (k n) -> p k n", n=n) for part in range(2)]

            def by_tile(w):
                return w.rearrange("(k p) (m c) -> m p k c", p=P, c=P)

            def load_tiles(c, w, m, k=KT):
                load(c, w[m], w[m + 1], *halves(k, P))

            def load_wide(c, w, m):
                v = w.rearrange("(k p) (m c) -> m p k c", p=P, c=2 * P)[m]
                load(c, v[:, 0:4, :], v[:, 4:8, :], *halves(4, 2 * P))

            def feed_forward(l, w_up, w_down):
                up, down = by_tile(w_up), by_tile(w_down)
                for half, (f0, n) in enumerate(HALVES):
                    c0 = start[f"up{l}{half}"][0]
                    with sp.Fori(0, n // 2) as i:
                        for s in range(2):
                            load(i * 2 + (c0 + s), up[i * 2 + (f0 + s)], up[i * 2 + (f0 + s + FT)],
                                 *halves(KT, P))
                    c0 = start[f"down{l}{half}"][0]
                    k = n // 2
                    with sp.Fori(0, KT // 2) as i:
                        for s in range(2):
                            tile = down[i * 2 + s]
                            load(i * 2 + (c0 + s), tile[:, f0:f0 + k, :], tile[:, f0 + k:f0 + n, :],
                                 *halves(k, P))

            sources = dict(dram)
            for l in range(DEPTH):
                sources[f"conv_w{l}"] = dram["conv_w"][l]
            sp.dma_start(const[:, 0:C_BIAS], dram["shape_constants"][:, 0:C_BIAS]).then_inc(tokens_landed, 16)
            for j in range(TT):
                sp.dma_start(x_tok[:, j, :], dram["x"][0, j * P:(j + 1) * P, :]).then_inc(tokens_landed, 16)
            for g, group in enumerate(VEC_GROUPS):
                row = 0
                for name, n in group:
                    a = sources[name]
                    flat = {1: "(r c) -> r c", 2: "a (r c) -> (a r) c"}
                    src = a.rearrange("a b (r c) -> (a b r) c", c=P) if len(a.shape) == 3 else \
                        a.rearrange(flat[len(a.shape)], c=P)
                    sp.dma_start(rows[row:row + n, g, :], src).then_inc(inputs_landed, 16)
                    row += n
            sp.dma_start(gate_bias[0:ML_HEADS, :], dram["od_gate_bias_2"][0].rearrange("(a p) -> p a", a=2),
                         allow_slow_non_contiguous=True).then_inc(inputs_landed, 16)

            for l in range(DEPTH):
                w = dram["w_in"][l]
                tiles = by_tile(w)
                c0 = start[f"qk{l}"][0]
                for n, m in enumerate((0, 2, 4, 6, 8, 10, 18, 20)):
                    load_tiles(c0 + n, tiles, m)
                    if l == 0 and n == 1:
                        sp.dma_start(const[:, C_BIAS:], dram["shape_constants"][:, C_BIAS:]).then_inc(bias_landed, 16)
                c0 = start[f"v{l}"][0]
                for n, m in enumerate((6, 7, 8, 11)):
                    load_wide(c0 + n, w, m)
                c0 = start[f"gate{l}"][0]
                with sp.Fori(0, 4) as i:
                    for s in range(2):
                        load(i * 2 + (c0 + s), tiles[i * 4 + (24 + 2 * s)], tiles[i * 4 + (25 + 2 * s)],
                             *halves(KT, P))
                c0 = start[f"br{l}"][0]
                w = dram["w_br"][l].rearrange("(k p) (m c) -> m p k c", p=P, c=S)
                for n in range(2):
                    load(c0 + n, w[n][:, 0:2, :], w[n][:, 2:4, :], *halves(2, S))
                c0 = start[f"wo{l}"][0]
                tiles = by_tile(dram["w_o"][l])
                with sp.Fori(0, 2) as i:
                    for s in range(2):
                        load(i * 2 + (c0 + s), tiles[i * 4 + 2 * s], tiles[i * 4 + (2 * s + 1)],
                             *halves(KT, P))
                feed_forward(l, dram["w_up"][l], dram["w_down"][l])

            def load_memory():
                for t in range(N_MEM // P):
                    sp.dma_start(mem_tok[:, t, :], dram["mem_2"][0, t * P:(t + 1) * P, :]).then_inc(mem_landed, 16)

            def cross_attention(l):
                for n in range(2):
                    load_tiles(start[f"xq{l}"][0] + n, by_tile(dram["xattn_wq_2"][l]), 2 * n)
                w = dram["xattn_wkv_2"][l]
                c0 = start[f"xkv{l}"][0]
                for n in range(2):
                    load_tiles(c0 + n, by_tile(w), 2 * n)
                for n in range(2):
                    load_wide(c0 + 2 + n, w, 2 + n)
                for n in range(4):
                    load_tiles(start[f"xo{l}"][0] + n, by_tile(dram["xattn_wo_2"][l]), 2 * n, k=4)
                feed_forward(2 + l, dram["ffn_w_gate_up_2"][l], dram["ffn_w_down_2"][l])

            tiles = by_tile(dram["ev_w_in_2"][0])
            for n in range(8):
                load_tiles(start["ev_in"][0] + n, tiles, 2 * (6, 7, 2, 3, 4, 5, 0, 1)[n])
                if n == 1:
                    sp.wait_ge(normed_done, norm_tiles(MIX[0]) + KT)
                    sp.dma_start(pool_w[:, :, :], dram["ev_pool_w_2"][0].rearrange("g c d -> c g d"))\
                      .then_inc(pool_landed, 16)
                    load_memory()
            for n in range(4):
                load_tiles(start["ev_out"][0] + n, by_tile(dram["ev_w_out_2"][0]), 2 * n)
            cross_attention(0)
            w = dram["od_w_in_2"][0]
            tiles = by_tile(w[:, 0:4 * S])
            c0 = start["od_in"][0]
            for n in range(4):
                load_tiles(c0 + n, tiles, 2 * n)
                if n == 1:
                    sp.wait_ge(normed_done, norm_tiles(MIX[1]) + KT)
                    sp.dma_start(pos[RR, :], dram["positions_2"].broadcast_to([ROPE, S])).then_inc(pos_landed, 16)
            for n in range(2):
                load_wide(c0 + 4 + n, w[:, 0:4 * S], 4 + n)
            for n in range(2):
                load_tiles(c0 + 6 + n, tiles, 12 + 2 * n)

            def columns(first, n=P):
                return w[:, first:first + n].rearrange("(k p) c -> p k c", p=P)
            lat = 4 * S + 2 * ML_HEADS
            blocks = [columns(lat + n * P) for n in range(5)] + [
                columns(lat + 5 * P + ROPE - QK_DIM, QK_DIM), columns(4 * S), columns(4 * S + ML_HEADS)]
            for n in range(4):
                c = start["od_lat"][0] + n
                dst = halves(KT, P)
                if n == 2:
                    dst[1] = dst[1][:, :, 0:QK_DIM]
                load(c, blocks[2 * n], blocks[2 * n + 1], *dst)
            uq = dram["od_w_uq_2"][0].rearrange("(k p) (h c) -> h p k c", p=P, c=QK_DIM)
            for n in range(4):
                load(start["od_uq"][0] + n, uq[2 * n], uq[2 * n + 1], *[d[:, :, 0:QK_DIM] for d in halves(3, P)])
            for n in range(4):
                load_tiles(start["od_ukv"][0] + n, by_tile(dram["od_w_ukv_2"][0]), 2 * n, k=2)
            uv = dram["od_w_ukv_2"][0].rearrange("(k p) (h c) -> k p h c", p=P, c=P)[:, :, :, NOPE:P]
            for n in range(2):
                load(start["od_uv"][0] + n, uv[0][:, 4 * n:4 * n + 4, :], uv[1][:, 4 * n:4 * n + 4, :],
                     *halves(4, HD))
            for n in range(4):
                load_tiles(start["od_out"][0] + n, by_tile(dram["od_w_out_2"][0]), 2 * n)
                if n == 2:
                    sp.wait_ge(rope_done, MLA_HEADS)
                    load_memory()
            cross_attention(1)
            sp.wait_ge(out_ready, KT)
            for t in range(TT):
                sp.dma_start(out[0, t * P:(t + 1) * P, :], x_out[:, t, :]).then_inc(out_stored, 16)
            sp.wait_ge(out_stored, 16 * TT)

        @block.tensor
        def _(pe):
            def product(bank, lhs, rhs, k):
                last = None
                for n in range(k):
                    (a_hi, a_lo), (b_hi, b_lo) = lhs(n), rhs(n)
                    pe.matmul(bank, a_hi, b_hi, start=(n == 0), stop=False)
                    pe.matmul(bank, a_hi, b_lo, start=False, stop=False)
                    last = pe.matmul(bank, a_lo, b_hi, start=False, stop=(n == k - 1))
                return last

            def weight(s, m, width=P):

                def at(k):
                    o = m * HALF + k * P
                    return w_hi[:, s, o:o + width], w_lo[:, s, o:o + width]
                return at

            def operand(hi, lo, n=S):
                def at(k):
                    return hi[:, k, 0:n], lo[:, k, 0:n]
                return at

            hidden = operand(hid_hi, hid_lo)
            normal = operand(h_hi, h_lo)

            def chunk_in(c):
                pe.wait_ge(w_lo_done, c * 2 + 2)
                pe.wait_ge(m_free, c + 1)

            def two_tiles(c, s, rhs, k, widths=(P, P), n=S):
                chunk_in(c)
                for m in range(2):
                    last = product(M[2 * s + m][0:widths[m], 0:n], weight(s, m, widths[m]), rhs, k)
                last.then_inc(w_used, 1)

            def token_major(c, s, hi, lo, k, tiles, pick=None):
                chunk_in(c)
                for t in range(tiles):
                    def tokens(n):
                        if pick is None:
                            return hi[:, n, t * P:(t + 1) * P], lo[:, n, t * P:(t + 1) * P]
                        return pick(hi[:, n, :], t), pick(lo[:, n, :], t)

                    def columns(n):
                        o = (n // (k // 2)) * HALF + (n % (k // 2)) * 2 * P
                        return w_hi[:, s, o:o + 2 * P], w_lo[:, s, o:o + 2 * P]
                    half = (t % 2) * 2 * P
                    last = product(M[2 * s + t // 2][:, half:half + 2 * P], tokens, columns, k)
                last.then_inc(w_used, 1)

            def norm(n, tokens=S):
                pe.wait_ge(square_added, additions(n + 1))
                pe.matmul(A[0][:, 0:tokens], ones, square_sum[:, 0:tokens], start=True, stop=True)\
                  .then_inc(spread_done, 1)

            def tiles_of(n_norm):
                return h_lo_done, split_norm(n_norm)

            def first_tiles(c, s, rhs, split, n=S, order=range(KT)):
                chunk_in(c)
                for j, k in enumerate(order):
                    pe.wait_ge(split[0], split[1] + j + 1)
                    b_hi, b_lo = rhs(k)
                    for m in range(2):
                        bank = M[2 * s + m][:, 0:n]
                        a_hi, a_lo = weight(s, m)(k)
                        pe.matmul(bank, a_hi, b_hi, start=(j == 0), stop=False)
                        pe.matmul(bank, a_hi, b_lo, start=False, stop=False)
                        last = pe.matmul(bank, a_lo, b_hi, start=False, stop=(j == KT - 1))
                last.then_inc(w_used, 1)

            def normed_tiles(name, n_norm):
                c0, n = start[name]
                first_tiles(c0, 0, normal, tiles_of(n_norm))
                two_tiles(c0 + 1, 1, normal, KT)
                with pe.Fori(1, n // 2) as i:
                    for s in range(2):
                        two_tiles(i * 2 + (c0 + s), s, normal, KT)

            def feed_forward(l, n_norm):
                for half, (f0, n) in enumerate(HALVES):
                    c0 = start[f"up{l}{half}"][0]
                    if half == 0:
                        normed_tiles(f"up{l}0", n_norm)
                    else:
                        with pe.Fori(0, n // 2) as i:
                            for s in range(2):
                                two_tiles(i * 2 + (c0 + s), s, normal, KT)
                    c0 = start[f"down{l}{half}"][0]

                    def down_weight(s):
                        def at(k):
                            o = (k // (n // 2)) * HALF + (k % (n // 2)) * P
                            return w_hi[:, s, o:o + P], w_lo[:, s, o:o + P]
                        return at

                    def hidden_as_split(k):
                        pe.wait_ge(hid_lo_done, up_counts(l, half) + k + 1)
                        return hidden(k)
                    chunk_in(c0)
                    product(M[0][:, :], down_weight(0), hidden_as_split, n).then_inc(w_used, 1)
                    chunk_in(c0 + 1)
                    product(M[2][:, :], down_weight(1), hidden, n).then_inc(w_used, 1)
                    with pe.Fori(1, KT // 2) as i:
                        for s in range(2):
                            chunk_in(i * 2 + (c0 + s))
                            product(M[2 * s][:, :], down_weight(s), hidden, n).then_inc(w_used, 1)

            def mixture_head(l, h):
                n = l * SLOTS + h
                lo = (h % 2) * HD
                q = [qk_a[lo:lo + HD, 2 * g + h // 2, :] for g in range(GROUPS)]
                k = [qk_a[lo:lo + HD, 6 + 2 * g + h // 2, :] for g in range(GROUPS)]
                blocks = [(0, 0, b, b) for b in range(TT)] + [(1, 0, b, b - 1) for b in range(1, TT)]
                blocks += [(g + 1, g, b, b) for g in (1, 2) for b in range(TT)]
                pe.wait_ge(a_free, l * 2 * SLOTS + h + 1)
                for plane, g, qb, kb in blocks:
                    last = pe.matmul(A[plane][:, qb * P:(qb + 1) * P], q[g][:, qb * P:(qb + 1) * P],
                                     k[g][:, kb * P:(kb + 1) * P], start=True, stop=True)
                last.then_inc(scores_done, 1)
                gate_tile(l, h, 0)
                pe.wait_ge(max_done, n + 1)
                for g, at in enumerate((0, 8, 12)):
                    for b in range(TT):
                        last = pe.matmul(A[g][:, b * P:(b + 1) * P],
                                         row_max[:, at + b:at + b + 1].broadcast_to([P, P]), ident,
                                         start=True, stop=True)
                last.then_inc(max_spread, 1)
                gate_tile(l, h, 1)
                pe.wait_ge(exp_done, n + 1)
                pe.wait_ge(max_copied, GROUPS * (n + 1))
                for plane in range(PLANES):
                    for b in range(1 if plane == 1 else 0, TT):
                        last = pe.transpose(A[plane][:, b * P:(b + 1) * P],
                                            prob[:, plane, b * P:(b + 1) * P], ident)
                    last.then_inc(turned_plane, 1)
                for g in range(GROUPS):
                    pair = g * SLOTS // 2 + h // 2
                    pe.wait_ge(plane_back, PLANES * n + (2 if g == 0 else g + 2))
                    for b in range(TT):
                        keys = [(0, b), (1, b - 1)] if g == 0 else [(g + 1, b)]
                        keys = [(plane, kb) for plane, kb in keys if kb >= 0]
                        for j, (plane, kb) in enumerate(keys):
                            last = pe.matmul(A[g][:, b * P:(b + 1) * P],
                                             v_a[:, kb, pair, h % 2:h % 2 + 2, :].rearrange("p a c -> p (a c)"),
                                             prob[:, plane, b * P:(b + 1) * P],
                                             start=(j == 0), stop=(j == len(keys) - 1))
                last.then_inc(pv_done, 1)

            where = [(A[0], 0), (A[1], 0), (A[2], 0), (A[2], 2 * P)]

            def stick_scores(l, h):
                lo = (h % 2) * HD
                q, k = qk_b[lo:lo + HD, h // 2, :], qk_b[lo:lo + HD, 2 + h // 2, :]
                for kb, (bank, at) in enumerate(where):
                    last = pe.matmul(bank[:, at:at + ST_N[kb]], k[:, kb * P:(kb + 1) * P], q[:, kb * P:],
                                     start=True, stop=True)
                last.then_inc(z_done, 1)

            def stick_head(l, h):
                n = l * SLOTS + h
                lo = (h % 2) * HD
                if h == 0:
                    pe.wait_ge(a_free, l * 2 * SLOTS + SLOTS + 1)
                    stick_scores(l, 0)
                gate_tile(l, SLOTS + h, 0)
                pe.wait_ge(stay_done, n + 1)
                for kb, (bank, at) in enumerate(where):
                    for jb in range(kb, TT):
                        skip = (jb - kb) * P
                        last = pe.matmul(bank[:, at + skip:at + ST_N[kb]], tri if jb == kb else ones,
                                         log_stay[:, ST[jb]:ST[jb] + ST_N[jb]],
                                         start=(jb == kb), stop=(jb == TT - 1))
                last.then_inc(later_done, 1)
                gate_tile(l, SLOTS + h, 1)
                if h + 1 < SLOTS:
                    pe.wait_ge(st_arg, n + 1)
                    stick_scores(l, h + 1)
                pe.wait_ge(a_free, l * 2 * SLOTS + SLOTS + h + 1)
                pe.wait_ge(st_prob, n + 1)
                for kb in range(TT):
                    last = pe.matmul(A[3][lo:lo + HD, kb * P:], v_b[:, kb, h * HD:(h + 1) * HD],
                                     log_one[:, ST[kb]:ST[kb] + ST_N[kb]], start=(kb == 0), stop=(kb == TT - 1))
                last.then_inc(st_pv, 1)

            def gate_tile(l, j, m):
                c = start[f"gate{l}"][0] + j
                if m == 0:
                    chunk_in(c)
                last = product(M[2 * (c % 2) + m][:, :], weight(c % 2, m), normal, KT)
                if m == 1:
                    last.then_inc(w_used, 1)

            pe.sem_inc(w_used, 2)
            pe.wait_ge(tokens_landed, 16 * (1 + TT))
            for k in range(KT):
                if k >= 4:
                    pe.wait_ge(turned_out, k - 3)
                for j in range(TT):
                    last = pe.transpose(A[k % 4][:, j * P:(j + 1) * P], x_tok[:, j, k * P:(k + 1) * P], ident)
                last.then_inc(turned, 1)
            pe.wait_ge(inputs_landed, 16 * INPUTS)
            pe.wait_ge(turned_out, KT - 2)
            for g, (at, n) in enumerate(VEC_ROWS):
                last = pe.transpose(A[1][:, at:at + n], rows[0:n, g, :], ident[0:n, 0:n])
            last.then_inc(turned, 1)

            for l in range(DEPTH):
                norm(2 * l)
                normed_tiles(f"qk{l}", 2 * l)
                c0 = start[f"v{l}"][0]
                for g in range(GROUPS):
                    def residue_tile(t, n, g=g):
                        if g == 0:
                            return t[:, n * P:(n + 1) * P]
                        r = by_residue(t, g)
                        return r[:, n, :]
                    token_major(c0 + g, g % 2, h_hi, h_lo, KT, TT, residue_tile)
                token_major(c0 + 3, 1, h_hi, h_lo, KT, TT)
                pe.wait_ge(m_free, c0 + 4 + 2)
                pe.wait_ge(ones_set, l + 1)
                for h in range(SLOTS):
                    mixture_head(l, h)
                for h in range(SLOTS):
                    stick_head(l, h)
                c0 = start[f"br{l}"][0]
                pe.wait_ge(o_lo_done, 2 * l + 2)
                for n in range(2):
                    chunk_in(c0 + n) if n == 0 else pe.wait_ge(w_lo_done, 2 * (c0 + n) + 2)
                    for m in range(4):
                        j = n * 4 + m
                        pe.wait_ge(br_free, l * KT + j + 1)
                        if j == 1:
                            pe.wait_ge(m_free, c0 + 2)
                        for ab in range(2):
                            def branch(k):
                                o = ab * HALF + k * S + m * P
                                return w_hi[:, n, o:o + P], w_lo[:, n, o:o + P]

                            def mixed(k):
                                return o_hi[:, 2 * ab + k, :], o_lo[:, 2 * ab + k, :]
                            last = product(M[2 * (j % 2) + ab][:, :], branch, mixed, 2)
                        last.then_inc(w_used if m == 3 else br_full, 1)
                c0 = start[f"wo{l}"][0]
                pe.wait_ge(br_free, l * KT + KT + 1)
                first_tiles(c0, 0, normal, (mg_lo_done, KT * l))
                two_tiles(c0 + 1, 1, normal, KT)
                with pe.Fori(1, 2) as i:
                    for s in range(2):
                        two_tiles(i * 2 + (c0 + s), s, normal, KT)
                norm(2 * l + 1)
                feed_forward(l, 2 * l + 1)
            norm(2 * DEPTH)

            def looped_tiles(name, rhs, k):
                c0, n = start[name]
                with pe.Fori(0, n // 2) as i:
                    for s in range(2):
                        two_tiles(i * 2 + (c0 + s), s, rhs, k)

            def attend(kind, scores, values):
                heads, key_tiles, widths, at, turned_at, first_q, prob_, turned_, _ = attention(kind)
                n0 = AT0[kind]

                def score(h):
                    for i in range(TT - 1, 0, -1):
                        scores(h, i, head_banks(h)[i])
                    if h >= 2:
                        pe.wait_ge(at_out, n0 + h - 1)
                    scores(h, 0, head_banks(h)[0]).then_inc(at_scores, 1)
                score(0)
                for h in range(heads):
                    if h + 1 < heads:
                        score(h + 1)
                    bank = head_banks(h)
                    pe.wait_ge(at_norm, n0 + h + 1)
                    for kt in range(key_tiles):
                        for i in range(first_q[kt] // P, TT):
                            last = pe.transpose(bank[kt][:, i * P:(i + 1) * P],
                                                prob_[:, h % 2, at[i] + kt * P:at[i] + (kt + 1) * P], ident)
                    last.then_inc(at_turned, 1)
                    pe.wait_ge(at_back, n0 + h + 1)
                    rows_ = result(kind, h)[2]
                    for kt in range(key_tiles):
                        last = pe.matmul(bank[0][rows_, first_q[kt]:], values(h, kt),
                                         turned_[:, h % 2, turned_at[kt]:turned_at[kt] + S - first_q[kt]],
                                         start=(kt == 0), stop=(kt == key_tiles - 1))
                    last.then_inc(at_pv, 1)

            def cross_attention(l):
                norm(XATTN[l])
                pe.wait_ge(mem_landed, 16 * (N_MEM // P) * (l + 1))
                for k in range(KT):
                    if k >= 3:
                        pe.wait_ge(mem_out, l * KT + k - 2)
                    for t in range(N_MEM // P):
                        last = pe.transpose(A[1 + k % 3][:, t * P:(t + 1) * P], mem_tok[:, t, k * P:(k + 1) * P], ident)
                    last.then_inc(mem_turned, 1)
                c0 = start[f"xq{l}"][0]
                first_tiles(c0, 0, normal, tiles_of(XATTN[l]))
                norm(MEMORY[l], N_MEM)
                two_tiles(c0 + 1, 1, normal, KT)
                c0 = start[f"xkv{l}"][0]
                memory = operand(mem_hi, mem_lo, N_MEM)
                first_tiles(c0, 0, memory, tiles_of(MEMORY[l]), N_MEM)
                two_tiles(c0 + 1, 1, memory, KT, n=N_MEM)
                for n in range(2):
                    token_major(c0 + 2 + n, n, mem_hi, mem_lo, KT, N_MEM // P)
                pe.wait_ge(m_free, sum(start[f"xkv{l}"]) + 2)

                def scores(h, i, bank):
                    return pe.matmul(bank[:, 0:N_MEM], q_x[:, h, i * P:(i + 1) * P], k_x[:, h, :],
                                     start=True, stop=True)
                attend(f"x{l}", scores, lambda h, kt: v_x[:, kt, h * P:(h + 1) * P])
                pe.wait_ge(at_out, AT0[f"x{l}"] + 4)
                looped_tiles(f"xo{l}", operand(xo_hi, xo_lo), 4)
                norm(FFN[l])
                feed_forward(2 + l, FFN[l])

            norm(MIX[0])
            c0 = start["ev_in"][0]
            for n in range(8):
                if n == 0:
                    first_tiles(c0, 0, normal, tiles_of(MIX[0]))
                else:
                    two_tiles(c0 + n, n % 2, normal, KT)
                if n == 2:
                    pe.wait_ge(pool_landed, 16)
                if n in (2, 3):
                    for g in (2 * n - 4, 2 * n - 3):
                        pe.wait_ge(pool_in, g + 1)
                        pe.matmul(A[g][:, :], pool_w[:, g, :], pooled[:, g, :], start=True, stop=True)\
                          .then_inc(pool_out, 1)
            c0 = start["ev_out"][0]
            mixed = operand(y_hi, y_lo)
            first_tiles(c0, 0, mixed, (ev_y_lo, 0), order=Y_ORDER)
            for n in range(1, 4):
                two_tiles(c0 + n, n % 2, mixed, KT)
            cross_attention(0)

            norm(MIX[1])
            c0 = start["od_in"][0]
            first_tiles(c0, 0, normal, tiles_of(MIX[1]))
            for n in range(1, 4):
                two_tiles(c0 + n, n % 2, normal, KT)
            for n in range(2):
                token_major(c0 + 4 + n, n, h_hi, h_lo, KT, TT)
            for n in range(2):
                two_tiles(c0 + 6 + n, n, normal, KT)
            c0 = start["od_lat"][0]
            for n in range(4):
                two_tiles(c0 + n, n % 2, normal, KT, widths=(P, QK_DIM) if n == 2 else (P, P))
                if n >= 2:
                    norm(LATENT_Q if n == 2 else LATENT_KV)
            pe.wait_ge(rows_done, 1)
            for t in range(TT):
                last = pe.transpose(A[1][:, t * ML_HEADS:(t + 1) * ML_HEADS],
                                    g_i[0:ML_HEADS, t * P:(t + 1) * P], ident[0:ML_HEADS, 0:ML_HEADS])
            last.then_inc(a_turned, 1)
            pe.wait_ge(a_out, 1)
            pe.wait_ge(rstd_done, LATENT_KV + 1)
            pe.wait_ge(m_free, sum(start["od_gk"]) + 2)
            pe.wait_ge(og_done, 2)

            key_banks = [(A[0], 0), (A[1], 0), (A[2], 0), (A[2], 2 * P)]

            def ml_score(h):
                for st, (bank, at) in enumerate(key_banks):
                    pe.matmul(bank[:, at:at + ST_N[st]], k_m[:, h, st * P:(st + 1) * P], q_m[:, h, st * P:],
                              start=True, stop=True)
                row = ident[0:ML_HEADS, h:h + 1].broadcast_to([ML_HEADS, P])
                pe.matmul(A[3][:, :], row, g_top[0:ML_HEADS, :], start=True, stop=True)
                pe.matmul(M[0][:, :], row, g_sum[0:ML_HEADS, :], start=True, stop=True).then_inc(ml_scores, 1)

            def ml_square_sum(h):
                pe.wait_ge(ml_sq, h + 1)
                if h:
                    pe.wait_ge(ml_ln, h)
                pe.matmul(M[3][:, :], ones, ml_3[:, :], start=True, stop=True).then_inc(ml_ss, 1)

            ml_score(0)
            for h in range(ML_HEADS):
                pe.wait_ge(ml_sw_done, h + 1)
                if h + 1 < ML_HEADS:
                    ml_score(h + 1)
                if h:
                    ml_square_sum(h - 1)
                    pe.wait_ge(ml_hm, h)
                for st in range(TT):
                    pe.matmul(M[1][:, st * P:], v_ml[:, st, h * P:(h + 1) * P], ml_sw[:, ST[st]:ST[st] + ST_N[st]],
                              start=(st == 0), stop=(st == TT - 1))
                for st in range(TT):
                    last = pe.matmul(M[2][:, st * P:], ones, ml_sw[:, ST[st]:ST[st] + ST_N[st]],
                                     start=(st == 0), stop=(st == TT - 1))
                last.then_inc(ml_nd, 1)
            ml_square_sum(ML_HEADS - 1)
            pe.wait_ge(ml_hm, ML_HEADS)
            pe.wait_ge(ml_ln, ML_HEADS)
            pe.wait_ge(h_lo_done, split_norm(LATENT_KV) + 2)
            for n in range(4):
                two_tiles(start["od_uq"][0] + n, n % 2, operand(cq_hi, cq_lo), 3, widths=(QK_DIM, QK_DIM))
            for n in range(4):
                two_tiles(start["od_ukv"][0] + n, n % 2, operand(ckv_hi, ckv_lo), 2)
            rot = const[RR, C_ROT:C_ROT + ROPE]
            pe.wait_ge(m_free, sum(start["od_uq"]) + 2)
            for n in range(MLA_HEADS + 1):
                if n >= 4:
                    pe.wait_ge(rope_free, n - 3)
                src = k_rope[RR, :] if n == 0 else q_h[RR, n - 1, :]
                pe.matmul(A[n % 4][RR, :], rot, src, start=True, stop=True).then_inc(rope_turned, 1)
            for n in range(2):
                token_major(start["od_uv"][0] + n, n % 2, ckv_hi, ckv_lo, 2, TT)
            pe.wait_ge(m_free, sum(start["od_uv"]) + 2)
            pe.wait_ge(rope_spread, 1)

            def scores(h, i, bank):
                pe.wait_ge(rope_done, h + 1)
                n = (i + 1) * P
                pe.matmul(bank[:, 0:n], q_h[0:QK_DIM, h, i * P:(i + 1) * P], k_h[0:QK_DIM, h, 0:n],
                          start=True, stop=False)
                return pe.matmul(bank[:, n - P:n], ident, const[:, C_CAUSAL:C_CAUSAL + P],
                                 start=False, stop=True)
            attend("mla", scores, lambda h, kt: v_h[:, kt, h * HD:(h + 1) * HD])
            pe.wait_ge(at_out, AT0["mla"] + MLA_HEADS)
            looped_tiles("od_out", normal, KT)
            cross_attention(1)
            norm(LAST_NORM)
            for k in range(KT):
                pe.wait_ge(normed_done, norm_tiles(LAST_NORM) + k + 1)
                if k >= 4:
                    pe.wait_ge(out_ready, k - 3)
                for t in range(TT):
                    last = pe.transpose(A[k % 4][:, t * P:(t + 1) * P], x[:, k, t * P:(t + 1) * P], ident)
                last.then_inc(out_turned, 1)

        @block.scalar
        def _(act):
            def split_hi(c, s, n=HALF):
                act.wait_ge(w_used, c + 1)
                for part in range(2):
                    act.wait_ge(landed[part], c * 16 + 16)
                    act.activation(w_hi[:, s, part * HALF:part * HALF + n], stage[:, part, 0:n], ACT.Copy)\
                       .then_inc(w_hi_done, 1)

            def split_after(c, s):
                if c + 2 < chunks:
                    split_hi(c + 2, s, size[c + 2])

            def splits(name):
                c0, n = start[name]
                with act.Fori(0, n // 2) as i:
                    for s in range(2):
                        split_hi(i * 2 + (c0 + s + 2), s)

            def squared(n, k, s, src=x, tokens=S):
                if not (isinstance(k, int) and k < 2):
                    act.wait_ge(square_added, k + additions(n))
                act.activation(square[:, s, 0:tokens], src[:, k, 0:tokens], ACT.Square).then_inc(square_done, 1)

            def splits_and_squares(name, n_norm):
                c0, n = start[name]
                per_chunk = KT // n

                def chunk(c, s, k, last):
                    if not last:
                        split_hi(c + 2, s)
                    act.wait_ge(m_free, c + 3)
                    for m in range(per_chunk):
                        squared(n_norm, k + m, (s * per_chunk + m) % 2)
                chunk(c0, 0, 0, False)
                chunk(c0 + 1, 1, per_chunk, False)
                if n > 4:
                    with act.Fori(1, n // 2 - 1) as i:
                        for s in range(2):
                            chunk(i * 2 + (c0 + s), s, i * (2 * per_chunk) + s * per_chunk, False)
                chunk(c0 + n - 2, 0, KT - 2 * per_chunk, False)
                chunk(c0 + n - 1, 1, KT - per_chunk, True)

            def norm(n, src=x, x_ready=None, hi=h_hi, tokens=S, behind=None, squares=True):
                kt, before = NORMS[n][0], norm_tiles(n)
                if n in (2, 4, MIX[1], LAST_NORM):
                    act.preload_act_table_set(LOG_EXP)
                if x_ready:
                    act.wait_ge(*x_ready)
                    for k in range(kt if squares else 0):
                        squared(n, k, k % 2, src, tokens)
                act.wait_ge(spread_done, n + 1)
                act.activation(rstd[:, 0:tokens], A[0][:, 0:tokens], ACT.Ln, bias=eps[:, 0:1], scale=1.0 / (kt * P))\
                   .then_inc(root_done, 1)
                act.wait_ge(root_done, n + 1)
                act.activation(rstd[:, 0:tokens], rstd[:, 0:tokens], ACT.Exp, scale=-0.5).then_inc(rstd_done, 1)
                if hi is not None:
                    for k in range(kt):
                        act.wait_ge(normed_done, before + k + 1)
                        act.activation(hi[:, k, 0:tokens], normed[:, k % 2, 0:tokens], ACT.Copy).then_inc(h_hi_done, 1)
                        if k == 1 and behind is not None:
                            split_after(behind, behind % 2)
                elif behind is not None:
                    split_after(behind, behind % 2)

            def feed_forward(l, kind, next_norm):
                for half, (f0, n) in enumerate(HALVES):
                    c0 = start[f"up{l}{half}"][0]
                    u0 = up_counts(l, half)
                    with act.Fori(0, n // 2) as i:
                        for s in range(2):
                            u = i * 2 + (u0 + s)
                            act.wait_ge(w_used, i * 2 + (c0 + s + 3))
                            if kind == "conv":
                                act.activation(conv[:, s, :], M[2 * s][:, :], ACT.Identity,
                                               bias=col_at("conv_b", i * 2 + (l * FT + f0 + s)),
                                               scale=col_at(f"conv_w{l}", i * 2 + (2 * FT + f0 + s)))\
                                   .then_inc(tap_done, 1)
                                split_hi(i * 2 + (c0 + s + 2), s)
                                act.wait_ge(conv_done, u + 1)
                                act.activation(acted[:, s, :], conv[:, s, :], ACT.Gelu).then_inc(acted_done, 1)
                            else:
                                act.activation(acted[:, s, :], M[2 * s][:, :], ACT.Silu).then_inc(acted_done, 1)
                                split_hi(i * 2 + (c0 + s + 2), s)
                            act.wait_ge(m_free, i * 2 + (c0 + s + 3))
                            act.activation(hid_hi[:, i * 2 + s, :], hid[:, s, :], ACT.Copy).then_inc(hid_hi_done, 1)
                    if half == 0:
                        splits(f"down{l}{half}")
                    elif sum(start[f"down{l}{half}"]) < chunks:
                        splits_and_squares(f"down{l}{half}", next_norm)
                    else:
                        for k in range(KT):
                            c = start[f"down{l}{half}"][0] + k
                            split_after(c, c % 2)
                            act.wait_ge(m_free, c + 3)
                            squared(next_norm, k, k % 2)

            def gate_chunk(l, j):
                c = start[f"gate{l}"][0] + j
                act.wait_ge(w_used, c + 3)
                for m in range(2):
                    act.activation(gate[:, 2 * j + m, :], M[2 * (c % 2) + m][:, :], ACT.Exp,
                                   bias=neg_gate[:, l * 16 + 2 * j + m:l * 16 + 2 * j + m + 1], scale=-1.0)\
                       .then_inc(gate_exp, 1)
                two = gate[:, 2 * j:2 * j + 2, :]
                act.wait_ge(gate_exp, (l * 8 + j) * 2 + 2)
                act.activation(two, two, ACT.Ln, bias=1.0).then_inc(gate_ln, 1)
                split_after(c, c % 2)
                act.wait_ge(gate_ln, l * 8 + j + 1)
                act.activation(two, two, ACT.Exp, scale=-1.0).then_inc(gate_done, 1)

            def mixture_head(l, h):
                n = l * SLOTS + h
                act.wait_ge(max_spread, n + 1)
                for g in range(GROUPS):
                    act.activation(nat(top[:, g, :], g), over(A[g][:, :], g), ACT.Copy).then_inc(max_copied, 1)
                act.wait_ge(shifted, n + 1)
                act.activation(prob[:, :, :], prob[:, :, :], ACT.Exp).then_inc(exp_done, 1)
                for plane in range(PLANES):
                    act.wait_ge(turned_plane, PLANES * n + plane + 1)
                    skip = P if plane == 1 else 0
                    act.activation(prob[:, plane, skip:], A[plane][:, skip:], ACT.Copy).then_inc(plane_back, 1)
                act.wait_ge(top_shift, n + 1)
                act.activation(top[:, :, :], top[:, :, :], ACT.Exp).then_inc(weight_done, 1)
                lo = (h % 2) * HD
                act.wait_ge(mix_step, 3 * n + 3)
                act.activation(prob[lo:lo + HD, 3, :], prob[lo:lo + HD, 3, :], ACT.Ln).then_inc(den_step, 1)
                act.wait_ge(den_step, n + 1)
                act.activation(prob[lo:lo + HD, 3, :], prob[lo:lo + HD, 3, :], ACT.Exp, scale=-1.0)\
                   .then_inc(den_done, 1)
                if h + 1 < SLOTS:
                    gate_chunk(l, h)

            def stick_head(l, h):
                n = l * SLOTS + h
                act.wait_ge(z_done, n + 1)
                if h == 0:
                    act.wait_ge(o_done, (l + 1) * SLOTS)
                else:
                    act.wait_ge(st_pv, n)
                for bank, at, width in ((A[0], 0, S), (A[1], S, S - P), (A[2], 2 * S - P, S - P)):
                    last = act.activation(log_one[:, at:at + width], bank[:, 0:width], ACT.Abs, scale=HD ** -0.5)
                last.then_inc(st_act, 1)
                act.wait_ge(st_act, 2 * n + 1)
                act.activation(log_one, log_one, ACT.Exp, scale=-1.0).then_inc(st_act, 1)
                act.wait_ge(st_act, 2 * n + 2)
                act.activation(log_one, log_one, ACT.Ln, bias=1.0).then_inc(log_done, 1)
                gate_chunk(l, SLOTS + h - 1)
                act.wait_ge(st_arg, n + 1)
                act.activation(log_one, log_sig, ACT.Exp).then_inc(st_exp, 1)

            split_hi(0, 0)
            split_hi(1, 1)
            act.preload_act_table_set(LOG_EXP)
            for k in range(KT):
                act.wait_ge(turned_out, k + 1)
                squared(0, k, k % 2)
            act.wait_ge(consts_set, 2)

            for l in range(DEPTH):
                norm(2 * l, behind=start[f"qk{l}"][0] - 1 if l else None)
                for stage_name in (f"qk{l}", f"v{l}"):
                    splits(stage_name)
                for h in range(SLOTS):
                    mixture_head(l, h)
                for h in range(SLOTS):
                    stick_head(l, h)
                    if h == 0:
                        act.wait_ge(o_done, (l + 1) * SLOTS)
                        act.activation(o_hi[:, 0:2, :], o_a[:, :, :], ACT.Copy).then_inc(o_hi_done, 1)
                act.wait_ge(a_free, (l + 1) * 2 * SLOTS + 1)
                act.activation(o_hi[:, 2:4, :], o_b[:, :, :], ACT.Copy).then_inc(o_hi_done, 1)
                gate_chunk(l, 2 * SLOTS - 1)
                c0 = start[f"br{l}"][0]
                for j in range(KT):
                    act.wait_ge(merged_done, l * KT + j + 1)
                    act.activation(h_hi[:, j, :], merged[:, j % 2, :], ACT.Copy).then_inc(mg_hi_done, 1)
                    if j % 4 == 3:
                        split_after(c0 + j // 4, (c0 + j // 4) % 2)
                splits_and_squares(f"wo{l}", 2 * l + 1)
                norm(2 * l + 1, behind=start[f"up{l}0"][0] - 1)
                feed_forward(l, "conv", 2 * l + 2)
            norm(2 * DEPTH, hi=None, behind=start["ev_in"][0] - 1)

            def attend(kind):
                heads, key_tiles, widths, at, turned_at, first_q, prob_, turned_, scale = attention(kind)
                n0 = AT0[kind]

                def exps(h):
                    act.wait_ge(at_max, n0 + h + 1)
                    for i in range(TT):
                        last = act.activation(prob_[:, h % 2, at[i]:at[i] + widths[i]],
                                              head_banks(h)[i][:, 0:widths[i]], ACT.Exp,
                                              bias=neg_max[:, 4 * (h % 2) + i:4 * (h % 2) + i + 1], scale=scale,
                                              accum_out=soft_den[:, 4 * (h % 2) + i:4 * (h % 2) + i + 1])
                    last.then_inc(at_exp, 1)
                exps(0)
                for h in range(heads):
                    act.wait_ge(at_turned, n0 + h + 1)
                    for kt in range(key_tiles):
                        last = act.activation(turned_[:, h % 2, turned_at[kt]:turned_at[kt] + S - first_q[kt]],
                                              head_banks(h)[kt][:, first_q[kt]:], ACT.Copy)
                    last.then_inc(at_back, 1)
                    if h + 1 < heads:
                        exps(h + 1)
                    act.wait_ge(at_pv, n0 + h + 1)
                    hi, _, rows_ = result(kind, h)
                    act.activation(hi, head_banks(h)[0][rows_, :], ACT.Copy).then_inc(at_hi, 1)

            def straight_splits(name):
                c0, n = start[name]
                for c in range(c0, c0 + n):
                    split_after(c, c % 2)

            def cross_attention(l):
                c0 = start[f"xq{l}"][0]
                norm(XATTN[l], behind=c0 - 1)
                act.wait_ge(mem_out, KT * (l + 1))
                for k in range(KT):
                    squared(MEMORY[l], k, k % 2, mem_t, N_MEM)
                split_after(c0, 0)
                norm(MEMORY[l], mem_t, hi=mem_hi, tokens=N_MEM)
                split_after(c0 + 1, 1)
                straight_splits(f"xkv{l}")
                attend(f"x{l}")
                splits_and_squares(f"xo{l}", FFN[l])
                norm(FFN[l], behind=start[f"up{2 + l}0"][0] - 1)
                feed_forward(2 + l, "silu", MIX[1] if l == 0 else LAST_NORM)

            norm(MIX[0], x, (normed_done, norm_tiles(MIX[0])))

            def round_y(t):
                act.wait_ge(ev_y, t + 1)
                act.activation(y_hi[:, Y_ORDER[t], :], y[:, t % 2, :], ACT.Copy).then_inc(ev_y_hi, 1)

            c0 = start["ev_in"][0]
            y_of = {2: (0, 1), 3: (2, 3), 6: (4, 5), 7: (6, 7)}
            for n in range(8):
                if n < 6:
                    split_after(c0 + n, n % 2)
                for t in y_of.get(n, ()):
                    round_y(t)
                if n >= 6:
                    split_after(c0 + n, n % 2)
            splits_and_squares("ev_out", XATTN[0])
            cross_attention(0)

            norm(MIX[1], behind=start["od_in"][0] - 1)
            act.wait_ge(trig_arg, 1)
            act.activation(sin[RR, :], rest[RR, :], ACT.Sin).then_inc(trig_done, 1)
            act.activation(rest_abs[RR, :], rest[RR, :], ACT.Abs).then_inc(trig_done, 1)
            act.wait_ge(trig_done, 2)
            act.activation(cos[RR, :], rest_abs[RR, :], ACT.Sin, bias=half_pi[RR, 0:1], scale=-1.0)\
               .then_inc(trig_done, 1)
            act.preload_act_table_set(LOG_EXP)
            c0 = start["od_in"][0]
            for c in range(c0, c0 + 6):
                split_after(c, c % 2)
            for n in range(2):
                c = c0 + 6 + n
                act.wait_ge(w_used, c + 3)
                for m in range(2):
                    act.activation(sig_o[:, 2 * n + m, :], M[2 * (c % 2) + m][:, :], ACT.Exp, scale=-1.0)\
                       .then_inc(og_exp, 1)
                two = sig_o[:, 2 * n:2 * n + 2, :]
                act.wait_ge(og_exp, 2 * n + 2)
                act.activation(two, two, ACT.Ln, bias=1.0).then_inc(og_ln, 1)
                act.wait_ge(og_ln, n + 1)
                act.activation(two, two, ACT.Exp, scale=-1.0).then_inc(og_done, 1)
                split_after(c, c % 2)
            straight_splits("od_lat")
            c0 = start["od_gk"][0]
            act.wait_ge(m_free, c0 + 2)
            for k in range(3):
                squared(LATENT_Q, k, k % 2, latent)
            split_after(c0, 0)
            norm(LATENT_Q, hi=cq_hi)
            act.wait_ge(m_free, c0 + 3)
            for k in range(2):
                squared(LATENT_KV, k, k % 2, latent[:, 3:5, :])
            split_after(c0 + 1, 1)
            act.wait_ge(f_in, 2)
            fr = g_one[0:ML_HEADS, :]
            act.activation(fr, g_f[0:ML_HEADS, :], ACT.Abs).then_inc(f_step, 1)
            act.wait_ge(f_step, 1)
            act.activation(fr, fr, ACT.Exp, scale=-1.0).then_inc(f_step, 1)
            act.wait_ge(f_step, 2)
            act.activation(fr, fr, ACT.Ln, bias=1.0).then_inc(f_log, 1)
            norm(LATENT_KV, hi=ckv_hi)

            def ml_weights(h):
                act.wait_ge(ml_diag_done, h + 1)
                act.activation(ml_floor[:, h % 2, :], M[0][:, :], ACT.Exp, scale=-1.0)
                for st in range(TT):
                    a_st = a_col[:, st * ML_HEADS + h:st * ML_HEADS + h + 1]
                    last = act.activation(ml_w[:, ST[st]:ST[st] + P], ml_diag[:, st * P:(st + 1) * P], ACT.Exp, bias=a_st)
                    if st + 1 < TT:
                        act.activation(ml_w[:, ST[st] + P:ST[st] + ST_N[st]], A[3][:, (st + 1) * P:], ACT.Exp,
                                       bias=a_st, scale=-1.0)
                last.then_inc(ml_w_done, 1)

            ml_weights(0)
            for h in range(ML_HEADS):
                if h + 1 < ML_HEADS:
                    ml_weights(h + 1)
                act.wait_ge(ml_nd, h + 1)
                act.activation(ml_1[:, :], M[2][:, :], ACT.Abs).then_inc(ml_abs, 1)
                act.wait_ge(ml_den, h + 1)
                act.activation(ml_1[:, :], ml_1[:, :], ACT.Ln).then_inc(ml_inv, 1)
                act.wait_ge(ml_inv, 2 * h + 1)
                act.activation(ml_1[:, :], ml_1[:, :], ACT.Exp, scale=-1.0).then_inc(ml_inv, 1)
                act.wait_ge(ml_hm, h + 1)
                act.activation(ml_3[:, :], ml_2[:, :], ACT.Square).then_inc(ml_sq, 1)
                act.wait_ge(ml_ss, h + 1)
                act.activation(ml_0[:, :], M[3][:, :], ACT.Ln, bias=eps[:, 0:1], scale=1.0 / P).then_inc(ml_ln, 1)
                act.wait_ge(ml_ln, h + 1)
                act.activation(ml_0[:, :], ml_0[:, :], ACT.Exp, scale=-0.5).then_inc(ml_rs, 1)
                act.wait_ge(ml_y, h + 1)
                act.activation(h_hi[:, h, :], ml_2[:, :], ACT.Copy).then_inc(ml_hi, 1)
            straight_splits("od_uq")
            straight_splits("od_ukv")
            act.wait_ge(rope_k, 1)
            act.activation(k_h[RR, :, :], k_rope[RR, :].unsqueeze(1).broadcast_to([ROPE, MLA_HEADS, S]), ACT.Copy)\
               .then_inc(rope_spread, 1)
            straight_splits("od_uv")
            attend("mla")
            splits_and_squares("od_out", XATTN[1])
            cross_attention(1)
            norm(LAST_NORM, hi=None)

        @block.vector
        def _(dve):
            def split_lo(c, s, n=HALF):
                for part in range(2):
                    dve.wait_ge(w_hi_done, c * 2 + (part + 1))
                    dve.tensor_tensor(w_lo[:, s, part * HALF:part * HALF + n], stage[:, part, 0:n],
                                      w_hi[:, s, part * HALF:part * HALF + n].bitcast(F32), ALU.subtract)\
                       .then_inc(w_lo_done, 1)

            def split_after(c, s):
                if c + 2 < chunks:
                    split_lo(c + 2, s, size[c + 2])

            def pass_banks(c):
                dve.wait_ge(m_free, c + 2)
                dve.sem_inc(m_free, 1)

            def clear_sum(n):
                if n:
                    dve.wait_ge(spread_done, n)
                dve.memset(square_sum[:, :], 0.0).then_inc(square_added, 1)

            def add_square(n, k, s, tokens=S):
                dve.wait_ge(square_done, k + (norm_tiles(n) + 1))
                dve.wait_ge(square_added, k + (additions(n) + 1))
                dve.tensor_tensor(square_sum[:, 0:tokens], square_sum[:, 0:tokens], square[:, s, 0:tokens], ALU.add)\
                   .then_inc(square_added, 1)

            def sum_squares(n, tokens=S):
                clear_sum(n)
                for k in range(NORMS[n][0]):
                    add_square(n, k, k % 2, tokens)

            def norm(n, src=x, hi=h_hi, lo=h_lo, gain=None, tokens=S, behind=None):
                kt, split = NORMS[n][0], split_norm(n)
                dve.wait_ge(rstd_done, n + 1)

                def scaled(k):
                    dst = normed[:, k % 2, 0:tokens] if hi is not None else src[:, k, 0:tokens]
                    if k >= 2 and hi is not None:
                        dve.wait_ge(h_lo_done, split + k - 1)
                    dve.scalar_tensor_tensor(dst, src[:, k, 0:tokens], col(gain[0], gain[1] + k),
                                             rstd[:, 0:tokens], ALU.mult, ALU.mult).then_inc(normed_done, 1)
                if split:
                    dve.wait_ge(h_lo_done, split)
                scaled(0)
                for k in range(kt):
                    if k + 1 < kt:
                        scaled(k + 1)
                    if hi is not None:
                        dve.wait_ge(h_hi_done, split + k + 1)
                        dve.tensor_tensor(lo[:, k, 0:tokens], normed[:, k % 2, 0:tokens],
                                          hi[:, k, 0:tokens].bitcast(F32), ALU.subtract).then_inc(h_lo_done, 1)
                        if k == 1 and behind is not None:
                            split_after(behind, behind % 2)
                if hi is None and behind is not None:
                    split_after(behind, behind % 2)

            def add_residual(name, n_norm):
                c0, n = start[name]
                per_chunk = KT // n
                clear_sum(n_norm)

                def chunk(c, s, k, last):
                    dve.wait_ge(w_used, c + 3)
                    for m in range(per_chunk):
                        added = dve.tensor_tensor(x[:, k + m, :], x[:, k + m, :], M[2 * s + m][:, :], ALU.add)
                    added.then_inc(m_free, 1)
                    if not last:
                        split_lo(c + 2, s)
                    for m in range(per_chunk):
                        add_square(n_norm, k + m, (s * per_chunk + m) % 2)
                with dve.Fori(0, n // 2 - 1) as i:
                    for s in range(2):
                        chunk(i * 2 + (c0 + s), s, i * (2 * per_chunk) + s * per_chunk, False)
                chunk(c0 + n - 2, 0, KT - 2 * per_chunk, False)
                chunk(c0 + n - 1, 1, KT - per_chunk, True)

            def feed_forward(l, kind, next_norm):
                for half, (f0, n) in enumerate(HALVES):
                    c0 = start[f"up{l}{half}"][0]
                    u0 = up_counts(l, half)
                    with dve.Fori(0, n // 2) as i:
                        for s in range(2):
                            u = i * 2 + (u0 + s)
                            if kind == "conv":
                                for tap in (1, 0):
                                    back = 2 - tap
                                    if tap == 1:
                                        dve.wait_ge(tap_done, u + 1)
                                    else:
                                        dve.wait_ge(conv_step, u + 1)
                                    dve.scalar_tensor_tensor(
                                        conv[:, s, back:], M[2 * s][:, 0:S - back],
                                        col_at(f"conv_w{l}", i * 2 + (tap * FT + f0 + s)), conv[:, s, back:],
                                        ALU.mult, ALU.add).then_inc(conv_step if tap == 1 else conv_done, 1)
                            split_lo(i * 2 + (c0 + s + 2), s)
                            dve.wait_ge(acted_done, u + 1)
                            dve.tensor_tensor(hid[:, s, :], acted[:, s, :], M[2 * s + 1][:, :], ALU.mult)\
                               .then_inc(m_free, 1)
                            dve.wait_ge(hid_hi_done, u + 1)
                            dve.tensor_tensor(hid_lo[:, i * 2 + s, :], hid[:, s, :],
                                              hid_hi[:, i * 2 + s, :].bitcast(F32), ALU.subtract)\
                               .then_inc(hid_lo_done, 1)
                    c0, count = start[f"down{l}{half}"]

                    def down_chunk(c, s, tile, n_split):
                        dve.wait_ge(w_used, c + 3)
                        dve.tensor_tensor(x[:, tile, :], x[:, tile, :], M[2 * s][:, :], ALU.add)\
                           .then_inc(m_free, 1)
                        if n_split:
                            split_lo(c + 2, s, n_split)
                    if half == 1 and c0 + count < chunks:
                        add_residual(f"down{l}{half}", next_norm)
                    elif half == 0:
                        with dve.Fori(0, KT // 2) as i:
                            for s in range(2):
                                down_chunk(i * 2 + (c0 + s), s, i * 2 + s, HALF)
                    else:
                        clear_sum(next_norm)
                        for j in range(KT):
                            down_chunk(c0 + j, j % 2, j, size[c0 + j + 2] if c0 + j + 2 < chunks else 0)
                            add_square(next_norm, j, j % 2)

            def gate_chunk(l, j):
                c = start[f"gate{l}"][0] + j
                dve.wait_ge(gate_exp, (l * 8 + j) * 2 + 2)
                pass_banks(c)
                split_after(c, c % 2)

            def mixture_head(l, h):
                n = l * SLOTS + h
                if n == 0:
                    dve.wait_ge(bias_landed, 16)
                dve.wait_ge(scores_done, n + 1)
                if n > 0:
                    dve.wait_ge(o_done, n)
                for plane in range(PLANES):
                    b = 1 if plane == 1 else 0
                    blocks = TT - b
                    dve.scalar_tensor_tensor(
                        prob[:, plane, b * P:].rearrange("p (b c) -> p b c", c=P),
                        A[plane][:, b * P:].rearrange("p (b c) -> p b c", c=P), HD ** -0.5,
                        bias[:, h, plane, :].unsqueeze(1).broadcast_to([P, blocks, P]), ALU.mult, ALU.add)\
                       .then_inc(plane_biased, 1)
                dve.memset(prob[:, 1, 0:P], MASKED).then_inc(plane_biased, 1)
                dve.wait_ge(plane_biased, (PLANES + 1) * (n + 1))
                blocks = prob[:, :, :].rearrange("p n (b c) -> p (n b) c", c=P)
                dve.tensor_reduce(row_max[:, :], blocks, AX_X, ALU.max).then_inc(max_a, 1)
                dve.wait_ge(max_a, n + 1)
                dve.tensor_tensor(row_max[:, 0:4], row_max[:, 0:4], row_max[:, 4:8], ALU.max).then_inc(max_b, 1)
                dve.wait_ge(max_b, n + 1)
                dve.tensor_copy(row_max[:, 4:8], row_max[:, 0:4]).then_inc(max_done, 1)
                dve.wait_ge(max_done, n + 1)
                dve.tensor_tensor(blocks, blocks, row_max[:, :].unsqueeze(2).broadcast_to([P, 16, P]), ALU.subtract)\
                   .then_inc(shifted, 1)
                if h:
                    gate_chunk(l, h - 1)
                dve.wait_ge(max_copied, GROUPS * (n + 1))
                dve.tensor_tensor(top_all[:, :], top[:, 0, :], top[:, 1, :], ALU.max).then_inc(top1, 1)
                dve.wait_ge(top1, n + 1)
                dve.tensor_tensor(top_all[:, :], top_all[:, :], top[:, 2, :], ALU.max).then_inc(top2, 1)
                dve.wait_ge(top2, n + 1)
                dve.tensor_tensor(top[:, :, :], top[:, :, :], top_all[:, :].unsqueeze(1).broadcast_to([P, GROUPS, S]),
                                  ALU.subtract).then_inc(top_shift, 1)
                dve.wait_ge(weight_done, n + 1)
                dve.wait_ge(pv_done, n + 1)
                for g in range(GROUPS):
                    last = dve.tensor_tensor(nat(prob[:, g, :], g), nat(top[:, g, :], g), over(A[g][:, :], g), ALU.mult)
                last.then_inc(a_free, 1)
                step = 3 * n
                dve.wait_ge(a_free, l * 2 * SLOTS + h + 2)
                dve.tensor_tensor(prob[:, 0, :], prob[:, 0, :], prob[:, 1, :], ALU.add).then_inc(mix_step, 1)
                dve.wait_ge(mix_step, step + 1)
                dve.tensor_tensor(prob[:, 0, :], prob[:, 0, :], prob[:, 2, :], ALU.add).then_inc(mix_step, 1)
                dve.wait_ge(mix_step, step + 2)
                lo = (h % 2) * HD
                den = HD - lo
                dve.tensor_copy(prob[lo:lo + HD, 3, :], prob[den:den + HD, 0, :]).then_inc(mix_step, 1)
                dve.wait_ge(den_done, n + 1)
                dve.tensor_tensor(o_a[lo:lo + HD, h // 2, :], prob[lo:lo + HD, 0, :], prob[lo:lo + HD, 3, :], ALU.mult)\
                   .then_inc(o_done, 1)

            def stick_head(l, h):
                n = l * SLOTS + h
                parts = ((A[0], 0, S), (A[1], S, S - P), (A[2], 2 * S - P, S - P))
                scale = HD ** -0.5
                dve.wait_ge(st_act, 2 * n + 1)
                if h == 0:
                    dve.wait_ge(o_done, (l + 1) * SLOTS)
                for bank, at, width in parts:
                    last = dve.tensor_scalar(log_sig[:, at:at + width], bank[:, 0:width], scale, 0.0, ALU.mult, ALU.min)
                last.then_inc(st_dve, 1)
                dve.wait_ge(st_dve, 3 * n + 1)
                dve.wait_ge(log_done, n + 1)
                dve.tensor_tensor(log_sig, log_sig, log_one, ALU.subtract).then_inc(st_dve, 1)
                dve.wait_ge(st_dve, 3 * n + 2)
                for bank, at, width in parts:
                    last = dve.scalar_tensor_tensor(log_stay[:, at:at + width], bank[:, 0:width], -scale,
                                                    log_sig[:, at:at + width], ALU.mult, ALU.add)
                last.then_inc(st_dve, 1)
                dve.wait_ge(st_dve, 3 * n + 3)
                for kb in range(TT):
                    diagonal = log_stay[:, ST[kb]:ST[kb] + P]
                    last = dve.tensor_tensor(diagonal, diagonal, later_mask, ALU.mult)
                last.then_inc(stay_done, 1)
                gate_chunk(l, SLOTS + h - 1)
                dve.wait_ge(later_done, n + 1)
                for bank, at, width in parts:
                    last = dve.tensor_tensor(log_sig[:, at:at + width], log_sig[:, at:at + width], bank[:, 0:width], ALU.add)
                last.then_inc(st_arg, 1)
                dve.wait_ge(st_exp, n + 1)
                for kb in range(TT):
                    diagonal = log_one[:, ST[kb]:ST[kb] + P]
                    last = dve.tensor_tensor(diagonal, diagonal, later_mask, ALU.mult)
                last.then_inc(st_prob, 1)
                if h == 0:
                    dve.wait_ge(o_hi_done, 2 * l + 1)
                    dve.tensor_tensor(o_lo[:, 0:2, :], o_a[:, :, :], o_hi[:, 0:2, :].bitcast(F32), ALU.subtract)\
                       .then_inc(o_lo_done, 1)
                dve.wait_ge(st_pv, n + 1)
                lo = (h % 2) * HD
                dve.tensor_copy(o_b[lo:lo + HD, h // 2, :], A[3][lo:lo + HD, :]).then_inc(a_free, 1)

            dve.memset(half_pi[:, 0:1], np.pi / 2)
            dve.memset(eps[:, 0:1], EPS).then_inc(consts_set, 1)
            dve.sem_inc(m_free, 2)
            dve.sem_inc(br_free, 2)
            dve.sem_inc(a_free, 1)
            split_lo(0, 0)
            split_lo(1, 1)
            clear_sum(0)
            for k in range(KT):
                dve.wait_ge(turned, k + 1)
                dve.tensor_copy(x[:, k, :], A[k % 4][:, :]).then_inc(turned_out, 1)
                if k >= 1:
                    add_square(0, k - 1, (k - 1) % 2)
            add_square(0, KT - 1, (KT - 1) % 2)
            dve.wait_ge(turned, KT + 1)
            dve.tensor_copy(vec[:, :], A[1][:, 0:VEC_COLS]).then_inc(turned_out, 1)
            dve.wait_ge(turned_out, KT + 1)
            dve.tensor_scalar(neg_gate[:, :], vec[:, VEC["b_gate"]:VEC["b_gate"] + DEPTH * 16], -1.0, None, ALU.mult)\
               .then_inc(consts_set, 1)

            for l in range(DEPTH):
                norm(2 * l, gain=("norm1", l * KT), behind=start["qk1"][0] - 1 if l else None)
                dve.memset(v_a[:, :, :, 1, :], 1.0).then_inc(ones_set, 1)
                c0 = start[f"qk{l}"][0]
                for j in range(8):
                    c = c0 + j
                    dve.wait_ge(w_used, c + 3)
                    for m in range(2):
                        if j < 6:
                            g = j % 3
                            dst = as_residue(qk_a[:, 2 * j + m, :], g)
                        else:
                            g = 0
                            dst = qk_b[:, 2 * (j - 6) + m, :]
                        last = dve.tensor_copy(dst, by_residue(M[2 * (c % 2) + m][:, :], g))
                    last.then_inc(m_free, 1)
                    split_after(c, c % 2)
                c0 = start[f"v{l}"][0]
                for j in range(4):
                    c = c0 + j
                    dve.wait_ge(w_used, c + 3)
                    for b in range(2):
                        src = M[2 * (c % 2) + b][:, :]
                        if j == GROUPS:
                            last = dve.tensor_copy(v_b[:, 2 * b:2 * b + 2, :], src.rearrange("p (t c) -> p t c", t=2))
                            continue
                        for t in range(2):
                            last = dve.tensor_copy(
                                v_a[:, 2 * b + t, 2 * j:2 * j + 2, 0:3:2, :],
                                src[:, t * 2 * P:(t + 1) * 2 * P].rearrange("p (a e c) -> p a e c", a=2, e=2))
                    last.then_inc(m_free, 1)
                    split_after(c, c % 2)
                for h in range(SLOTS):
                    mixture_head(l, h)
                for h in range(SLOTS):
                    stick_head(l, h)
                dve.wait_ge(o_hi_done, 2 * l + 2)
                dve.tensor_tensor(o_lo[:, 2:4, :], o_b[:, :, :], o_hi[:, 2:4, :].bitcast(F32), ALU.subtract)\
                   .then_inc(o_lo_done, 1)
                gate_chunk(l, 2 * SLOTS - 1)

                def merged_rest(j):
                    dve.wait_ge(mg_hi_done, l * KT + j + 1)
                    dve.tensor_tensor(h_lo[:, j, :], merged[:, j % 2, :], h_hi[:, j, :].bitcast(F32), ALU.subtract)\
                       .then_inc(mg_lo_done, 1)
                c0 = start[f"br{l}"][0]
                for j in range(KT):
                    n, m = divmod(j, 4)
                    dve.wait_ge(gate_done, l * 8 + SLOTS + j // 2 + 1)
                    jj = l * KT + j
                    if m < 3:
                        dve.wait_ge(br_full, l * 6 + n * 3 + m + 1)
                    else:
                        dve.wait_ge(w_used, c0 + n + 3)
                    if j >= 2:
                        dve.wait_ge(mg_lo_done, jj - 1)
                    dve.tensor_tensor(merged[:, j % 2, :], gate[:, j, :], M[2 * (j % 2)][:, :], ALU.mult)
                    dve.tensor_tensor(merged[:, 2 + j % 2, :], gate[:, KT + j, :], M[2 * (j % 2) + 1][:, :], ALU.mult)\
                       .then_inc(br_free, 1)
                    dve.wait_ge(br_free, jj + 3)
                    dve.tensor_tensor(merged[:, j % 2, :], merged[:, j % 2, :], merged[:, 2 + j % 2, :], ALU.add)\
                       .then_inc(merged_done, 1)
                    if j:
                        merged_rest(j - 1)
                    if j == KT - 1:
                        merged_rest(j)
                    if m == 3:
                        pass_banks(c0 + n)
                        split_after(c0 + n, (c0 + n) % 2)
                add_residual(f"wo{l}", 2 * l + 1)
                norm(2 * l + 1, gain=("norm2", l * KT), behind=start[f"up{l}0"][0] - 1)
                feed_forward(l, "conv", 2 * l + 2)
            norm(2 * DEPTH, hi=None, gain=("norm_f", 0), behind=start["ev_in"][0] - 1)
            done = [0]

            def link(instruction):
                done[0] += 1
                instruction.then_inc(chain, 1)
                dve.wait_ge(chain, done[0])

            def read_out(name, c, tiles):
                dve.wait_ge(w_used, c + 3)
                for dst, src, factor in tiles:
                    if factor is None:
                        last = dve.tensor_copy(dst, src)
                    else:
                        last = dve.tensor_scalar(dst, src, factor, None, ALU.mult)
                last.then_inc(m_free, 1)
                split_after(c, c % 2)

            def attend(kind, beside=None):
                heads, key_tiles, widths, at, turned_at, first_q, prob_, turned_, scale = attention(kind)
                n0 = AT0[kind]

                def maxima(h):
                    col0 = 4 * (h % 2)
                    dve.wait_ge(at_scores, n0 + h + 1)
                    for i in range(TT):
                        last = dve.tensor_reduce(soft_max[:, col0 + i:col0 + i + 1], head_banks(h)[i][:, 0:widths[i]],
                                                 AX_X, ALU.max)
                    last.then_inc(at_reduced, 1)
                    dve.wait_ge(at_reduced, n0 + h + 1)
                    dve.tensor_scalar(neg_max[:, col0:col0 + 4], soft_max[:, col0:col0 + 4], -scale, None, ALU.mult)\
                       .then_inc(at_max, 1)
                maxima(0)
                for h in range(heads):
                    col0 = 4 * (h % 2)
                    dve.wait_ge(at_exp, n0 + h + 1)
                    dve.reciprocal(soft_den[:, col0:col0 + 4], soft_den[:, col0:col0 + 4]).then_inc(at_recip, 1)
                    dve.wait_ge(at_recip, n0 + h + 1)
                    for i in range(TT):
                        part = prob_[:, h % 2, at[i]:at[i] + widths[i]]
                        last = dve.tensor_scalar(part, part, soft_den[:, col0 + i:col0 + i + 1], None, ALU.mult)
                    last.then_inc(at_norm, 1)
                    if h + 1 < heads:
                        maxima(h + 1)
                    if beside:
                        beside(h)
                    hi, lo, rows_ = result(kind, h)
                    dve.wait_ge(at_hi, n0 + h + 1)
                    dve.tensor_tensor(lo, head_banks(h)[0][rows_, :], hi.bitcast(F32), ALU.subtract).then_inc(at_out, 1)

            def cross_attention(l):
                for k in range(KT):
                    dve.wait_ge(mem_turned, l * KT + k + 1)
                    dve.tensor_copy(mem_t[:, k, :], A[1 + k % 3][:, 0:N_MEM]).then_inc(mem_out, 1)
                c0 = start[f"xq{l}"][0]
                norm(XATTN[l], gain=("norm_xattn_g_2", l * KT), behind=c0 - 1)
                sum_squares(MEMORY[l], N_MEM)
                read_out("q", c0, [(q_x[:, m, :], M[m][:, :], None) for m in range(2)])
                norm(MEMORY[l], mem_t, hi=mem_hi, lo=mem_lo, gain=("mem_norm_g_2", l * KT), tokens=N_MEM)
                read_out("q", c0 + 1, [(q_x[:, 2 + m, :], M[2 + m][:, :], None) for m in range(2)])
                c0 = start[f"xkv{l}"][0]
                for n in range(2):
                    read_out("k", c0 + n, [(k_x[:, 2 * n + m, :], M[2 * n + m][:, 0:N_MEM], None) for m in range(2)])
                for n in range(2):
                    read_out("v", c0 + 2 + n, [(v_x[:, :, n * 2 * P:(n + 1) * 2 * P],
                                                M[2 * n][:, :].rearrange("p (t c) -> p t c", t=2), None)])
                attend(f"x{l}")
                add_residual(f"xo{l}", FFN[l])
                norm(FFN[l], gain=("norm_ffn_g_2", l * KT), behind=start[f"up{2 + l}0"][0] - 1)
                feed_forward(2 + l, "silu", MIX[1] if l == 0 else LAST_NORM)

            sum_squares(MIX[0])
            norm(MIX[0], gain=("norm_mix_g_2", 0))
            y_count = [0]

            def y_slot():
                t = y_count[0]
                if t >= 2:
                    dve.wait_ge(ev_y_hi, t - 1)
                return y[:, t % 2, :]

            def y_split():
                t = y_count[0]
                dve.wait_ge(ev_y_hi, t + 1)
                tile = Y_ORDER[t]
                dve.tensor_tensor(y_lo[:, tile, :], y[:, t % 2, :], y_hi[:, tile, :].bitcast(F32), ALU.subtract)\
                   .then_inc(ev_y_lo, 1)
                y_count[0] += 1

            def convolve(t):
                u, v = gated[:, t, :], g_c[:, t, :]
                link(dve.tensor_scalar(v, u, col("ev_conv_w_2", 8 + t), None, ALU.mult))
                for back in (1, 2):
                    link(dve.scalar_tensor_tensor(v[:, back:], u[:, 0:S - back], col("ev_conv_w_2", (2 - back) * 4 + t),
                                                  v[:, back:], ALU.mult, ALU.add))

            def pool_result(g):
                dve.wait_ge(pool_out, g + 1)
                dve.tensor_scalar(y_slot(), A[g][:, :], col("ev_pool_scale_2", g), None, ALU.mult).then_inc(ev_y, 1)
                y_split()

            def pool(g):
                width = WINDOWS[g]
                src, span, n = pooled[:, g, :], 1, 0
                while span < width:
                    dst = window[:, n % 2, :]
                    dve.tensor_copy(dst[:, 0:span], src[:, 0:span])
                    link(dve.tensor_tensor(dst[:, span:], src[:, span:], src[:, 0:S - span], ALU.add))
                    src, span, n = dst, span * 2, n + 1
                head = window[:, n % 2, 0:width]
                link(dve.tensor_tensor(head, src[:, 0:width], const[:, C_INV:C_INV + width], ALU.mult))
                dve.scalar_tensor_tensor(pooled[:, g, width:], src[:, width:], 1.0 / width, pooled[:, g, width:],
                                         ALU.mult, ALU.subtract)
                link(dve.tensor_tensor(pooled[:, g, 0:width], head, pooled[:, g, 0:width], ALU.subtract))
                dve.sem_inc(pool_in, 1)

            c0 = start["ev_in"][0]
            for n in range(8):
                bank = [M[2 * (n % 2) + m][:, :] for m in range(2)]
                if n < 2:
                    read_out("xb", c0 + n, [(pooled[:, 2 * n + m, :], bank[m], None) for m in range(2)])
                    dve.wait_ge(m_free, c0 + n + 3)
                    pool(2 * n)
                    pool(2 * n + 1)
                elif n < 4:
                    read_out("g_c", c0 + n, [(g_c[:, 2 * (n % 2) + m, :], bank[m], None) for m in range(2)])
                    pool_result(2 * n - 4)
                    pool_result(2 * n - 3)
                elif n < 6:
                    dve.wait_ge(w_used, c0 + n + 3)
                    for m in range(2):
                        t = 2 * (n - 4) + m
                        last = dve.tensor_tensor(gated[:, t, :], g_c[:, t, :], bank[m], ALU.mult)
                    last.then_inc(m_free, 1)
                    split_after(c0 + n, n % 2)
                    dve.wait_ge(m_free, c0 + n + 3)
                    convolve(2 * (n - 4))
                    convolve(2 * (n - 4) + 1)
                else:
                    dve.wait_ge(w_used, c0 + n + 3)
                    for m in range(2):
                        dve.tensor_tensor(y_slot(), g_c[:, 2 * (n - 6) + m, :], bank[m], ALU.mult).then_inc(ev_y, 1)
                        y_split()
                    pass_banks(c0 + n)
                    split_after(c0 + n, n % 2)
            add_residual("ev_out", XATTN[0])
            cross_attention(0)

            norm(MIX[1], gain=("norm_mix_g_2", KT), behind=start["od_in"][0] - 1)
            dve.wait_ge(pos_landed, 16)
            ang, turn, left = angle[RR, :], turns[RR, :], rest[RR, :]
            link(dve.tensor_copy(ang, pos[RR, :]))
            link(dve.tensor_scalar(ang, ang, const[RR, C_FREQ:C_FREQ + 1], None, ALU.mult))
            link(dve.tensor_scalar(turn, ang, 1.0 / TWO_PI, ROUND, ALU.mult, ALU.add))
            link(dve.tensor_scalar(turn, turn, -ROUND, None, ALU.add))
            for n, part in enumerate((TURN_1, TURN_2, TURN_3)):
                link(dve.scalar_tensor_tensor(left, turn, -part, ang if n == 0 else left, ALU.mult, ALU.add))
            dve.tensor_scalar(left, left, -3.1415925, 3.1415925, ALU.max, ALU.min).then_inc(trig_arg, 1)

            c0 = start["od_in"][0]
            for n in range(4):
                dst, factor = (q_m, None) if n < 2 else (k_m, P ** -0.5)
                read_out("qk", c0 + n, [(dst[:, 2 * (n % 2) + m, :], M[2 * (n % 2) + m][:, :], factor) for m in range(2)])
            for n in range(2):
                read_out("v", c0 + 4 + n, [(v_ml[:, 2 * b:2 * b + 2, n * 2 * P:(n + 1) * 2 * P],
                                            M[2 * n + b][:, :].rearrange("p (t c) -> p t c", t=2), None)
                                           for b in range(2)])
            for n in range(2):
                dve.wait_ge(og_exp, 2 * n + 2)
                pass_banks(c0 + 6 + n)
                split_after(c0 + 6 + n, n % 2)
            c0 = start["od_lat"][0]
            for n in range(2):
                read_out("latent", c0 + n, [(latent[:, 2 * n + m, :], M[2 * n + m][:, :], None) for m in range(2)])
            sum_squares(LATENT_Q)
            read_out("latent", c0 + 2, [(latent[:, 4, :], M[0][:, :], None), (k_rope[RR, :], M[1][RR, :], None)])
            norm(LATENT_Q, latent[:, 0:3, :], hi=cq_hi, lo=cq_lo, gain=("od_q_norm_g_2", 0))
            sum_squares(LATENT_KV)
            H4 = slice(0, ML_HEADS)
            dve.wait_ge(w_used, c0 + 3 + 3)
            dve.tensor_scalar(g_i[H4, :], M[2][H4, :], gate_bias[H4, 0:1], None, ALU.add).then_inc(f_in, 1)
            dve.tensor_scalar(g_f[H4, :], M[3][H4, :], gate_bias[H4, 1:2], None, ALU.add).then_inc(f_in, 1)
            dve.wait_ge(f_in, 2)
            pass_banks(c0 + 3)
            split_after(c0 + 3, 1)
            dve.wait_ge(f_log, 1)
            link(dve.tensor_scalar(g_f[H4, :], g_f[H4, :], 0.0, None, ALU.min))
            link(dve.tensor_tensor(g_f[H4, :], g_f[H4, :], g_one[H4, :], ALU.subtract))
            link(dve.memset(g_one[H4, :], 1.0))
            link(dve.tensor_tensor_scan(g_sum[H4, :], g_one[H4, :], g_f[H4, :], 0.0, ALU.mult, ALU.add))
            link(dve.tensor_tensor(g_i[H4, :], g_i[H4, :], g_sum[H4, :], ALU.subtract))
            link(dve.tensor_tensor_scan(g_top[H4, :], g_i[H4, :], g_i[H4, :], 0.0, ALU.max, ALU.max))
            dve.tensor_tensor(g_sum[H4, :], g_sum[H4, :], g_top[H4, :], ALU.add).then_inc(rows_done, 1)
            norm(LATENT_KV, latent[:, 3:5, :], hi=ckv_hi, lo=ckv_lo, gain=("od_kv_norm_g_2", 0))
            dve.wait_ge(a_turned, 1)
            dve.tensor_copy(a_col[:, :], A[1][:, 0:16]).then_inc(a_out, 1)

            def ml_diagonal(h):
                dve.wait_ge(ml_scores, h + 1)
                dve.scalar_tensor_tensor(ml_diag[:, :].rearrange("p (t c) -> p t c", t=TT),
                                         A[3][:, :].rearrange("p (t c) -> p t c", t=TT), -1.0,
                                         const[:, C_CAUSAL_T:C_CAUSAL_T + P].unsqueeze(1).broadcast_to([P, TT, P]),
                                         ALU.mult, ALU.add).then_inc(ml_diag_done, 1)

            def ml_weighted(h):
                dve.wait_ge(ml_w_done, h + 1)
                for bank, at, width in ((A[0], 0, S), (A[1], S, S - P), (A[2], 2 * S - P, S - P)):
                    last = dve.tensor_tensor(ml_sw[:, at:at + width], ml_w[:, at:at + width], bank[:, 0:width], ALU.mult)
                last.then_inc(ml_sw_done, 1)

            ml_diagonal(0)
            ml_weighted(0)
            for h in range(ML_HEADS):
                if h + 1 < ML_HEADS:
                    ml_diagonal(h + 1)
                dve.wait_ge(ml_abs, h + 1)
                dve.tensor_tensor(ml_1[:, :], ml_1[:, :], ml_floor[:, h % 2, :], ALU.max).then_inc(ml_den, 1)
                if h + 1 < ML_HEADS:
                    ml_weighted(h + 1)
                dve.wait_ge(ml_inv, 2 * h + 2)
                link(dve.tensor_tensor(ml_2[:, :], M[1][:, :], ml_1[:, :], ALU.mult))
                dve.tensor_tensor(ml_2[:, :], ml_2[:, :], sig_o[:, h, :], ALU.mult).then_inc(ml_hm, 1)
                dve.wait_ge(ml_rs, h + 1)
                dve.scalar_tensor_tensor(ml_2[:, :], ml_2[:, :], col("od_ml_norm_g_2", h), ml_0[:, :], ALU.mult, ALU.mult)\
                   .then_inc(ml_y, 1)
                dve.wait_ge(ml_hi, h + 1)
                dve.tensor_tensor(h_lo[:, h, :], ml_2[:, :], h_hi[:, h, :].bitcast(F32), ALU.subtract).then_inc(ml_out, 1)
            for n in range(4):
                read_out("q", start["od_uq"][0] + n,
                         [(q_h[0:QK_DIM, 2 * n + m, :], M[2 * (n % 2) + m][0:QK_DIM, :], None) for m in range(2)])
            for n in range(4):
                read_out("k", start["od_ukv"][0] + n,
                         [(k_h[0:NOPE, 2 * n + m, :], M[2 * (n % 2) + m][0:NOPE, :], None) for m in range(2)])
            dve.wait_ge(trig_done, 3)
            dve.wait_ge(rope_turned, 1)
            dve.tensor_tensor(rotated[RR, 0, :], A[0][RR, :], sin[RR, :], ALU.mult).then_inc(rope_free, 1)
            dve.wait_ge(rope_free, 1)
            link(dve.tensor_tensor(k_rope[RR, :], k_rope[RR, :], cos[RR, :], ALU.mult))
            dve.tensor_tensor(k_rope[RR, :], k_rope[RR, :], rotated[RR, 0, :], ALU.add).then_inc(rope_k, 1)
            dve.wait_ge(rope_k, 1)
            for h in range(MLA_HEADS):
                dve.wait_ge(rope_turned, h + 2)
                dve.tensor_tensor(rotated[RR, h, :], A[(h + 1) % 4][RR, :], sin[RR, :], ALU.mult).then_inc(rope_free, 1)

            def rope_query(h):
                if h < MLA_HEADS:
                    q_rope = q_h[RR, h, :]
                    dve.wait_ge(rope_free, h + 2)
                    link(dve.tensor_tensor(q_rope, q_rope, cos[RR, :], ALU.mult))
                    dve.tensor_tensor(q_rope, q_rope, rotated[RR, h, :], ALU.add).then_inc(rope_done, 1)
            rope_query(0)
            rope_query(1)
            for n in range(2):
                read_out("v", start["od_uv"][0] + n,
                         [(v_h[:, 2 * b:2 * b + 2, n * 2 * P:(n + 1) * 2 * P],
                           M[2 * n + b][:, :].rearrange("p (t c) -> p t c", t=2), None) for b in range(2)])
            attend("mla", beside=lambda h: rope_query(h + 2))
            add_residual("od_out", XATTN[1])
            cross_attention(1)
            norm(LAST_NORM, hi=None, gain=("final_norm_g_2", 0))
            for k in range(KT):
                dve.wait_ge(out_turned, k + 1)
                dve.tensor_copy(x_out[:, :, k * P:(k + 1) * P], A[k % 4][:, :].rearrange("p (t c) -> p t c", t=TT))\
                   .then_inc(out_ready, 1)


_INS = ['x', 'norm1', 'w_in', 'b_gate', 'w_br', 'w_o', 'norm2', 'w_up', 'conv_w', 'conv_b', 'w_down', 'norm_f',
        'mem_2', 'positions_2', 'norm_mix_g_2', 'norm_xattn_g_2', 'mem_norm_g_2', 'xattn_wq_2', 'xattn_wkv_2',
        'xattn_wo_2', 'norm_ffn_g_2', 'ffn_w_gate_up_2', 'ffn_w_down_2', 'ev_w_in_2', 'ev_conv_w_2', 'ev_pool_w_2',
        'ev_pool_scale_2', 'ev_w_out_2', 'od_w_in_2', 'od_gate_bias_2', 'od_ml_norm_g_2', 'od_q_norm_g_2',
        'od_kv_norm_g_2', 'od_w_uq_2', 'od_w_ukv_2', 'od_w_out_2', 'final_norm_g_2']


def kernel(**inputs):
    import concourse.bacc as _bacc
    from concourse.bass_utils import run_bass_kernel_spmd as _run

    nc = _bacc.Bacc("TRN2", target_bir_lowering=False, num_devices=1)
    arrays, dram = {}, {}
    for name in _INS:
        a = np.ascontiguousarray(inputs[name])
        arrays[f"in_{name}"] = a
        dram[name] = nc.dram_tensor(f"in_{name}", a.shape, mybir.dt.from_np(a.dtype), kind="ExternalInput").ap()
    a = shape_constants()
    arrays["in_shape_constants"] = a
    dram["shape_constants"] = nc.dram_tensor("in_shape_constants", a.shape, F32, kind="ExternalInput").ap()
    out = nc.dram_tensor("out_0", (1, S, D), F32, kind="ExternalOutput").ap()
    block_program(nc, dram, out)
    r = _run(nc, [arrays], core_ids=[0])
    return np.array(r.results[0]["out_0"])
```
